# Optimizing a Trainium2 kernel written in Bass

```python
import math
import jax, jax.numpy as jnp
from jax import lax
import numpy as np

D_MODEL = 1024
BATCH = 1
SEQ = 512
DEPTH = 2

N_MIXERS = 2
D_FF = 2816
EPS = 1e-6
A_HEADS = 4
A_DK = 128
A_DV = 256
A_QK = A_HEADS * A_DK
A_V = A_HEADS * A_DV
A_CONV = 4
A_CHUNK = 64
A_PROJ = 2 * A_QK + 2 * A_V + 2 * A_HEADS
B_HEADS = 4
B_DH = 128
B_DV = 2 * B_DH
B_QK = B_HEADS * 2 * B_DH
B_V = B_HEADS * B_DV
B_PROJ = 2 * B_QK + B_V
ROPE_THETA = 500000.0
ROPE_DIM = B_DH // 4
Q_BLOCK = 128
N_A = (DEPTH + 1) // 2
N_B = DEPTH // 2

kernel_name = "hybrid_mlstm_diffattn_macaron_adaln"

def rmsnorm(x, g):
    x32 = x.astype(jnp.float32)
    y = x32 * lax.rsqrt(jnp.mean(x32 * x32, -1, keepdims=True) + EPS)
    return (y * g.astype(jnp.float32)).astype(x.dtype)

def modulate(x, g, shift, scale):
    return rmsnorm(x, g) * (1.0 + scale[:, None, :]) + shift[:, None, :]

def swiglu(h, w13, w2):
    gate, up = jnp.split(h @ w13, 2, axis=-1)
    return (jax.nn.silu(gate) * up) @ w2

def rope_partial(x, cos, sin):
    half = ROPE_DIM // 2
    c = cos[:, :, None, None, :]
    s = sin[:, :, None, None, :]
    x1 = x[..., :half]
    x2 = x[..., half:ROPE_DIM]
    return jnp.concatenate([x1 * c - x2 * s, x2 * c + x1 * s, x[..., ROPE_DIM:]], axis=-1)

def mlstm_cell(q, k, v, log_i, log_f):
    nb, H, S, dk = q.shape
    dv = v.shape[-1]
    L = A_CHUNK
    nc = S // L

    def to_chunks(t):
        return jnp.moveaxis(t.reshape(nb, H, nc, L, *t.shape[3:]), 2, 0)

    xs = tuple(to_chunks(t) for t in (q, k, v, log_i, log_f))
    causal = jnp.tril(jnp.ones((L, L), dtype=bool))

    def step(carry, inp):
        C, n, m = carry
        qc, kc, vc, ic, fc = inp
        b = jnp.cumsum(fc, axis=-1)
        a = b + m[..., None]
        dlog = jnp.where(causal, b[..., :, None] - b[..., None, :] + ic[..., None, :], -jnp.inf)
        m_t = jnp.maximum(a, dlog.max(-1))
        dw = jnp.exp(dlog - m_t[..., None])
        inter = jnp.exp(a - m_t)
        s = jnp.einsum('bhtd,bhsd->bhts', qc, kc) * dw
        num = inter[..., None] * jnp.einsum('bhtd,bhvd->bhtv', qc, C) + jnp.einsum('bhts,bhsv->bhtv', s, vc)
        den = inter * jnp.einsum('bhtd,bhd->bht', qc, n) + s.sum(-1)
        h = num / jnp.maximum(jnp.abs(den), jnp.exp(-m_t))[..., None]
        b_last = b[..., -1]
        wlog = b_last[..., None] - b + ic
        m_new = jnp.maximum(b_last + m, wlog.max(-1))
        decay = jnp.exp(b_last + m - m_new)
        w = jnp.exp(wlog - m_new[..., None])
        C_new = decay[..., None, None] * C + jnp.einsum('bhs,bhsv,bhsd->bhvd', w, vc, kc)
        n_new = decay[..., None] * n + jnp.einsum('bhs,bhsd->bhd', w, kc)
        return (C_new, n_new, m_new), h

    init = (jnp.zeros((nb, H, dv, dk), jnp.float32),
            jnp.zeros((nb, H, dk), jnp.float32),
            jnp.zeros((nb, H), jnp.float32))
    _, hs = lax.scan(step, init, xs)
    return jnp.moveaxis(hs, 0, 2).reshape(nb, H, S, dv)

def mlstm_mixer(h, w_in, conv_w, conv_b, b_if, norm_g, w_out):
    nb, S, _ = h.shape
    p = h @ w_in
    qk, v, o, gates = jnp.split(p, [2 * A_QK, 2 * A_QK + A_V, 2 * A_QK + 2 * A_V], axis=-1)
    qk = lax.conv_general_dilated(qk, conv_w[:, None, :], window_strides=(1,),
                                  padding=[(A_CONV - 1, 0)],
                                  dimension_numbers=('NWC', 'WIO', 'NWC'),
                                  feature_group_count=2 * A_QK) + conv_b
    qk = jax.nn.silu(qk)
    q, k = jnp.split(qk, 2, axis=-1)

    def heads(t, d):
        return t.reshape(nb, S, A_HEADS, d).transpose(0, 2, 1, 3).astype(jnp.float32)

    q = heads(q, A_DK)
    k = heads(k, A_DK) * (A_DK ** -0.5)
    v = heads(v, A_DV)
    gates = (gates + b_if).astype(jnp.float32).transpose(0, 2, 1)
    log_i = gates[:, :A_HEADS]
    log_f = jax.nn.log_sigmoid(gates[:, A_HEADS:])
    hh = mlstm_cell(q, k, v, log_i, log_f).transpose(0, 2, 1, 3)
    hh = hh * lax.rsqrt(jnp.mean(hh * hh, -1, keepdims=True) + EPS)
    hh = hh.reshape(nb, S, A_V) * norm_g.astype(jnp.float32)
    y = (jax.nn.sigmoid(o.astype(jnp.float32)) * hh).astype(h.dtype)
    return y @ w_out

def diff_attn_mixer(h, cos, sin, w_in, lam, norm_g, w_out, lam_init):
    nb, S, _ = h.shape
    p = h @ w_in
    q, k, v = jnp.split(p, [B_QK, 2 * B_QK], axis=-1)
    q = rope_partial(q.reshape(nb, S, B_HEADS, 2, B_DH).astype(jnp.float32), cos, sin) * (B_DH ** -0.5)
    k = rope_partial(k.reshape(nb, S, B_HEADS, 2, B_DH).astype(jnp.float32), cos, sin)
    v = v.reshape(nb, S, B_HEADS, B_DV).astype(jnp.float32).transpose(0, 2, 1, 3)
    lf = lam.astype(jnp.float32)
    lam_full = jnp.exp(jnp.sum(lf[0] * lf[1])) - jnp.exp(jnp.sum(lf[2] * lf[3])) + lam_init
    q = q.transpose(0, 2, 3, 1, 4)
    k = k.transpose(0, 2, 3, 1, 4)
    n_blk = S // Q_BLOCK
    qb = jnp.moveaxis(q.reshape(nb, B_HEADS, 2, n_blk, Q_BLOCK, B_DH), 3, 0)
    k_idx = jnp.arange(S)

    def block(args):
        qblk, bi = args
        q_idx = bi * Q_BLOCK + jnp.arange(Q_BLOCK)
        s = jnp.einsum('bhcqd,bhckd->bhcqk', qblk, k)
        s = jnp.where(k_idx[None, :] <= q_idx[:, None], s, -jnp.inf)
        pr = jax.nn.softmax(s, axis=-1)
        a = pr[:, :, 0] - lam_full * pr[:, :, 1]
        return jnp.einsum('bhqk,bhkd->bhqd', a, v)

    o = lax.map(block, (qb, jnp.arange(n_blk)))
    o = jnp.moveaxis(o, 0, 2).reshape(nb, B_HEADS, S, B_DV).transpose(0, 2, 1, 3)
    o = o * lax.rsqrt(jnp.mean(o * o, -1, keepdims=True) + EPS) * norm_g.astype(jnp.float32) * (1.0 - lam_init)
    return o.reshape(nb, S, B_V).astype(h.dtype) @ w_out

def setup_inputs(seed: int = 0) -> dict:
    key = jax.random.key(seed)
    ks = jax.random.split(key, 24)
    f32 = jnp.float32

    def nrm(k, shape, scale):
        return jax.random.normal(k, shape, f32) * scale

    x = nrm(ks[0], (BATCH, SEQ, D_MODEL), 1.0)
    c = nrm(ks[1], (BATCH, D_MODEL), 1.0)
    offs = jax.random.randint(ks[2], (BATCH, 1), 0, 1024, dtype=jnp.int32)
    positions = (offs + jnp.arange(SEQ, dtype=jnp.int32)[None, :]).astype(jnp.int32)

    ada_w = nrm(ks[3], (DEPTH, D_MODEL, 9 * D_MODEL), 0.3 * D_MODEL ** -0.5)
    ada_base = jnp.zeros((DEPTH, 3, 3, D_MODEL), f32).at[:, :, 2, :].set(1.0)
    ada_b = (ada_base + nrm(ks[4], (DEPTH, 3, 3, D_MODEL), 0.02)).reshape(DEPTH, 9 * D_MODEL)
    norm_g = 1.0 + nrm(ks[5], (DEPTH, 3, D_MODEL), 0.02)
    ffn_w13 = nrm(ks[6], (DEPTH, 2, D_MODEL, 2 * D_FF), D_MODEL ** -0.5)
    ffn_w2 = nrm(ks[7], (DEPTH, 2, D_FF, D_MODEL), D_FF ** -0.5)

    a_w_in = nrm(ks[8], (N_A, D_MODEL, A_PROJ), D_MODEL ** -0.5)
    a_conv_w = nrm(ks[9], (N_A, A_CONV, 2 * A_QK), A_CONV ** -0.5)
    a_conv_b = nrm(ks[10], (N_A, 2 * A_QK), 0.02)
    i_bias = nrm(ks[11], (N_A, A_HEADS), 0.1)
    f_bias = jnp.linspace(3.0, 6.0, A_HEADS, dtype=f32)[None, :] + nrm(ks[12], (N_A, A_HEADS), 0.1)
    a_b_if = jnp.concatenate([i_bias, f_bias], axis=-1)
    a_norm_g = 1.0 + nrm(ks[13], (N_A, A_V), 0.02)
    a_w_out = nrm(ks[14], (N_A, A_V, D_MODEL), A_V ** -0.5)

    b_w_in = nrm(ks[15], (N_B, D_MODEL, B_PROJ), D_MODEL ** -0.5)
    b_lam = nrm(ks[16], (N_B, 4, B_DH), 0.1)
    b_norm_g = 1.0 + nrm(ks[17], (N_B, B_DV), 0.02)
    b_w_out = nrm(ks[18], (N_B, B_V, D_MODEL), B_V ** -0.5)

    final_g = 1.0 + nrm(ks[19], (D_MODEL,), 0.02)
    return {"x": x, "c": c, "positions": positions, "ada_w": ada_w, "ada_b": ada_b,
            "norm_g": norm_g, "ffn_w13": ffn_w13, "ffn_w2": ffn_w2,
            "a_w_in": a_w_in, "a_conv_w": a_conv_w, "a_conv_b": a_conv_b, "a_b_if": a_b_if,
            "a_norm_g": a_norm_g, "a_w_out": a_w_out,
            "b_w_in": b_w_in, "b_lam": b_lam, "b_norm_g": b_norm_g, "b_w_out": b_w_out,
            "final_g": final_g}

def reference(x, c, positions, ada_w, ada_b, norm_g, ffn_w13, ffn_w2,
              a_w_in, a_conv_w, a_conv_b, a_b_if, a_norm_g, a_w_out,
              b_w_in, b_lam, b_norm_g, b_w_out, final_g):
    inv_freq = ROPE_THETA ** (-jnp.arange(0, ROPE_DIM, 2, dtype=jnp.float32) / ROPE_DIM)
    ang = positions.astype(jnp.float32)[..., None] * inv_freq
    cos, sin = jnp.cos(ang), jnp.sin(ang)
    cond = jax.nn.silu(c)
    for i in range(DEPTH):
        ada = (cond @ ada_w[i] + ada_b[i]).reshape(-1, 3, 3, D_MODEL)
        h = modulate(x, norm_g[i, 0], ada[:, 0, 0], ada[:, 0, 1])
        x = x + 0.5 * ada[:, 0, 2, None, :] * swiglu(h, ffn_w13[i, 0], ffn_w2[i, 0])
        h = modulate(x, norm_g[i, 1], ada[:, 1, 0], ada[:, 1, 1])
        j = i // N_MIXERS
        if i % N_MIXERS == 0:
            y = mlstm_mixer(h, a_w_in[j], a_conv_w[j], a_conv_b[j], a_b_if[j], a_norm_g[j], a_w_out[j])
        else:
            lam_init = 0.8 - 0.6 * math.exp(-0.3 * i)
            y = diff_attn_mixer(h, cos, sin, b_w_in[j], b_lam[j], b_norm_g[j], b_w_out[j], lam_init)
        x = x + ada[:, 1, 2, None, :] * y
        h = modulate(x, norm_g[i, 2], ada[:, 2, 0], ada[:, 2, 1])
        x = x + 0.5 * ada[:, 2, 2, None, :] * swiglu(h, ffn_w13[i, 1], ffn_w2[i, 1])
    return rmsnorm(x, final_g)


_drawn_inputs = setup_inputs


def setup_inputs(seed=0):
    import zlib

    import numpy as np

    out = dict(_drawn_inputs(seed))
    spreads = {}
    factors = {'a_conv_b': 8.0, 'a_norm_g': 12.773, 'b_norm_g': 23.937, 'final_g': 7.907}
    for name, (base, spread) in spreads.items():
        noise = np.random.default_rng([zlib.crc32(name.encode()), seed]).standard_normal(out[name].shape)
        drawn = base * np.exp(spread * noise) if base else spread * noise
        out[name] = __import__('jax').numpy.asarray(drawn.astype(out[name].dtype))
    for name, factor in factors.items():
        out[name] = (out[name] * factor).astype(out[name].dtype)
    return out
```

```python
import math
from contextlib import ExitStack

import numpy as np
import concourse.bass as bass
from concourse import mybir

F32 = mybir.dt.float32
F32R = mybir.dt.float32r
I32 = mybir.dt.int32
ALU = mybir.AluOpType
ACT = mybir.ActivationFunctionType
AX = mybir.AxisListType

P = 128
D = 1024
S = 512
FF = 2816
KT = D // P
FT = FF // P
ST = S // P
HEADS = 4
DK = 128
DV = 256
TAPS = 4
EPS = 1e-6
LAYERS = 2
SUBS = 3 * LAYERS
ROPE_DIM = DK // 4
HALF = ROPE_DIM // 2
ROPE_THETA = 500000.0
LAM_INIT = 0.8 - 0.6 * math.exp(-0.3 * 1)
MASKED = -1e30

SLOTS = 4
RAWS = 2
W2_SPLIT = (6, 6, 5, 5)
W2_START = (0, 6, 12, 17)

N13 = 2 * FT
NW2 = 4 * KT
UNITS_FFN = N13 + NW2
UNITS_A = 8 + 1 + 8 + 8 + 8
UNITS_B = 16 + 8 + 8
U_F0 = 0
U_A = U_F0 + UNITS_FFN
U_F1 = U_A + UNITS_A
U_F2 = U_F1 + UNITS_FFN
U_B = U_F2 + UNITS_FFN
U_F3 = U_B + UNITS_B
U_END = U_F3 + UNITS_FFN
U_FFN = (U_F0, U_F1, U_F2, U_F3)

T_A = N13
T_F1 = T_A + 60
T_F2 = T_F1 + N13
T_B = T_F2 + N13
T_F3 = T_B + 68
T_FFN = (0, T_F1, T_F2, T_F3)
O_FFN = (0, 8, 12, 24)
O_A = 4
O_B = 16
N_FFN = (0, 2, 3, 5)
Q_FFN = (0, 3, 4, 7)
N_MIX = (1, 4)
Q_MIX = ((1, 2), (5, 6))

SLICES = 9 * LAYERS
EARLY = 2
ADA_F0 = FT // 2
ADA_F1 = SLICES - EARLY - ADA_F0

COLS = {}
_n = 0
for _name, _w in (("c", KT), ("ada_b", SLICES * KT), ("norm_g", SUBS * KT), ("final_g", KT),
                  ("conv_w", TAPS * 8), ("conv_b", 8), ("a_norm_g", 8), ("b_norm_g", 2), ("lam", 4)):
    COLS[_name] = _n
    _n += _w
N_COLS = _n

TWO_PI = 2.0 * math.pi


def two_pi_parts(step):
    rest, parts = step * TWO_PI, []
    for _ in range(4):
        scale = 2.0 ** (10 - math.floor(math.log2(rest)))
        part = math.floor(rest * scale) / scale
        parts.append(part)
        rest -= part
    return parts


def build_trunk(nc, xT, cols, gate_bias, rope_rows, positions, ada, w13, w2, wa, wb, out):
    ctx = ExitStack()
    with ctx:
        def sem(name):
            return ctx.enter_context(nc.semaphore(name))

        top = [(nc.sbuf_base + 63) // 64 * 64]

        def at(name, shape, dt, offset):
            return nc.alloc_sbuf_tensor_at(name, shape, dt, offset=offset)

        def place(name, shape, dt=F32):
            offset = top[0]
            top[0] += (int(np.prod(shape[1:])) * 4 + 31) // 32 * 32
            return at(name, shape, dt, offset)

        x = place("x", [P, KT, S])
        h_hi = place("h_hi", [P, KT, S], F32R)
        h_lo = place("h_lo", [P, KT, S], F32R)
        raw = [place(f"raw{i}", [P, 1024]) for i in range(RAWS)]
        w_hi = [place(f"w_hi{i}", [P, 1024], F32R) for i in range(SLOTS)]
        w_lo = [place(f"w_lo{i}", [P, 1024], F32R) for i in range(SLOTS)]
        buf = [place(f"buf{i}", [P, S]) for i in range(2)]
        sq = place("sq", [P, S])
        sumsq = place("sumsq", [P, S])
        rstd = place("rstd", [P, S])
        ada_region = top[0]
        ada_raw = [place(f"ada_raw{i}", [P, 1024]) for i in range(2)]
        ada_acc = place("ada_acc", [P, 1024])
        region = top[0]
        g_hi = place("g_hi", [P, FT, S], F32R)
        g_lo = place("g_lo", [P, FT, S], F32R)
        region_end = top[0]
        col = place("col", [P, N_COLS])
        ada_v = place("ada_v", [P, SLICES, KT])
        cond = place("cond", [P, KT])
        scale_col = place("scale_col", [P, KT])
        gate_col = place("gate_col", [P, KT])
        ones = place("ones", [P, P])
        ident = place("ident", [P, P])
        mask_st = place("mask_st", [P, P])
        mask_ts = place("mask_ts", [P, P])
        select = place("select", [HEADS, HEADS, P])
        eps = place("eps", [P, 1])
        rows_one = place("rows_one", [HEADS, S])
        gbias = place("gbias", [HEADS, 2])
        rope_row = place("rope_row", [ROPE_DIM, 2])
        lam_mul = place("lam_mul", [P, 2])
        lam_exp = place("lam_exp", [P, 2])
        neg_lam = place("neg_lam", [P, 1])
        u_col = place("u_col", [P, ST * HEADS])
        neg_max = place("neg_max", [P, 2, 2])
        row_max = place("row_max", [P, 2, 2])
        row_sum = place("row_sum", [P, 2, 2])
        row_inv = place("row_inv", [P, 2, 2])
        bg_col = place("bg_col", [P, 2])
        assert top[0] <= nc.sbuf_usable_end, (top[0], nc.sbuf_usable_end)

        def carve(parts, start, end):
            made = []
            for name, shape in parts:
                made.append(at(name, shape, F32, start))
                start += int(np.prod(shape[1:])) * 4
            assert start <= end, (parts, start - end)
            return made

        early_ada, x_sq, early_acc = carve(
            [("early_ada", [P, EARLY * KT, 1024]), ("x_sq", [P, KT, S]), ("early_acc", [P, 1024])],
            region, region_end)
        a_qk, a_v, a_o, a_h, neg_m, exp_m = carve(
            [("a_qk", [P, 8, S]), ("a_v", [P, ST, 1024]), ("a_o", [P, 8, S]), ("a_h", [P, 8, S]),
             ("neg_m", [P, HEADS, S]), ("exp_m", [P, HEADS, S])], region, region_end)
        rows = at("rows", [HEADS, 8, S], F32, region + 3 * 16384)
        WT_OFF = (0, 512, 896, 1152)
        a_wt = carve([("a_wt0", [P, 1280]), ("a_wt1", [P, 1280])], ada_region, region)
        b_qk, b_v, b_o, b_at0, b_at1, b_cos, b_sin, b_rot, b_tmp = carve(
            [("b_qk", [P, 16, S]), ("b_v", [P, ST, 1024]), ("b_o", [P, 8, S]),
             ("b_at0", [P, ST, S]), ("b_at1", [P, ST, S]),
             ("b_cos", [ROPE_DIM, S]), ("b_sin", [ROPE_DIM, S]), ("b_rot", [ROPE_DIM, S]),
             ("b_tmp", [ROPE_DIM, S])], region, region_end)
        b_at = (b_at0, b_at1)
        b_p = carve([("b_p0", [P, 2, S]), ("b_p1", [P, 2, S])], ada_region, region)
        pos_i = at("pos_i", [ROPE_DIM, S], I32, ada_region + 8192)

        acc = ctx.enter_context(nc.psum_tensor("acc", [P, 4, S], F32))
        outp = ctx.enter_context(nc.psum_tensor("outp", [P, 2, S], F32))
        stat = ctx.enter_context(nc.psum_tensor("stat", [P, S], F32))
        aux = ctx.enter_context(nc.psum_tensor("aux", [P, S], F32))

        raw_loaded = [sem(f"raw_loaded{i}") for i in range(RAWS)]
        hi_ready = sem("hi_ready")
        lo_ready = sem("lo_ready")
        unit_done = sem("unit_done")
        acc_free = [sem(f"acc_free{i}") for i in range(4)]
        out_free = [sem(f"out_free{i}") for i in range(2)]
        sq_done = sem("sq_done")
        sq_added = sem("sq_added")
        stat_done = sem("stat_done")
        std_ready = sem("std_ready")
        rstd_ready = sem("rstd_ready")
        scale_ready = sem("scale_ready")
        gate_ready = sem("gate_ready")
        src_ready = sem("src_ready")
        act_hi_ready = sem("act_hi_ready")
        act_lo_ready = sem("act_lo_ready")
        g_hi_ready = sem("g_hi_ready")
        g_lo_ready = sem("g_lo_ready")
        early_loaded = [sem(f"early_loaded{i}") for i in range(4)]
        ada_loaded = [sem(f"ada_loaded{i}") for i in range(2)]
        ada_used = sem("ada_used")
        early_used = sem("early_used")
        colsum_done = sem("colsum_done")
        ada_ready = sem("ada_ready")
        col_loaded = sem("col_loaded")
        small_loaded = sem("small_loaded")
        pos_loaded = sem("pos_loaded")
        x_loaded = sem("x_loaded")
        cond_ready = sem("cond_ready")
        pool_consts = sem("pool_consts")
        dve_consts = sem("dve_consts")
        lam_mul_ready = sem("lam_mul_ready")
        lam_sum_done = sem("lam_sum_done")
        lam_exp_ready = sem("lam_exp_ready")
        lam_ready = sem("lam_ready")
        a_qk_ready = sem("a_qk_ready")
        f_arg_ready = sem("f_arg_ready")
        f_log_ready = sem("f_log_ready")
        m_rows_ready = sem("m_rows_ready")
        em_row_ready = sem("em_row_ready")
        u_turned = sem("u_turned")
        u_col_ready = sem("u_col_ready")
        spread_done = sem("spread_done")
        diag_ready = sem("diag_ready")
        decay_ready = sem("decay_ready")
        st_done = sem("st_done")
        av_done = sem("av_done")
        den_read = sem("den_read")
        a_sq_ready = sem("a_sq_ready")
        a_ss_done = sem("a_ss_done")
        trig_arg = sem("trig_arg")
        trig_ready = sem("trig_ready")
        rope_done = sem("rope_done")
        s_done = sem("s_done")
        max_ready = sem("max_ready")
        p_ready = sem("p_ready")
        turned = sem("turned")
        pv_done = sem("pv_done")
        b_o_ready = sem("b_o_ready")
        b_sq_ready = sem("b_sq_ready")
        b_ss_done = sem("b_ss_done")
        stored = sem("stored")
        dve_step = sem("dve_step")
        act_step = sem("act_step")
        pool_step = sem("pool_step")

        def read_out(eng, use):
            eng.wait_ge(acc_free[use % 4], use // 4 + 1)

        block = ctx.enter_context(nc.Block())

        @block.sync
        def _(sp):
            def load_unit(u, src, n=1024, wait=None):
                base, more = u
                if wait is not False:
                    sp.wait_ge(lo_ready, base + more - RAWS + 1)
                sp.dma_start(raw[base % RAWS][:, 0:n], src).then_inc(raw_loaded[base % RAWS], 16)

            def load_ada(sl, first, more=0):
                for k in range(first, first + 4):
                    a = (sl - EARLY) * KT + k
                    if a >= 2:
                        sp.wait_ge(ada_used, a + more * KT - 1)
                    sp.dma_start(ada_raw[k % 2][:, :], ada[EARLY * KT + a + more * KT])\
                      .then_inc(ada_loaded[k % 2], 16)

            def ffn(p, ada_first, ada_steps):
                U = U_FFN[p]
                last = FT // 2 - 1

                def load13(n, more=0):
                    load_unit((U + n, 4 * more), w13[p * N13 + n + 4 * more],
                              wait=None if U + n >= RAWS else False)

                def load2(o, m, more=0):
                    n, k0 = W2_SPLIT[m] * P, W2_START[m] * P
                    load_unit((U + N13 + 4 * o + m, 4 * more), w2[p * KT + o + more][:, k0:k0 + n], n)

                def step(i, more, with_ada):
                    for j in range(2):
                        load13(4 * i + 4 + 2 * j, more)
                        load13(4 * i + 5 + 2 * j, more)
                        if with_ada:
                            load_ada(ada_first + i, 4 * j, more)

                for n in range(4):
                    load13(n)
                if ada_steps:
                    step(0, 0, True)
                    with sp.Fori(0, min(ada_steps, last) - 1) as i:
                        step(1, i, True)
                done = min(ada_steps, last)
                if done < last:
                    with sp.Fori(0, last - done) as i:
                        step(done, i, False)
                for j in range(2):
                    load2(0, 2 * j)
                    load2(0, 2 * j + 1)
                    if ada_steps > last:
                        load_ada(ada_first + last, 4 * j)
                with sp.Fori(0, KT - 1) as o:
                    for m in range(4):
                        load2(1, m, o)

            for c in range(4):
                sp.dma_start(early_ada[:, 4 * c:4 * c + 4, :],
                             ada[4 * c:4 * c + 4].rearrange("u p n -> p u n")).then_inc(early_loaded[c], 16)
            ffn(0, EARLY, ADA_F0)
            with sp.Fori(0, (UNITS_A - 1) // 4) as i:
                for k in range(4):
                    load_unit((U_A + k, 4 * i), wa[4 * i + k])
            load_unit((U_A + UNITS_A - 1, 0), wa[UNITS_A - 1])
            ffn(1, EARLY + ADA_F0, ADA_F1)
            ffn(2, 0, 0)
            sp.wait_ge(ada_ready, SLICES)
            sp.dma_start(pos_i[:, :], positions.partition_broadcast(ROPE_DIM) if False else
                         positions.broadcast_to([ROPE_DIM, S])).then_inc(pos_loaded, 16)
            with sp.Fori(0, UNITS_B // 4) as i:
                for k in range(4):
                    load_unit((U_B + k, 4 * i), wb[4 * i + k])
            ffn(3, 0, 0)
            for k in range(KT):
                sp.wait_ge(src_ready, 8 * 8 + k + 1)
                sp.dma_start(out[k], x[:, k, :]).then_inc(stored, 16)
            sp.wait_ge(stored, 16 * KT)

        @block.gpsimd
        def _(pool):
            pool.memset(ident[:, :], 0.0).then_inc(pool_step, 1)
            pool.memset(mask_st[:, :], 0.0).then_inc(pool_step, 1)
            pool.memset(mask_ts[:, :], 0.0).then_inc(pool_step, 1)
            pool.memset(select[:, :, :], 0.0).then_inc(pool_step, 1)
            pool.memset(ones[:, :], 1.0).then_inc(pool_consts, 1)
            pool.memset(eps[:, :], EPS).then_inc(pool_consts, 1)
            pool.wait_ge(pool_step, 4)
            pool.affine_select(out=ident[:, :], in_=ident[:, :], compare_op=ALU.not_equal, fill=1.0,
                               base=0, pattern=[[-1, P]], channel_multiplier=1).then_inc(pool_consts, 1)
            pool.affine_select(out=mask_st[:, :], in_=mask_st[:, :], compare_op=ALU.is_ge, fill=MASKED,
                               base=0, pattern=[[1, P]], channel_multiplier=-1).then_inc(pool_consts, 1)
            pool.affine_select(out=mask_ts[:, :], in_=mask_ts[:, :], compare_op=ALU.is_ge, fill=MASKED,
                               base=0, pattern=[[-1, P]], channel_multiplier=1).then_inc(pool_consts, 1)
            pool.affine_select(out=select[:, :, :], in_=select[:, :, :], compare_op=ALU.not_equal, fill=1.0,
                               base=0, pattern=[[-1, HEADS], [0, P]], channel_multiplier=1)\
                .then_inc(pool_consts, 1)

            def low_part(base, more, n=1024):
                pool.wait_ge(hi_ready, base + more + 1)
                s = base % SLOTS
                pool.tensor_tensor(w_lo[s][:, 0:n], raw[base % RAWS][:, 0:n],
                                   w_hi[s][:, 0:n].bitcast(F32), ALU.subtract).then_inc(lo_ready, 1)

            def group_loop(U, n):
                with pool.Fori(0, n) as i:
                    for k in range(4):
                        low_part(U + k, 4 * i)

            def ffn(p):
                group_loop(U_FFN[p], N13 // 4)
                with pool.Fori(0, KT) as o:
                    for m in range(4):
                        low_part(U_FFN[p] + N13 + m, 4 * o, W2_SPLIT[m] * P)

            ffn(0)
            group_loop(U_A, (UNITS_A - 1) // 4)
            low_part(U_A + UNITS_A - 1, 0)
            ffn(1)
            ffn(2)
            group_loop(U_B, UNITS_B // 4)
            ffn(3)

        @block.tensor
        def _(pe):
            def three(bank, a_hi, a_lo, b_hi, b_lo, start, stop):
                pe.matmul(bank, a_hi, b_hi, start=start, stop=False)
                pe.matmul(bank, a_hi, b_lo, start=False, stop=False)
                return pe.matmul(bank, a_lo, b_hi, start=False, stop=stop)

            def block_of(s, n):
                return w_hi[s][:, n * P:(n + 1) * P], w_lo[s][:, n * P:(n + 1) * P]

            def take_acc(use):
                if use >= 4:
                    pe.wait_ge(acc_free[use % 4], use // 4)

            def unit(base, more, bank):
                pe.wait_ge(lo_ready, base + more + 1)
                for k in range(KT):
                    last = three(bank, *block_of(base % SLOTS, k), h_hi[:, k, :], h_lo[:, k, :],
                                 k == 0, k == KT - 1)
                last.then_inc(unit_done, 1)

            def first_group(U, T, q):
                for k in range(KT):
                    pe.wait_ge(act_lo_ready, 8 * q + k + 1)
                    for s in range(4):
                        if k == 0:
                            pe.wait_ge(lo_ready, U + s + 1)
                            take_acc(T + s)
                        last = three(acc[:, (T + s) % 4, :], *block_of((U + s) % SLOTS, k),
                                     h_hi[:, k, :], h_lo[:, k, :], k == 0, k == KT - 1)
                        if k == KT - 1:
                            last.then_inc(unit_done, 1)

            def v_groups(U, T):
                for half in range(2):
                    for m in range(4):
                        u = U + 4 * half + m
                        s = u % SLOTS
                        pe.wait_ge(lo_ready, u + 1)
                        for tt in range(ST):
                            if m == 0:
                                take_acc(T + 4 * half + tt)
                            for kk in range(2):
                                k = 2 * m + kk
                                t0 = tt * P
                                last = three(acc[:, tt, :], h_hi[:, k, t0:t0 + P], h_lo[:, k, t0:t0 + P],
                                             w_hi[s][:, kk * 512:kk * 512 + 512],
                                             w_lo[s][:, kk * 512:kk * 512 + 512],
                                             k == 0, k == KT - 1)
                        last.then_inc(unit_done, 1)

            def colsum(sums, n):
                for t in range(KT):
                    last = pe.matmul(aux[:, t:t + 1], sums[:, t * P:(t + 1) * P], ones[:, 0:1],
                                     start=True, stop=True)
                last.then_inc(colsum_done, 1)

            def norm_sum(n):
                pe.wait_ge(sq_added, 9 * n)
                pe.wait_ge(std_ready, n)
                pe.matmul(stat[:, :], ones[:, :], sumsq[:, :], start=True, stop=True).then_inc(stat_done, 1)

            def ffn(p, ada_first, ada_steps):
                U, T, q = U_FFN[p], T_FFN[p], Q_FFN[p]
                first_group(U, T, q)

                def step(i, more, with_ada):
                    for k in range(4):
                        pe.wait_ge(acc_free[k], T // 4 + i + more)
                        unit(U + 4 * i + k, 4 * more, acc[:, k, :])
                        if k == 1 and with_ada:
                            pe.wait_ge(ada_used, 8 * (ada_first - EARLY + i + more))
                            pe.wait_ge(ada_ready, ada_first + i - 1 + more)
                            colsum(ada_acc, 0)

                if ada_steps:
                    n = min(ada_steps, FT // 2 - 1)
                    with pe.Fori(0, n) as i:
                        step(1, i, True)
                    if n + 1 < FT // 2:
                        with pe.Fori(0, FT // 2 - 1 - n) as i:
                            step(n + 1, i, False)
                    if n < ada_steps:
                        pe.wait_ge(ada_used, 8 * (ada_first - EARLY + ada_steps))
                        pe.wait_ge(ada_ready, ada_first + ada_steps - 1)
                        colsum(ada_acc, 0)
                else:
                    with pe.Fori(0, FT // 2 - 1) as i:
                        step(1, i, False)
                with pe.Fori(0, KT // 2) as i:
                    for j in range(2):
                        pe.wait_ge(out_free[j], O_FFN[p] + 1 + i)
                        for m in range(4):
                            base = U + N13 + 4 * j + m
                            pe.wait_ge(lo_ready, base + 1 + 8 * i)
                            pe.wait_ge(g_lo_ready, FT * p + W2_START[m] + W2_SPLIT[m])
                            for b in range(W2_SPLIT[m]):
                                kt = W2_START[m] + b
                                last = three(outp[:, j, :], *block_of(base % SLOTS, b),
                                             g_hi[:, kt, :], g_lo[:, kt, :], kt == 0, kt == FT - 1)
                            last.then_inc(unit_done, 1)
                norm_sum(N_FFN[p] + 1)

            def out_projection(U, T, q):
                first_group(U, T, q)
                for s in range(4, 8):
                    take_acc(T + s)
                    unit(U + s, 0, acc[:, s % 4, :])

            def mixer_a():
                U, T = U_A, T_A
                first_group(U, T, 1)
                for s in range(4, 8):
                    take_acc(T + s)
                    unit(U + s, 0, acc[:, s % 4, :])
                pe.wait_ge(ada_ready, EARLY + ADA_F0)
                unit(U + 8, 0, aux[:, :])
                v_groups(U + 9, T + 8)
                for s in range(8):
                    take_acc(T + 16 + s)
                    unit(U + 17 + s, 0, acc[:, s % 4, :])
                pe.wait_ge(m_rows_ready, 1)
                for j in range(ST):
                    last = pe.transpose(stat[:, 4 * j:4 * j + 4], rows[:, 2, j * P:(j + 1) * P],
                                        ident[0:HEADS, 0:HEADS])
                last.then_inc(u_turned, 1)
                for h in range(HEADS):
                    take_acc(T + 24 + h)
                    pe.matmul(acc[:, h, :], select[:, h, :], rows[:, 4, :], start=True, stop=True)\
                      .then_inc(spread_done, 1)
                pe.wait_ge(em_row_ready, 1)
                for h in range(HEADS):
                    take_acc(T + 28 + h)
                    pe.matmul(acc[:, h, :], select[:, h, :], rows[:, 6, :], start=True, stop=True)\
                      .then_inc(spread_done, 1)
                pe.wait_ge(a_qk_ready, 8)

                def scores(h):
                    for j in range(ST):
                        take_acc(T + 32 + 4 * h + j)
                        pe.matmul(acc[:, j, 0:S - j * P], a_qk[:, 4 + h, j * P:(j + 1) * P],
                                  a_qk[:, h, j * P:S], start=True, stop=True).then_inc(st_done, 1)

                def mix(h):
                    pe.wait_ge(out_free[0], O_A + h + 1)
                    pe.wait_ge(out_free[1], O_A + h + 1)
                    if h:
                        pe.wait_ge(den_read, h)
                    for j in range(ST):
                        read_out(pe, T + 32 + 4 * h + j)
                        w = a_wt[h % 2][:, WT_OFF[j]:WT_OFF[j] + S - j * P]
                        pe.matmul(aux[:, j * P:S], ones[:, :], w, start=j == 0, stop=j == ST - 1)
                        for d in range(2):
                            c0 = h * DV + d * P
                            last = pe.matmul(outp[:, d, j * P:S], a_v[:, j, c0:c0 + P], w,
                                             start=j == 0, stop=j == ST - 1)
                    last.then_inc(av_done, 1)

                scores(0)
                for h in range(HEADS):
                    if h + 1 < HEADS:
                        scores(h + 1)
                    mix(h)
                head_sums(a_qk, T + 48, a_sq_ready, a_ss_done)
                out_projection(U + 25, T + 52, 2)
                norm_sum(2)

            def head_sums(squares, T, ready, done):
                for h in range(HEADS):
                    pe.wait_ge(ready, h + 1)
                    take_acc(T + h)
                    pe.matmul(acc[:, h, :], ones[:, :], squares[:, 2 * h, :], start=True, stop=False)
                    pe.matmul(acc[:, h, :], ones[:, :], squares[:, 2 * h + 1, :], start=False, stop=True)\
                      .then_inc(done, 1)

            def mixer_b():
                U, T = U_B, T_B
                first_group(U, T, 5)
                for s in range(4, 16):
                    take_acc(T + s)
                    unit(U + s, 0, acc[:, s % 4, :])
                v_groups(U + 16, T + 16)

                def scores(n):
                    h, i = divmod(n, ST)
                    for c in range(2):
                        use = T + 24 + 2 * n + c
                        take_acc(use)
                        pe.matmul(acc[:, use % 4, 0:(i + 1) * P], b_qk[:, 2 * h + c, i * P:(i + 1) * P],
                                  b_qk[:, 8 + 2 * h + c, 0:(i + 1) * P], start=True, stop=True)\
                          .then_inc(s_done, 1)

                def turn(n):
                    h, i = divmod(n, ST)
                    pe.wait_ge(p_ready, n + 1)
                    pe.wait_ge(out_free[n % 2], O_B + n // 2 + 1)
                    for j in range(i + 1):
                        last = pe.transpose(outp[:, n % 2, j * P:(j + 1) * P],
                                            b_p[n % 2][:, 0, j * P:(j + 1) * P], ident[:, :])
                    last.then_inc(turned, 1)

                def mix(h):
                    for j in range(2):
                        pe.wait_ge(out_free[j], O_B + 1 + 2 * h + 2)
                    if h:
                        pe.wait_ge(b_o_ready, h)
                    for d, bank in enumerate((stat, aux)):
                        c0 = h * DV + d * P
                        for j in range(ST):
                            last = pe.matmul(bank[:, j * P:S], b_v[:, j, c0:c0 + P],
                                             b_at[h % 2][:, j, j * P:S], start=j == 0, stop=j == ST - 1)
                    last.then_inc(pv_done, 1)

                pe.wait_ge(rope_done, 16)
                pe.wait_ge(std_ready, 5)
                for n in range(4 * HEADS + 2):
                    if n < 4 * HEADS:
                        scores(n)
                    if 1 <= n <= 4 * HEADS:
                        turn(n - 1)
                    if n >= 5 and (n - 5) % 4 == 0:
                        mix((n - 5) // 4)
                head_sums(b_qk, T + 56, b_sq_ready, b_ss_done)
                out_projection(U + 24, T + 60, 6)
                norm_sum(5)

            pe.wait_ge(pool_consts, 6)
            for k in range(KT):
                pe.wait_ge(sq_done, k + 1)
                last = pe.matmul(stat[:, :], ones[:, :], x_sq[:, k, :], start=k == 0, stop=k == KT - 1)
            last.then_inc(stat_done, 1)
            pe.wait_ge(lam_mul_ready, 1)
            pe.matmul(aux[:, 16:18], ones[:, :], lam_mul[:, :], start=True, stop=True).then_inc(lam_sum_done, 1)
            pe.wait_ge(lam_exp_ready, 1)
            pe.wait_ge(early_used, KT)
            colsum(ada_acc, 0)
            pe.wait_ge(early_used, 2 * KT)
            pe.wait_ge(ada_ready, 1)
            colsum(early_acc, 1)
            ffn(0, EARLY, ADA_F0)
            mixer_a()
            ffn(1, EARLY + ADA_F0, ADA_F1)
            ffn(2, 0, 0)
            mixer_b()
            ffn(3, 0, 0)

        @block.scalar
        def _(act):
            def high_part(base, more=0, n=1024):
                act.wait_ge(raw_loaded[base % RAWS], 16 * (base // RAWS + 1) + (16 // RAWS) * more)
                if base >= SLOTS:
                    act.wait_ge(unit_done, base + more - SLOTS + 1)
                act.activation(w_hi[base % SLOTS][:, 0:n], raw[base % RAWS][:, 0:n], ACT.Copy)\
                   .then_inc(hi_ready, 1)

            def split_high(q, bias=None):
                for k in range(KT):
                    act.wait_ge(src_ready, 8 * q + k + 1)
                    if bias is None:
                        ins = act.activation(h_hi[:, k, :], buf[k % 2][:, :], ACT.Copy)
                    else:
                        ins = act.activation(h_hi[:, k, :], buf[k % 2][:, :], ACT.Identity,
                                             bias=bias[:, k:k + 1])
                    ins.then_inc(act_hi_ready, 1)

            def root(n):
                act.wait_ge(stat_done, n + 1)
                act.activation(sq[:, :], stat[:, :], ACT.Sqrt, bias=eps[:, 0:1], scale=1.0 / D)\
                   .then_inc(std_ready, 1)

            def norm(n, q):
                root(n)
                act.wait_ge(ada_ready, 3 * n + 1)
                split_high(q, ada_v[:, 3 * n, :])

            def square(r, o, more=0, xs=None):
                act.wait_ge(sq_added, 9 * r + o + 1 + more)
                act.activation(sq[:, :], x[:, o, :] if xs is None else xs, ACT.Square).then_inc(sq_done, 1)

            def ffn(p):
                U, T, r = U_FFN[p], T_FFN[p], N_FFN[p]
                norm(r, Q_FFN[p])

                def step(i, more):
                    for j in range(2):
                        u, f = U + 4 * i + 2 * j, 2 * i + j
                        F = FT * p + f
                        act.wait_ge(unit_done, u + 1 + 4 * more)
                        if F >= 2:
                            act.wait_ge(g_lo_ready, F - 1 + 2 * more)
                        act.activation(buf[j][:, :], acc[:, 2 * j, :], ACT.Silu)\
                           .then_inc(acc_free[2 * j], 1)
                        high_part(u + 4, 4 * more)
                        act.wait_ge(acc_free[2 * j + 1], T // 4 + i + 1 + more)
                        dst = g_hi[:, f, :] if isinstance(more, int) else \
                            g_hi[:, bass.ds(2 * more + f, 1), :].rearrange("p a s -> p (a s)")
                        act.activation(dst, buf[j][:, :], ACT.Copy).then_inc(g_hi_ready, 1)
                        high_part(u + 5, 4 * more)

                step(0, 0)
                with act.Fori(0, FT // 2 - 1) as i:
                    step(1, i)
                W = U + N13

                act.preload_act_table(ACT.Sqrt)

                def out_tile(o, more, split, n=None):
                    if split:
                        for m in range(4):
                            high_part(W + 4 * (o + 1) + m, 8 * more, n or W2_SPLIT[m] * P)
                    act.wait_ge(out_free[o % 2], O_FFN[p] + 1 + o // 2 + 1 + more)
                    if isinstance(more, int):
                        square(r, o)
                    else:
                        square(r, o, 2 * more, x[:, bass.ds(2 * more + o, 1), :].rearrange("p a s -> p (a s)"))

                with act.Fori(0, KT // 2 - 1) as i:
                    out_tile(0, i, True)
                    out_tile(1, i, True)
                out_tile(KT - 2, 0, True)
                out_tile(KT - 1, 0, p < 3, 1024)

            def out_projection(U, T, r):
                act.preload_act_table(ACT.Sqrt)
                for o in range(KT):
                    high_part(U + o + 4)
                    read_out(act, T + o)
                    square(r, o)

            def mixer_a():
                U, T = U_A, T_A
                norm(1, 1)
                for t in range(8):
                    high_part(U + t + 4)
                    read_out(act, T + t)
                    act.activation(a_qk[:, t, :], buf[t % 2][:, :], ACT.Silu).then_inc(a_qk_ready, 1)
                high_part(U + 12)
                act.wait_ge(f_arg_ready, 1)
                act.activation(rows[:, 5, :], rows[:, 3, :], ACT.Exp).then_inc(act_step, 1)
                act.wait_ge(act_step, 1)
                act.activation(rows[:, 6, :], rows[:, 5, :], ACT.Ln, bias=1.0).then_inc(f_log_ready, 1)
                v_evac(U + 9, a_v)
                act.wait_ge(m_rows_ready, 1)
                act.activation(rows[:, 6, :], rows[:, 5, :], ACT.Exp, scale=-1.0).then_inc(em_row_ready, 1)
                for t in range(8):
                    act.wait_ge(unit_done, U + 17 + t + 1)
                    act.activation(a_o[:, t, :], acc[:, t % 4, :], ACT.Sigmoid).then_inc(acc_free[t % 4], 1)
                    high_part(U + 17 + t + 4)
                for n, dst in ((0, neg_m), (1, exp_m)):
                    for h in range(HEADS):
                        act.wait_ge(spread_done, 4 * n + h + 1)
                        act.activation(dst[:, h, :], acc[:, h, :], ACT.Copy).then_inc(acc_free[h], 1)
                act.wait_ge(u_col_ready, 1)
                for h in range(HEADS):
                    act.wait_ge(diag_ready, h + 1)
                    read_out(act, T + 24 + h)
                    if h >= 2:
                        act.wait_ge(av_done, h - 1)
                    for j in range(ST):
                        u = u_col[:, 4 * j + h:4 * j + h + 1]
                        o = WT_OFF[j]
                        ins = act.activation(a_wt[h % 2][:, o:o + P], buf[h % 2][:, j * P:(j + 1) * P],
                                             ACT.Exp, bias=u)
                        if j < ST - 1:
                            ins = act.activation(a_wt[h % 2][:, o + P:o + S - j * P],
                                                 neg_m[:, h, (j + 1) * P:S], ACT.Exp, bias=u)
                    ins.then_inc(decay_ready, 1)
                act.wait_ge(st_done, 16)

                def wait_head(h):
                    for d in range(2):
                        act.wait_ge(out_free[d], O_A + 1 + h + 1)
                squares_and_roots(a_h, wait_head, a_qk, a_sq_ready, a_ss_done, exp_m)
                split_high(2)
                out_projection(U + 25, T + 52, 1)

            def squares_and_roots(h_src, wait_head, squares, sq_rdy, ss_done, std):
                for h in range(HEADS):
                    wait_head(h)
                    act.activation(squares[:, 2 * h:2 * h + 2, :], h_src[:, 2 * h:2 * h + 2, :], ACT.Square)\
                       .then_inc(sq_rdy, 1)
                for h in range(HEADS):
                    act.wait_ge(ss_done, h + 1)
                    act.activation(std[:, h, :], acc[:, h, :], ACT.Sqrt, bias=eps[:, 0:1], scale=1.0 / DV)\
                       .then_inc(acc_free[h], 1)

            def v_evac(U, dst):
                for half in range(2):
                    for m in range(4):
                        high_part(U + 4 * half + m + 4)
                    act.wait_ge(unit_done, U + 4 * half + 4)
                    for tt in range(2):
                        act.activation(dst[:, tt, half * 512:half * 512 + 512], acc[:, tt, :], ACT.Copy)\
                           .then_inc(acc_free[tt], 1)

            def mixer_b():
                U, T = U_B, T_B
                norm(4, 5)
                for t in range(16):
                    high_part(U + t + 4)
                    act.wait_ge(unit_done, U + t + 1)
                    act.activation(b_qk[:, t, :], acc[:, t % 4, :], ACT.Copy,
                                   scale=DK ** -0.5 if t < 8 else 1.0)\
                       .then_inc(acc_free[t % 4], 1)
                    if t == 3:
                        act.wait_ge(trig_arg, 2)
                        act.activation(b_cos[:, :], b_cos[:, :], ACT.Sin).then_inc(trig_ready, 1)
                        act.activation(b_sin[:, :], b_sin[:, :], ACT.Sin).then_inc(trig_ready, 1)
                v_evac(U + 16, b_v)

                def exps(n):
                    h, i = divmod(n, ST)
                    act.wait_ge(max_ready, n + 1)
                    if n >= 2:
                        act.wait_ge(turned, n - 1)
                        act.wait_ge(p_ready, n - 1)
                    for c in range(2):
                        b = (T + 24 + 2 * n + c) % 4
                        act.activation(b_p[n % 2][:, c, 0:(i + 1) * P], acc[:, b, 0:(i + 1) * P], ACT.Exp,
                                       bias=neg_max[:, n % 2, c:c + 1], accum_out=row_sum[:, n % 2, c:c + 1])\
                           .then_inc(acc_free[b], 1)

                def keep(n):
                    h, i = divmod(n, ST)
                    act.wait_ge(turned, n + 1)
                    if h >= 2:
                        act.wait_ge(pv_done, h - 1)
                    act.activation(b_at[h % 2][:, 0:i + 1, i * P:(i + 1) * P],
                                   outp[:, n % 2, 0:(i + 1) * P].rearrange("p (j k) -> p j k", k=P), ACT.Copy)\
                       .then_inc(out_free[n % 2], 1)

                for n in range(4 * HEADS + 1):
                    if n < 4 * HEADS:
                        exps(n)
                    if n >= 1:
                        keep(n - 1)
                squares_and_roots(b_o, lambda h: act.wait_ge(b_o_ready, h + 1), b_qk, b_sq_ready, b_ss_done,
                                  b_at0)
                split_high(6)
                out_projection(U + 24, T + 60, 4)

            act.dma_start(col[:, :], cols).then_inc(col_loaded, 16)
            act.dma_start(x[:, :, :], xT).then_inc(x_loaded, 16)
            act.dma_start(gbias[:, :], gate_bias).then_inc(small_loaded, 16)
            act.dma_start(rope_row[:, :], rope_rows).then_inc(small_loaded, 16)
            act.wait_ge(col_loaded, 16)
            act.activation(cond[:, :], col[:, COLS["c"]:COLS["c"] + KT], ACT.Silu).then_inc(cond_ready, 1)
            act.wait_ge(x_loaded, 16)
            for k in range(KT):
                act.activation(x_sq[:, k, :], x[:, k, :], ACT.Square).then_inc(sq_done, 1)
            act.wait_ge(lam_sum_done, 1)
            act.activation(lam_exp[:, :], aux[:, 16:18], ACT.Exp).then_inc(lam_exp_ready, 1)
            act.wait_ge(pool_consts, 6)
            for u in range(SLOTS):
                high_part(u)
            ffn(0)
            mixer_a()
            ffn(1)
            ffn(2)
            mixer_b()
            ffn(3)
            root(6)

        @block.vector
        def _(dve):
            chain = [0]

            def link(ins):
                chain[0] += 1
                ins.then_inc(dve_step, 1)
                dve.wait_ge(dve_step, chain[0])

            def colv(name, k, n=1):
                return col[:, COLS[name] + k:COLS[name] + k + n]

            def lows(q, bias, make):
                def low(k):
                    dve.wait_ge(act_hi_ready, 8 * q + k + 1)
                    hi = h_hi[:, k, :].bitcast(F32)
                    if bias is None:
                        ins = dve.tensor_tensor(h_lo[:, k, :], buf[k % 2][:, :], hi, ALU.subtract)
                    else:
                        ins = dve.scalar_tensor_tensor(out=h_lo[:, k, :], in0=buf[k % 2][:, :],
                                                       scalar=bias[:, k:k + 1], in1=hi,
                                                       op0=ALU.add, op1=ALU.subtract)
                    ins.then_inc(act_lo_ready, 1)

                for k in range(KT + 1):
                    if k < KT:
                        make(k)
                    if k >= 1:
                        low(k - 1)

            def norm(n, q):
                dve.wait_ge(ada_ready, 3 * n + 2)
                dve.scalar_tensor_tensor(out=scale_col[:, :], in0=ada_v[:, 3 * n + 1, :], scalar=1.0,
                                         in1=colv("norm_g", n * KT, KT), op0=ALU.add, op1=ALU.mult)\
                   .then_inc(scale_ready, 1)
                dve.wait_ge(std_ready, n + 1)
                dve.reciprocal(rstd[:, :], sq[:, :]).then_inc(rstd_ready, 1)
                dve.wait_ge(scale_ready, n + 1)
                dve.wait_ge(rstd_ready, n + 1)

                def make(k):
                    if k >= 2:
                        dve.wait_ge(act_lo_ready, 8 * q + k - 1)
                    dve.scalar_tensor_tensor(out=buf[k % 2][:, :], in0=x[:, k, :],
                                             scalar=scale_col[:, k:k + 1], in1=rstd[:, :],
                                             op0=ALU.mult, op1=ALU.mult).then_inc(src_ready, 1)
                lows(q, ada_v[:, 3 * n, :], make)

            def prepare_residual(r, factor):
                dve.wait_ge(ada_ready, 3 * r + 3)
                dve.tensor_scalar(gate_col[:, :], ada_v[:, 3 * r + 2, :], factor, None, ALU.mult)\
                   .then_inc(gate_ready, 1)
                dve.memset(sumsq[:, :], 0.0).then_inc(sq_added, 1)
                dve.wait_ge(gate_ready, r + 1)

            def residual(r, o, bank, free, more=0, dyn=None):
                xs = x[:, o, :] if dyn is None else x[:, bass.ds(dyn, 1), :].rearrange("p a s -> p (a s)")
                g = gate_col[:, o:o + 1] if dyn is None else gate_col[:, bass.ds(dyn, 1)]
                dve.scalar_tensor_tensor(out=xs, in0=bank, scalar=g, in1=xs, op0=ALU.mult, op1=ALU.add)\
                   .then_inc(free, 1)
                dve.wait_ge(sq_done, 8 + 8 * r + o + 1 + more)
                dve.wait_ge(sq_added, 9 * r + o + 1 + more)
                dve.tensor_tensor(sumsq[:, :], sumsq[:, :], sq[:, :], ALU.add).then_inc(sq_added, 1)

            def ada_evac(sl, more=0):
                dve.wait_ge(colsum_done, sl + 1 + more)
                if isinstance(more, int):
                    dst, b = ada_v[:, sl + more, :], colv("ada_b", (sl + more) * KT, KT)
                else:
                    dst = ada_v[:, bass.ds(more + sl, 1), :].rearrange("p a s -> p (a s)")
                    b = col[:, bass.ds(8 * more + COLS["ada_b"] + sl * KT, KT)]
                dve.tensor_tensor(dst, aux[:, 0:KT], b, ALU.add).then_inc(ada_ready, 1)

            def ada_half(sl, first, more=0):
                for k in range(first, first + 4):
                    a = (sl - EARLY) * KT + k
                    dve.wait_ge(ada_loaded[k % 2], 16 * (a // 2 + 1) + 64 * more)
                    if k == 0:
                        dve.wait_ge(colsum_done, sl + more)
                        ins = dve.tensor_scalar(ada_acc[:, :], ada_raw[0][:, :], cond[:, 0:1], None, ALU.mult)
                    else:
                        dve.wait_ge(ada_used, a + 8 * more)
                        ins = dve.scalar_tensor_tensor(out=ada_acc[:, :], in0=ada_raw[k % 2][:, :],
                                                       scalar=cond[:, k:k + 1], in1=ada_acc[:, :],
                                                       op0=ALU.mult, op1=ALU.add)
                    ins.then_inc(ada_used, 1)

            def ffn(p, ada_first, ada_steps):
                U, T, r = U_FFN[p], T_FFN[p], N_FFN[p]
                norm(r, Q_FFN[p])

                def step(i, more, halves, evac):
                    for j in range(2):
                        u, f = U + 4 * i + 2 * j, 2 * i + j
                        F = FT * p + f
                        dve.wait_ge(unit_done, u + 2 + 4 * more)
                        dve.wait_ge(acc_free[2 * j], T // 4 + i + 1 + more)
                        dve.tensor_tensor(buf[j][:, :], buf[j][:, :], acc[:, 2 * j + 1, :], ALU.mult)\
                           .then_inc(acc_free[2 * j + 1], 1)
                        dve.wait_ge(g_hi_ready, F + 1 + 2 * more)
                        if isinstance(more, int):
                            lo, hi = g_lo[:, f, :], g_hi[:, f, :]
                        else:
                            lo, hi = (g[:, bass.ds(2 * more + f, 1), :].rearrange("p a s -> p (a s)")
                                      for g in (g_lo, g_hi))
                        dve.tensor_tensor(lo, buf[j][:, :], hi.bitcast(F32), ALU.subtract)\
                           .then_inc(g_lo_ready, 1)
                        if evac and j == 0:
                            ada_evac(ada_first + i - 1, more)
                        if halves:
                            ada_half(ada_first + i, 4 * j, more)

                step(0, 0, ada_steps > 0, False)
                done = 1
                if ada_steps > 1:
                    with dve.Fori(0, ada_steps - 1) as i:
                        step(1, i, True, True)
                    done = ada_steps
                if ada_steps and done < FT // 2:
                    step(done, 0, False, True)
                    done += 1
                    evac_left = False
                else:
                    evac_left = ada_steps > 0
                if done < FT // 2:
                    with dve.Fori(0, FT // 2 - done) as i:
                        step(done, i, False, False)
                if evac_left:
                    ada_evac(ada_first + ada_steps - 1)
                prepare_residual(r, 0.5)
                W = U + N13
                with dve.Fori(0, KT // 2) as i:
                    for j in range(2):
                        dve.wait_ge(unit_done, W + 4 * j + 4 + 8 * i)
                        residual(r, j, outp[:, j, :], out_free[j], 2 * i, 2 * i + j)

            def out_projection(U, r):
                prepare_residual(r, 1.0)
                for o in range(KT):
                    dve.wait_ge(unit_done, U + o + 1)
                    residual(r, o, acc[:, o % 4, :], acc_free[o % 4])

            def v_evac(U, dst):
                for half in range(2):
                    dve.wait_ge(unit_done, U + 4 * half + 4)
                    for tt in range(2, 4):
                        dve.tensor_copy(dst[:, tt, half * 512:half * 512 + 512], acc[:, tt, :])\
                           .then_inc(acc_free[tt], 1)

            def mixer_a():
                U, T = U_A, T_A
                norm(1, 1)
                for t in range(8):
                    dve.wait_ge(unit_done, U + t + 1)
                    if t >= 2:
                        dve.wait_ge(a_qk_ready, t - 1)
                    y, p = buf[t % 2], acc[:, t % 4, :]
                    tap = [colv("conv_w", TAPS * t + j) for j in range(TAPS)]
                    link(dve.tensor_scalar(y[:, :], p, tap[3], colv("conv_b", t), ALU.mult, ALU.add))
                    for back in range(1, TAPS):
                        ins = dve.scalar_tensor_tensor(out=y[:, back:S], in0=p[:, 0:S - back],
                                                       scalar=tap[3 - back], in1=y[:, back:S],
                                                       op0=ALU.mult, op1=ALU.add)
                        if back < TAPS - 1:
                            link(ins)
                    ins.then_inc(acc_free[t % 4], 1)
                dve.wait_ge(unit_done, U + 9)
                dve.wait_ge(small_loaded, 32)
                R = [rows[:, n, :] for n in range(8)]
                dve.tensor_scalar(R[0], aux[0:HEADS, :], gbias[:, 0:1], None, ALU.add).then_inc(dve_step, 1)
                link(dve.tensor_copy(R[1], aux[32:32 + HEADS, :]))
                chain[0] += 1
                dve.wait_ge(dve_step, chain[0])
                link(dve.tensor_scalar(R[2], R[1], gbias[:, 1:2], None, ALU.add))
                dve.tensor_scalar(R[4], R[2], 0.0, None, ALU.min).then_inc(dve_step, 1)
                chain[0] += 1
                dve.scalar_tensor_tensor(out=R[3], in0=R[2], scalar=-1.0, in1=R[2],
                                         op0=ALU.mult, op1=ALU.min).then_inc(f_arg_ready, 1)
                dve.wait_ge(dve_step, chain[0])
                dve.wait_ge(f_log_ready, 1)
                link(dve.tensor_tensor(R[7], R[4], R[6], ALU.subtract))
                link(dve.tensor_tensor_scan(R[1], rows_one[:, :], R[7], 0.0, ALU.mult, ALU.add))
                link(dve.tensor_tensor(R[2], R[0], R[1], ALU.subtract))
                link(dve.tensor_tensor_scan(R[3], R[2], R[2], 0.0, ALU.max, ALU.max))
                link(dve.tensor_scalar(R[4], R[3], -1.0, None, ALU.mult))
                dve.tensor_tensor(R[5], R[1], R[3], ALU.add).then_inc(m_rows_ready, 1)
                v_evac(U + 9, a_v)
                dve.wait_ge(u_turned, 1)
                dve.tensor_copy(u_col[:, :], stat[:, 0:ST * HEADS]).then_inc(u_col_ready, 1)

                def diagonal(h):
                    read_out(dve, T + 24 + h)
                    if h >= 2:
                        dve.wait_ge(decay_ready, h - 1)
                    dve.tensor_tensor(buf[h % 2][:, :].rearrange("p (j k) -> p j k", k=P),
                                      neg_m[:, h, :].rearrange("p (j k) -> p j k", k=P),
                                      mask_st[:, :].unsqueeze(1).broadcast_to([P, ST, P]), ALU.add)\
                       .then_inc(diag_ready, 1)

                def weights(h):
                    dve.wait_ge(decay_ready, h + 1)
                    for j in range(ST):
                        dve.wait_ge(st_done, 4 * h + j + 1)
                        w = a_wt[h % 2][:, WT_OFF[j]:WT_OFF[j] + S - j * P]
                        dve.scalar_tensor_tensor(out=w, in0=acc[:, j, 0:S - j * P], scalar=DK ** -0.5, in1=w,
                                                 op0=ALU.mult, op1=ALU.mult)\
                           .then_inc(acc_free[j], 1)

                def heads_out(h):
                    dve.wait_ge(av_done, h + 1)
                    read_out(dve, T + 28 + h)
                    dve.scalar_tensor_tensor(out=rstd[:, :], in0=aux[:, :], scalar=-1.0, in1=exp_m[:, h, :],
                                             op0=ALU.mult, op1=ALU.max).then_inc(dve_step, 1)
                    chain[0] += 1
                    dve.wait_ge(dve_step, chain[0])
                    dve.tensor_tensor(rstd[:, :], aux[:, :], rstd[:, :], ALU.max).then_inc(den_read, 1)
                    dve.wait_ge(den_read, h + 1)
                    link(dve.reciprocal(sq[:, :], rstd[:, :]))
                    for d in range(2):
                        dve.tensor_tensor(a_h[:, 2 * h + d, :], outp[:, d, :], sq[:, :], ALU.mult)\
                           .then_inc(out_free[d], 1)

                diagonal(0)
                diagonal(1)
                for h in range(HEADS):
                    weights(h)
                    if h + 2 < HEADS:
                        diagonal(h + 2)
                    if h >= 1:
                        heads_out(h - 1)
                heads_out(HEADS - 1)

                def make(t):
                    h = t // 2
                    if t % 2 == 0:
                        read_out(dve, T + 48 + h)
                        link(dve.reciprocal(neg_m[:, h, :], exp_m[:, h, :]))
                    if t >= 2:
                        dve.wait_ge(act_lo_ready, 8 * 2 + t - 1)
                    dve.wait_ge(out_free[t % 2], O_A + 1 + h + 1)
                    link(dve.scalar_tensor_tensor(out=buf[t % 2][:, :], in0=a_h[:, t, :],
                                                  scalar=colv("a_norm_g", t), in1=neg_m[:, h, :],
                                                  op0=ALU.mult, op1=ALU.mult))
                    dve.tensor_tensor(buf[t % 2][:, :], buf[t % 2][:, :], a_o[:, t, :], ALU.mult)\
                       .then_inc(src_ready, 1)
                lows(2, None, make)
                out_projection(U + 25, 1)

            def trig_tables():
                C, Sn, A, B = b_cos[:, :], b_sin[:, :], b_rot[:, :], b_tmp[:, :]
                dve.wait_ge(pos_loaded, 16)
                link(dve.tensor_copy(A, pos_i[:, :]))
                link(dve.tensor_scalar(A, A, rope_row[:, 0:1], None, ALU.mult))
                rounder = 1.5 * 2.0 ** 23
                for step in (2.0 ** 20, 2.0 ** 10, 1.0):
                    link(dve.tensor_scalar(B, A, 1.0 / (step * TWO_PI), rounder, ALU.mult, ALU.add))
                    link(dve.tensor_scalar(B, B, rounder, None, ALU.subtract))
                    for part in two_pi_parts(step):
                        link(dve.scalar_tensor_tensor(out=A, in0=B, scalar=-part, in1=A,
                                                      op0=ALU.mult, op1=ALU.add))
                link(dve.tensor_scalar(A, A, math.pi * (1 - 2.0 ** -22), -math.pi * (1 - 2.0 ** -22),
                                       ALU.min, ALU.max))
                dve.tensor_scalar(Sn, A, rope_row[:, 1:2], None, ALU.mult).then_inc(trig_arg, 1)
                link(dve.scalar_tensor_tensor(out=B, in0=A, scalar=-1.0, in1=A, op0=ALU.mult, op1=ALU.min))
                dve.tensor_scalar(C, B, math.pi / 2, None, ALU.add).then_inc(trig_arg, 1)

            def mixer_b():
                U, T = U_B, T_B
                norm(4, 5)
                trig_tables()
                dve.wait_ge(trig_ready, 2)
                swap = [(n + HALF) % ROPE_DIM for n in range(ROPE_DIM)]
                for t in range(16):
                    read_out(dve, T + t)
                    q = b_qk[0:ROPE_DIM, t, :]
                    link(dve.stream_shuffle(b_rot[:, :], q, swap))
                    dve.tensor_tensor(b_tmp[:, :], q, b_cos[:, :], ALU.mult).then_inc(dve_step, 1)
                    chain[0] += 1
                    link(dve.tensor_tensor(b_rot[:, :], b_rot[:, :], b_sin[:, :], ALU.mult))
                    dve.tensor_tensor(q, b_tmp[:, :], b_rot[:, :], ALU.add).then_inc(rope_done, 1)
                    dve.wait_ge(rope_done, t + 1)
                    if t == 0:
                        dve.tensor_scalar(bg_col[:, :], colv("b_norm_g", 0, 2), 1.0 - LAM_INIT, None, ALU.mult)\
                           .then_inc(dve_step, 1)
                        chain[0] += 1
                v_evac(U + 16, b_v)

                def maxima(n):
                    h, i = divmod(n, ST)
                    b = (T + 24 + 2 * n) % 4
                    dve.wait_ge(s_done, 2 * n + 2)
                    diag = acc[:, b:b + 2, i * P:(i + 1) * P]
                    link(dve.tensor_tensor(diag, diag, mask_ts[:, :].unsqueeze(1).broadcast_to([P, 2, P]), ALU.add))
                    link(dve.tensor_reduce(row_max[:, n % 2, :], acc[:, b:b + 2, 0:(i + 1) * P], AX.X, ALU.max))
                    dve.tensor_scalar(neg_max[:, n % 2, :], row_max[:, n % 2, :], -1.0, None, ALU.mult)\
                       .then_inc(max_ready, 1)

                def combine(n):
                    h, i = divmod(n, ST)
                    N = (i + 1) * P
                    inv, pr = row_inv[:, n % 2, :], b_p[n % 2]
                    for c in range(2):
                        read_out(dve, T + 24 + 2 * n + c)
                    link(dve.reciprocal(inv, row_sum[:, n % 2, :]))
                    link(dve.tensor_tensor(inv[:, 1:2], inv[:, 1:2], neg_lam[:, :], ALU.mult))
                    link(dve.tensor_scalar(pr[:, 1, 0:N], pr[:, 1, 0:N], inv[:, 1:2], None, ALU.mult))
                    dve.scalar_tensor_tensor(out=pr[:, 0, 0:N], in0=pr[:, 0, 0:N], scalar=inv[:, 0:1],
                                             in1=pr[:, 1, 0:N], op0=ALU.mult, op1=ALU.add).then_inc(p_ready, 1)

                def keep(h):
                    dve.wait_ge(pv_done, h + 1)
                    dve.tensor_copy(b_o[:, 2 * h, :], stat[:, :]).then_inc(dve_step, 1)
                    chain[0] += 1
                    dve.wait_ge(dve_step, chain[0])
                    dve.tensor_copy(b_o[:, 2 * h + 1, :], aux[:, :]).then_inc(b_o_ready, 1)

                dve.wait_ge(lam_ready, 1)
                for n in range(4 * HEADS + 3):
                    if n < 4 * HEADS:
                        maxima(n)
                    if 1 <= n <= 4 * HEADS:
                        combine(n - 1)
                    if n >= 6 and (n - 6) % 4 == 0:
                        keep((n - 6) // 4)

                def make(t):
                    h = t // 2
                    if t % 2 == 0:
                        read_out(dve, T + 56 + h)
                        link(dve.reciprocal(b_at1[:, h, :], b_at0[:, h, :]))
                    if t >= 2:
                        dve.wait_ge(act_lo_ready, 8 * 6 + t - 1)
                    dve.scalar_tensor_tensor(out=buf[t % 2][:, :], in0=b_o[:, t, :],
                                             scalar=bg_col[:, t % 2:t % 2 + 1], in1=b_at1[:, h, :],
                                             op0=ALU.mult, op1=ALU.mult).then_inc(src_ready, 1)
                lows(6, None, make)
                out_projection(U + 24, 4)

            for j in range(2):
                dve.memset(outp[:, j, :], 0.0).then_inc(out_free[j], 1)
            link(dve.memset(rows_one[:, :], 1.0))
            dve.wait_ge(col_loaded, 16)
            lam = COLS["lam"]
            dve.tensor_tensor(lam_mul[:, :], col[:, lam:lam + 3:2], col[:, lam + 1:lam + 4:2], ALU.mult)\
               .then_inc(lam_mul_ready, 1)
            dve.wait_ge(lam_exp_ready, 1)
            link(dve.tensor_tensor(neg_lam[:, :], lam_exp[:, 1:2], lam_exp[:, 0:1], ALU.subtract))
            dve.tensor_scalar(neg_lam[:, :], neg_lam[:, :], LAM_INIT, None, ALU.subtract).then_inc(lam_ready, 1)
            dve.wait_ge(cond_ready, 1)
            for sl, sums in enumerate((ada_acc, early_acc)):
                for k in range(KT):
                    n = sl * KT + k
                    if n % 4 == 0:
                        dve.wait_ge(early_loaded[n // 4], 16)
                    if k == 0:
                        ins = dve.tensor_scalar(sums[:, :], early_ada[:, n, :], cond[:, 0:1], None, ALU.mult)
                    else:
                        dve.wait_ge(early_used, n)
                        ins = dve.scalar_tensor_tensor(out=sums[:, :], in0=early_ada[:, n, :],
                                                       scalar=cond[:, k:k + 1], in1=sums[:, :],
                                                       op0=ALU.mult, op1=ALU.add)
                    ins.then_inc(early_used, 1)
            ada_evac(0)
            ada_evac(1)
            ffn(0, EARLY, ADA_F0)
            mixer_a()
            ffn(1, EARLY + ADA_F0, ADA_F1)
            ffn(2, 0, 0)
            mixer_b()
            ffn(3, 0, 0)
            dve.wait_ge(std_ready, 7)
            dve.reciprocal(rstd[:, :], sq[:, :]).then_inc(rstd_ready, 1)
            dve.wait_ge(rstd_ready, 7)
            for k in range(KT):
                dve.scalar_tensor_tensor(out=x[:, k, :], in0=x[:, k, :], scalar=colv("final_g", k),
                                         in1=rstd[:, :], op0=ALU.mult, op1=ALU.mult).then_inc(src_ready, 1)


def tiles(w):
    n = w.shape[1] // P
    return w.reshape(KT, P, n, P).transpose(2, 1, 0, 3).reshape(n, P, KT * P)


def v_units(w):
    return w.reshape(4, 2, P, 2, 512).transpose(3, 0, 2, 1, 4).reshape(8, P, 1024)


def columns(v):
    return v.reshape(-1, P).T


def kernel(**inputs):
    import concourse.bacc as bacc
    from concourse.bass_utils import run_bass_kernel_spmd

    a = {k: np.asarray(v) for k, v in inputs.items()}
    gates = np.zeros((D, P), np.float32)
    w_in = a["a_w_in"][0]
    gates[:, 0:HEADS] = w_in[:, 3072:3072 + HEADS]
    gates[:, 32:32 + HEADS] = w_in[:, 3072 + HEADS:3080]
    wb_in = a["b_w_in"][0]
    cols = np.concatenate([
        columns(a["c"][0]), columns(a["ada_b"]), columns(a["norm_g"]), columns(a["final_g"]),
        a["a_conv_w"][0].reshape(TAPS, 8, P).transpose(2, 1, 0).reshape(P, 32),
        columns(a["a_conv_b"][0]), columns(a["a_norm_g"][0]), columns(a["b_norm_g"][0]),
        a["b_lam"][0].T], axis=1)
    inv_freq = (ROPE_THETA ** (-np.arange(0, ROPE_DIM, 2, dtype=np.float64) / ROPE_DIM)).astype(np.float32)
    rope_rows = np.stack([np.concatenate([inv_freq, inv_freq]),
                          np.repeat(np.array([-1.0, 1.0], np.float32), HALF)], axis=1)
    arrays = {
        "xT": a["x"][0].T.reshape(KT, P, S).transpose(1, 0, 2),
        "cols": cols,
        "gate_bias": a["a_b_if"][0].reshape(2, HEADS).T,
        "rope_rows": rope_rows,
        "positions": a["positions"],
        "ada": a["ada_w"].reshape(LAYERS, KT, P, 9, D).transpose(0, 3, 1, 2, 4).reshape(SLICES * KT, P, D),
        "w13": a["ffn_w13"].reshape(4, KT, P, 2, FT, P).transpose(0, 4, 3, 2, 1, 5).reshape(4 * N13, P, D),
        "w2": a["ffn_w2"].reshape(4, FT, P, KT, P).transpose(0, 3, 2, 1, 4).reshape(4 * KT, P, FF),
        "wa": np.concatenate([tiles(w_in[:, 0:1024]), tiles(gates), v_units(w_in[:, 1024:2048]),
                              tiles(w_in[:, 2048:3072]), tiles(a["a_w_out"][0])]),
        "wb": np.concatenate([tiles(wb_in[:, 0:2048]), v_units(wb_in[:, 2048:3072]),
                              tiles(a["b_w_out"][0])]),
    }
    nc = bacc.Bacc("TRN2", target_bir_lowering=False, num_devices=1)
    arrays = {k: np.ascontiguousarray(v) for k, v in arrays.items()}
    aps = [nc.dram_tensor(k, v.shape, mybir.dt.from_np(v.dtype), kind="ExternalInput").ap()
           for k, v in arrays.items()]
    out = nc.dram_tensor("out", (KT, P, S), F32, kind="ExternalOutput").ap()
    build_trunk(nc, *aps, out)
    r = run_bass_kernel_spmd(nc, [arrays], core_ids=[0])
    return r.results[0]["out"].reshape(D, S).T.reshape(1, S, D)
```

```python
import math
from contextlib import ExitStack

import numpy as np
import concourse.bass as bass
from concourse import mybir

F32 = mybir.dt.float32
F32R = mybir.dt.float32r
I32 = mybir.dt.int32
ALU = mybir.AluOpType
ACT = mybir.ActivationFunctionType
AX = mybir.AxisListType

P = 128
D = 1024
S = 512
FF = 2816
KT = D // P
FT = FF // P
ST = S // P
HEADS = 4
DK = 128
DV = 256
TAPS = 4
EPS = 1e-6
LAYERS = 2
SUBS = 3 * LAYERS
ROPE_DIM = DK // 4
HALF = ROPE_DIM // 2
ROPE_THETA = 500000.0
LAM_INIT = 0.8 - 0.6 * math.exp(-0.3 * 1)
MASKED = -1e30

SLOTS = 4
RAWS = 2
W2_SPLIT = (6, 6, 5, 5)
W2_START = (0, 6, 12, 17)

N13 = 2 * FT
NW2 = 4 * KT
UNITS_FFN = N13 + NW2
UNITS_A = 8 + 1 + 8 + 8 + 8
UNITS_B = 16 + 8 + 8
U_F0 = 0
U_A = U_F0 + UNITS_FFN
U_F1 = U_A + UNITS_A
U_F2 = U_F1 + UNITS_FFN
U_B = U_F2 + UNITS_FFN
U_F3 = U_B + UNITS_B
U_END = U_F3 + UNITS_FFN
U_FFN = (U_F0, U_F1, U_F2, U_F3)




def more_uses(before, *uses):
    return tuple(b + u for b, u in zip(before, uses))


T_F0 = (0, 0, 0, 0)
T_A = more_uses(T_F0, *[N13 // 4] * 4)
T_A_OUT = more_uses(T_A, 10, 10, 10, 10)
T_F1 = more_uses(T_A_OUT, 3, 3, 3, 3)
T_F2 = more_uses(T_F1, *[N13 // 4] * 4)
T_B = more_uses(T_F2, *[N13 // 4] * 4)
T_B_OUT = more_uses(T_B, 10, 10, 18, 18)
T_F3 = more_uses(T_B_OUT, 3, 3, 3, 3)
T_FFN = (T_F0, T_F1, T_F2, T_F3)
O_FFN = ((0, 0), (9, 8), (14, 12), (27, 24))
O_A = (5, 4)
O_B = (19, 16)
N_FFN = (0, 2, 3, 5)
SQUARES = (KT + 1, KT + 4, KT + 1, KT + 1, KT + 4, KT + 1)
SQ_BASE = tuple(sum(SQUARES[:r]) for r in range(SUBS))
ADD_BASE = tuple(SQ_BASE[r] + r for r in range(SUBS))
Q_IN = (0, 16, 40, 56, 72, 96, 112)
HALVES = tuple(SQ_BASE[r] - KT * r for r in range(SUBS))
Q_A_OUT = 32
Q_B_OUT = 88
QK_TILE = tuple(8 * (r % 4 // 2) + 2 * (r // 4) + r % 2 for r in range(16))
H2 = S // 2

SLICES = 9 * LAYERS
EARLY = 2
ADA_F0 = 8
ADA_F1 = SLICES - EARLY - ADA_F0

COLS = {}
_n = 0
for _name, _w in (("c", KT), ("ada_b", SLICES * KT), ("norm_g", SUBS * KT), ("final_g", KT),
                  ("conv_w", TAPS * 8), ("conv_b", 8), ("a_norm_g", 8), ("b_norm_g", 2), ("lam", 4)):
    COLS[_name] = _n
    _n += _w
N_COLS = _n

TWO_PI = 2.0 * math.pi


def two_pi_parts(step):
    rest, parts = step * TWO_PI, []
    for _ in range(4):
        scale = 2.0 ** (10 - math.floor(math.log2(rest)))
        part = math.floor(rest * scale) / scale
        parts.append(part)
        rest -= part
    return parts


def build_trunk(nc, xT, cols, gate_bias, rope_rows, positions, ada, w13, w2, wa, wb, out):
    ctx = ExitStack()
    with ctx:
        def sem(name):
            return ctx.enter_context(nc.semaphore(name))

        top = [(nc.sbuf_base + 63) // 64 * 64]

        def at(name, shape, dt, offset):
            return nc.alloc_sbuf_tensor_at(name, shape, dt, offset=offset)

        def place(name, shape, dt=F32):
            offset = top[0]
            top[0] += (int(np.prod(shape[1:])) * 4 + 31) // 32 * 32
            return at(name, shape, dt, offset)

        x = place("x", [P, KT, S])
        h_hi = place("h_hi", [P, KT, S], F32R)
        h_lo = place("h_lo", [P, KT, S], F32R)
        raw = [place(f"raw{i}", [P, 1024]) for i in range(RAWS)]
        w_hi = [place(f"w_hi{i}", [P, 1024], F32R) for i in range(SLOTS)]
        w_lo = [place(f"w_lo{i}", [P, 1024], F32R) for i in range(SLOTS)]
        buf = [place(f"buf{i}", [P, S]) for i in range(2)]
        sq = place("sq", [P, S])
        sumsq = place("sumsq", [P, S])
        rstd = place("rstd", [P, S])
        ada_region = top[0]
        ada_raw = [place(f"ada_raw{i}", [P, 1024]) for i in range(2)]
        ada_acc = place("ada_acc", [P, 1024])
        region = top[0]
        g_hi = place("g_hi", [P, FT, S], F32R)
        g_lo = place("g_lo", [P, FT, S], F32R)
        region_end = top[0]
        col = place("col", [P, N_COLS])
        ada_v = place("ada_v", [P, SLICES, KT])
        cond = place("cond", [P, KT])
        scale_col = place("scale_col", [P, KT])
        gate_col = place("gate_col", [P, KT])
        ones = place("ones", [P, P])
        ident = place("ident", [P, P])
        mask_st = place("mask_st", [P, P])
        mask_ts = place("mask_ts", [P, P])
        select = place("select", [HEADS, HEADS, P])
        eps = place("eps", [P, 1])
        std_col = place("std_col", [P, ST])
        inv_col = place("inv_col", [P, ST])
        head_std = place("head_std", [P, HEADS * ST])
        head_inv = place("head_inv", [P, HEADS * ST])
        ag_col = place("ag_col", [P, 8])
        rows_one = place("rows_one", [HEADS, S])
        gbias = place("gbias", [HEADS, 2])
        rope_row = place("rope_row", [ROPE_DIM, 2])
        lam_mul = place("lam_mul", [P, 2])
        lam_exp = place("lam_exp", [P, 2])
        neg_lam = place("neg_lam", [P, 1])
        u_col = place("u_col", [P, ST * HEADS])
        neg_max = place("neg_max", [P, 2, 2])
        row_max = place("row_max", [P, 2, 2])
        row_sum = place("row_sum", [P, 2, 2])
        row_inv = place("row_inv", [P, 2, 2])
        bg_col = place("bg_col", [P, 2])
        assert top[0] <= nc.sbuf_usable_end, (top[0], nc.sbuf_usable_end)

        def carve(parts, start, end):
            made = []
            for name, shape in parts:
                made.append(at(name, shape, F32, start))
                start += int(np.prod(shape[1:])) * 4
            assert start <= end, (parts, start - end)
            return made

        early_ada, x_sq, early_acc = carve(
            [("early_ada", [P, EARLY * KT, 1024]), ("x_sq", [P, KT, S]), ("early_acc", [P, 1024])],
            region, region_end)
        a_qk, a_v, a_o, a_h, neg_m, exp_m = carve(
            [("a_qk", [P, 8, S]), ("a_v", [P, ST, 1024]), ("a_o", [P, 8, S]), ("a_h", [P, 8, S]),
             ("neg_m", [P, HEADS, S]), ("exp_m", [P, HEADS, S])], region, region_end)
        rows = at("rows", [HEADS, 8, S], F32, region + 3 * 16384)
        WT_OFF = (0, 512, 896, 1152)
        a_wt = carve([("a_wt0", [P, 1280]), ("a_wt1", [P, 1280])], ada_region, region)
        b_qk, b_v, b_o, b_at0, b_at1, b_cos, b_sin, b_rot, b_tmp = carve(
            [("b_qk", [P, 16, S]), ("b_v", [P, ST, 1024]), ("b_o", [P, 8, S]),
             ("b_at0", [P, ST, S]), ("b_at1", [P, ST, S]),
             ("b_cos", [ROPE_DIM, S]), ("b_sin", [ROPE_DIM, S]), ("b_rot", [ROPE_DIM, S]),
             ("b_tmp", [ROPE_DIM, S])], region, region_end)
        b_at = (b_at0, b_at1)
        b_p = carve([("b_p0", [P, 2, S]), ("b_p1", [P, 2, S])], ada_region, region)
        pos_i = at("pos_i", [ROPE_DIM, S], I32, ada_region + 8192)

        acc = ctx.enter_context(nc.psum_tensor("acc", [P, 4, S], F32))
        outp = ctx.enter_context(nc.psum_tensor("outp", [P, 2, S], F32))
        stat = ctx.enter_context(nc.psum_tensor("stat", [P, S], F32))
        aux = ctx.enter_context(nc.psum_tensor("aux", [P, S], F32))

        raw_loaded = [sem(f"raw_loaded{i}") for i in range(RAWS)]
        hi_ready = sem("hi_ready")
        lo_ready = sem("lo_ready")
        unit_done = sem("unit_done")
        half_done = sem("half_done")
        acc_free = [sem(f"acc_free{i}") for i in range(4)]
        out_free = [sem(f"out_free{i}") for i in range(2)]
        sq_done = sem("sq_done")
        sq_added = sem("sq_added")
        stat_done = sem("stat_done")
        std_ready = sem("std_ready")
        rstd_ready = sem("rstd_ready")
        rstd_spread = sem("rstd_spread")
        scale_ready = sem("scale_ready")
        gate_ready = sem("gate_ready")
        src_ready = sem("src_ready")
        act_hi_ready = sem("act_hi_ready")
        act_lo_ready = sem("act_lo_ready")
        g_hi_ready = sem("g_hi_ready")
        g_lo_ready = sem("g_lo_ready")
        early_loaded = [sem(f"early_loaded{i}") for i in range(4)]
        ada_loaded = [sem(f"ada_loaded{i}") for i in range(2)]
        ada_used = sem("ada_used")
        early_used = sem("early_used")
        colsum_done = sem("colsum_done")
        ada_ready = sem("ada_ready")
        col_loaded = sem("col_loaded")
        small_loaded = sem("small_loaded")
        pos_loaded = sem("pos_loaded")
        x_loaded = sem("x_loaded")
        cond_ready = sem("cond_ready")
        pool_consts = sem("pool_consts")
        dve_consts = sem("dve_consts")
        lam_mul_ready = sem("lam_mul_ready")
        lam_sum_done = sem("lam_sum_done")
        lam_exp_ready = sem("lam_exp_ready")
        lam_ready = sem("lam_ready")
        a_qk_ready = sem("a_qk_ready")
        f_arg_ready = sem("f_arg_ready")
        f_log_ready = sem("f_log_ready")
        m_rows_ready = sem("m_rows_ready")
        em_row_ready = sem("em_row_ready")
        u_turned = sem("u_turned")
        u_col_ready = sem("u_col_ready")
        spread_done = sem("spread_done")
        diag_ready = sem("diag_ready")
        decay_ready = sem("decay_ready")
        st_done = sem("st_done")
        av_done = sem("av_done")
        den_read = sem("den_read")
        a_o_ready = sem("a_o_ready")
        gated_ready = sem("gated_ready")
        a_sq_ready = sem("a_sq_ready")
        a_ss_done = sem("a_ss_done")
        a_std_ready = sem("a_std_ready")
        a_inv_ready = sem("a_inv_ready")
        a_inv_spread = sem("a_inv_spread")
        a_factor_ready = sem("a_factor_ready")
        trig_arg = sem("trig_arg")
        trig_ready = sem("trig_ready")
        rope_done = sem("rope_done")
        s_done = sem("s_done")
        max_ready = sem("max_ready")
        p_ready = sem("p_ready")
        turned = sem("turned")
        pv_done = sem("pv_done")
        b_o_ready = sem("b_o_ready")
        v_part_done = sem("v_part_done")
        b_sq_ready = sem("b_sq_ready")
        b_ss_done = sem("b_ss_done")
        b_std_ready = sem("b_std_ready")
        b_inv_ready = sem("b_inv_ready")
        b_inv_spread = sem("b_inv_spread")
        b_factor_ready = sem("b_factor_ready")
        stored = sem("stored")
        dve_step = sem("dve_step")
        act_step = sem("act_step")
        pool_step = sem("pool_step")

        def read_out(eng, T, n):
            eng.wait_ge(acc_free[n % 4], T[n % 4] + n // 4 + 1)

        def tok(half):
            return slice(half * H2, (half + 1) * H2)

        def head_bank(h, d):
            return outp[:, d, :] if h == HEADS - 1 else (stat, aux)[d][:, :]

        def rstd_bank(half):
            return aux[:, 0:H2] if half == 0 else stat[:, H2:S]

        block = ctx.enter_context(nc.Block())

        @block.sync
        def _(sp):
            def load_unit(u, src, n=1024, wait=None):
                base, more = u
                if wait is not False:
                    sp.wait_ge(lo_ready, base + more - RAWS + 1)
                sp.dma_start(raw[base % RAWS][:, 0:n], src).then_inc(raw_loaded[base % RAWS], 16)

            def load_ada(sl, first, more=0):
                for k in range(first, first + 4):
                    a = (sl - EARLY) * KT + k
                    if a >= 2:
                        sp.wait_ge(ada_used, a + more * KT - 1)
                    sp.dma_start(ada_raw[k % 2][:, :], ada[EARLY * KT + a + more * KT])\
                      .then_inc(ada_loaded[k % 2], 16)

            def ffn(p, ada_first, ada_steps):
                U = U_FFN[p]
                last = FT // 2 - 1

                def load13(n, more=0):
                    load_unit((U + n, 4 * more), w13[p * N13 + n + 4 * more],
                              wait=None if U + n >= RAWS else False)

                def load2(o, m, more=0):
                    n, k0 = W2_SPLIT[m] * P, W2_START[m] * P
                    load_unit((U + N13 + 4 * o + m, 4 * more), w2[p * KT + o + more][:, k0:k0 + n], n)

                def step(i, more, with_ada):
                    for j in range(2):
                        load13(4 * i + 4 + 2 * j, more)
                        load13(4 * i + 5 + 2 * j, more)
                        if with_ada:
                            load_ada(ada_first + i, 4 * j, more)

                for n in range(4):
                    load13(n)
                if ada_steps:
                    step(0, 0, True)
                    with sp.Fori(0, min(ada_steps, last) - 1) as i:
                        step(1, i, True)
                done = min(ada_steps, last)
                if done < last:
                    with sp.Fori(0, last - done) as i:
                        step(done, i, False)
                for j in range(2):
                    load2(0, 2 * j)
                    load2(0, 2 * j + 1)
                    if ada_steps > last:
                        load_ada(ada_first + last, 4 * j)
                with sp.Fori(0, KT - 1) as o:
                    for m in range(4):
                        load2(1, m, o)

            for c in range(4):
                sp.dma_start(early_ada[:, 4 * c:4 * c + 4, :],
                             ada[4 * c:4 * c + 4].rearrange("u p n -> p u n")).then_inc(early_loaded[c], 16)
            ffn(0, EARLY, ADA_F0)
            with sp.Fori(0, (UNITS_A - 1) // 4) as i:
                for k in range(4):
                    load_unit((U_A + k, 4 * i), wa[4 * i + k])
            load_unit((U_A + UNITS_A - 1, 0), wa[UNITS_A - 1])
            ffn(1, EARLY + ADA_F0, ADA_F1)
            ffn(2, 0, 0)
            sp.wait_ge(ada_ready, SLICES)
            sp.dma_start(pos_i[:, :], positions.broadcast_to([ROPE_DIM, S])).then_inc(pos_loaded, 16)
            with sp.Fori(0, UNITS_B // 4) as i:
                for k in range(4):
                    load_unit((U_B + k, 4 * i), wb[4 * i + k])
            ffn(3, 0, 0)
            for half in range(2):
                for k in (0, 4):
                    sp.wait_ge(src_ready, Q_IN[SUBS] + 8 * half + k + 4)
                    sp.dma_start(out[k:k + 4, :, tok(half)].rearrange("k p s -> p k s"),
                                 x[:, k:k + 4, tok(half)]).then_inc(stored, 16)
            sp.wait_ge(stored, 16 * 4)

        @block.gpsimd
        def _(pool):
            pool.memset(ident[:, :], 0.0).then_inc(pool_step, 1)
            pool.memset(mask_st[:, :], 0.0).then_inc(pool_step, 1)
            pool.memset(mask_ts[:, :], 0.0).then_inc(pool_step, 1)
            pool.memset(select[:, :, :], 0.0).then_inc(pool_step, 1)
            pool.memset(ones[:, :], 1.0).then_inc(pool_consts, 1)
            pool.memset(eps[:, :], EPS).then_inc(pool_consts, 1)
            pool.wait_ge(pool_step, 4)
            pool.affine_select(out=ident[:, :], in_=ident[:, :], compare_op=ALU.not_equal, fill=1.0,
                               base=0, pattern=[[-1, P]], channel_multiplier=1).then_inc(pool_consts, 1)
            pool.affine_select(out=mask_st[:, :], in_=mask_st[:, :], compare_op=ALU.is_ge, fill=MASKED,
                               base=0, pattern=[[1, P]], channel_multiplier=-1).then_inc(pool_consts, 1)
            pool.affine_select(out=mask_ts[:, :], in_=mask_ts[:, :], compare_op=ALU.is_ge, fill=MASKED,
                               base=0, pattern=[[-1, P]], channel_multiplier=1).then_inc(pool_consts, 1)
            pool.affine_select(out=select[:, :, :], in_=select[:, :, :], compare_op=ALU.not_equal, fill=1.0,
                               base=0, pattern=[[-1, HEADS], [0, P]], channel_multiplier=1)\
                .then_inc(pool_consts, 1)

            def low_part(base, more, n=1024):
                pool.wait_ge(hi_ready, base + more + 1)
                s = base % SLOTS
                pool.tensor_tensor(w_lo[s][:, 0:n], raw[base % RAWS][:, 0:n],
                                   w_hi[s][:, 0:n].bitcast(F32), ALU.subtract).then_inc(lo_ready, 1)

            def group_loop(U, n):
                with pool.Fori(0, n) as i:
                    for k in range(4):
                        low_part(U + k, 4 * i)

            def ffn(p):
                group_loop(U_FFN[p], N13 // 4)
                with pool.Fori(0, KT) as o:
                    for m in range(4):
                        low_part(U_FFN[p] + N13 + m, 4 * o, W2_SPLIT[m] * P)

            ffn(0)
            group_loop(U_A, (UNITS_A - 1) // 4)
            low_part(U_A + UNITS_A - 1, 0)
            ffn(1)
            ffn(2)
            group_loop(U_B, UNITS_B // 4)
            ffn(3)

        @block.tensor
        def _(pe):
            def three(bank, a_hi, a_lo, b_hi, b_lo, start, stop):
                pe.matmul(bank, a_hi, b_hi, start=start, stop=False)
                pe.matmul(bank, a_hi, b_lo, start=False, stop=False)
                return pe.matmul(bank, a_lo, b_hi, start=False, stop=stop)

            def block_of(s, n):
                return w_hi[s][:, n * P:(n + 1) * P], w_lo[s][:, n * P:(n + 1) * P]

            def take_acc(T, n):
                if T[n % 4] + n // 4:
                    pe.wait_ge(acc_free[n % 4], T[n % 4] + n // 4)

            def unit(base, more, bank):
                pe.wait_ge(lo_ready, base + more + 1)
                for k in range(KT):
                    last = three(bank, *block_of(base % SLOTS, k), h_hi[:, k, :], h_lo[:, k, :],
                                 k == 0, k == KT - 1)
                last.then_inc(unit_done, 1)

            def first_group(U, T, n):
                for half in range(2):
                    t = tok(half)
                    for pair in range(2):
                        for k in range(KT):
                            if pair == 0:
                                pe.wait_ge(act_lo_ready, Q_IN[n] + 8 * half + k + 1)
                            for s in (2 * pair, 2 * pair + 1):
                                if half == 0 and k == 0:
                                    pe.wait_ge(lo_ready, U + s + 1)
                                    take_acc(T, s)
                                last = three(acc[:, s, t], *block_of((U + s) % SLOTS, k),
                                             h_hi[:, k, t], h_lo[:, k, t], k == 0, k == KT - 1)
                                if half == 1 and k == KT - 1:
                                    last.then_inc(unit_done, 1)
                            if half == 0 and pair == 1 and k == KT // 2 - 1:
                                spread_rstd(n, 1)
                        if half == 0 and pair == 0 and n:
                            norm_sum(n, 1)

            def out_first_group(U, T, q, before):
                for s, k in [(s, k) for k in range(KT - 2) for s in range(4)] + \
                            [(s, k) for s in range(4) for k in range(KT - 2, KT)]:
                    if s == 0:
                        if k in before:
                            before[k]()
                        pe.wait_ge(act_lo_ready, q + k + 1)
                    if k == 0:
                        pe.wait_ge(lo_ready, U + s + 1)
                        take_acc(T, s)
                    last = three(acc[:, s, :], *block_of((U + s) % SLOTS, k),
                                 h_hi[:, k, :], h_lo[:, k, :], k == 0, k == KT - 1)
                    if k == KT - 1:
                        last.then_inc(unit_done, 1)

            def v_half(U, T, first):
                for m in range(4):
                    u = U + m
                    s = u % SLOTS
                    pe.wait_ge(lo_ready, u + 1)
                    for tt in range(ST):
                        if m == 0:
                            take_acc(T, first + tt)
                        for k in (2 * m, 2 * m + 1):
                            last = v_product(acc[:, tt, :], tt, k, s)
                    last.then_inc(unit_done, 1)

            def v_product(bank, tt, k, s):
                t, n = slice(tt * P, tt * P + P), k % 2 * 512
                return three(bank, h_hi[:, k, t], h_lo[:, k, t], w_hi[s][:, n:n + 512],
                             w_lo[s][:, n:n + 512], k == 0, k == KT - 1)

            def colsum(sums, n):
                for t in range(KT):
                    last = pe.matmul(aux[:, t:t + 1], sums[:, t * P:(t + 1) * P], ones[:, 0:1],
                                     start=True, stop=True)
                last.then_inc(colsum_done, 1)

            def norm_sum(n, half):
                r = n - 1
                if r >= 0:
                    pe.wait_ge(sq_added, ADD_BASE[r] + 1 + (KT if half == 0 else SQUARES[r]))
                for j in (2 * half, 2 * half + 1):
                    t = slice(j * P, (j + 1) * P)
                    if r >= 0:
                        last = pe.matmul(stat[:, j:j + 1], sumsq[:, t], ones[:, 0:1], start=True, stop=True)
                        continue
                    for k in range(KT):
                        pe.wait_ge(sq_done, k + 1)
                        last = pe.matmul(stat[:, j:j + 1], x_sq[:, k, t], ones[:, 0:1],
                                         start=k == 0, stop=k == KT - 1)
                last.then_inc(stat_done, 1)

            def spread_rstd(n, half):
                pe.wait_ge(rstd_ready, 2 * n + half + 1)
                pe.matmul(rstd_bank(half), ones[:, :], rstd[:, tok(half)], start=True, stop=True)\
                  .then_inc(rstd_spread, 1)

            def ffn(p, ada_first, ada_steps):
                U, T, W = U_FFN[p], T_FFN[p], U_FFN[p] + N13
                first_group(U, T, N_FFN[p])

                def step(i, more, with_ada):
                    for k in range(4):
                        pe.wait_ge(acc_free[k], T[k] + i + more)
                        unit(U + 4 * i + k, 4 * more, acc[:, k, :])
                        if k == 1 and with_ada:
                            pe.wait_ge(ada_used, 8 * (ada_first - EARLY + i + more))
                            pe.wait_ge(ada_ready, ada_first + i - 1 + more)
                            colsum(ada_acc, 0)

                if ada_steps:
                    n = min(ada_steps, FT // 2 - 1)
                    with pe.Fori(0, n) as i:
                        step(1, i, True)
                    if n + 1 < FT // 2:
                        with pe.Fori(0, FT // 2 - 1 - n) as i:
                            step(n + 1, i, False)
                    if n < ada_steps:
                        pe.wait_ge(ada_used, 8 * (ada_first - EARLY + ada_steps))
                        pe.wait_ge(ada_ready, ada_first + ada_steps - 1)
                        colsum(ada_acc, 0)
                else:
                    with pe.Fori(0, FT // 2 - 1) as i:
                        step(1, i, False)

                def out_tile(j, bank, t, use, more=0, hold=False, between=lambda m: None):
                    pe.wait_ge(out_free[bank], O_FFN[p][bank] + 1 + use + more)
                    for m in range(4):
                        base = W + 4 * j + m
                        pe.wait_ge(lo_ready, base + 1 + 8 * more)
                        pe.wait_ge(g_lo_ready, FT * p + W2_START[m] + W2_SPLIT[m])
                        for b in range(W2_SPLIT[m]):
                            kt = W2_START[m] + b
                            last = three(outp[:, bank, t], *block_of(base % SLOTS, b),
                                         g_hi[:, kt, t], g_lo[:, kt, t], kt == 0, kt == FT - 1)
                        if not hold:
                            last.then_inc(unit_done, 1)
                        elif m == 3:
                            last.then_inc(half_done, 1)
                        between(m)

                whole = slice(0, S)
                with pe.Fori(0, KT // 2 - 1) as i:
                    out_tile(0, 0, whole, 0, i)
                    out_tile(1, 1, whole, 0, i)
                out_tile(KT - 2, 0, whole, KT // 2 - 1)
                out_tile(KT - 1, 1, tok(0), KT // 2 - 1, hold=True)
                n = N_FFN[p] + 1

                def norm_first_half(m):
                    if m == 0:
                        norm_sum(n, 0)
                    if m == 1:
                        spread_rstd(n, 0)
                out_tile(KT - 1, 0, tok(1), KT // 2, between=norm_first_half)
                if p == 3:
                    norm_sum(n, 1)
                    spread_rstd(n, 1)

            def out_projection(U, T, q, n, before):
                out_first_group(U, T, q, before)
                for half in range(2):
                    t = tok(half)
                    for s in range(4, 8):
                        take_acc(T, s + 4 * half)
                        pe.wait_ge(lo_ready, U + s + 1)
                        for k in range(KT):
                            last = three(acc[:, s % 4, t], *block_of((U + s) % SLOTS, k),
                                         h_hi[:, k, t], h_lo[:, k, t], k == 0, k == KT - 1)
                        last.then_inc(unit_done if half else half_done, 1)
                        if half and s == 4:
                            norm_sum(n, 0)
                        if half and s == 5:
                            spread_rstd(n, 0)

            def mixer_a():
                U, T = U_A, T_A
                first_group(U, T, 1)
                for s in range(4, 8):
                    take_acc(T, s)
                    unit(U + s, 0, acc[:, s % 4, :])
                pe.wait_ge(ada_ready, EARLY + ADA_F0)
                unit(U + 8, 0, aux[:, :])
                v_half(U + 9, T, 8)
                v_half(U + 13, T, 12)

                def o_tile(t):
                    if t == 0:
                        pe.wait_ge(u_col_ready, 1)
                    else:
                        pe.wait_ge(a_o_ready, t)
                    unit(U + 17 + t, 0, stat[:, :])

                def spread_row(row, first):
                    for h in range(HEADS):
                        take_acc(T, first + h)
                        pe.matmul(acc[:, h, :], select[:, h, :], rows[:, row, :], start=True, stop=True)\
                          .then_inc(spread_done, 1)

                def scores(h):
                    for j in range(ST):
                        take_acc(T, 24 + 4 * h + j)
                        pe.matmul(acc[:, j, 0:S - j * P], a_qk[:, 4 + h, j * P:(j + 1) * P],
                                  a_qk[:, h, j * P:S], start=True, stop=True).then_inc(st_done, 1)

                def mix(h):
                    pe.wait_ge(out_free[0], O_A[0] + h + 1)
                    pe.wait_ge(out_free[1], O_A[1] + h + 1)
                    if h:
                        pe.wait_ge(den_read, h)
                    for j in range(ST):
                        read_out(pe, T, 24 + 4 * h + j)
                        w = a_wt[h % 2][:, WT_OFF[j]:WT_OFF[j] + S - j * P]
                        pe.matmul(aux[:, j * P:S], ones[:, :], w, start=j == 0, stop=j == ST - 1)
                        for d in range(2):
                            c0 = h * DV + d * P
                            last = pe.matmul(outp[:, d, j * P:S], a_v[:, j, c0:c0 + P], w,
                                             start=j == 0, stop=j == ST - 1)
                    last.then_inc(av_done, 1)

                def head_sum(h, bank):
                    pe.wait_ge(a_sq_ready, h + 1)
                    for j in range(ST):
                        for d in range(2):
                            last = pe.matmul(bank[:, ST * h + j:ST * h + j + 1],
                                             a_qk[:, 4 * d + h, j * P:(j + 1) * P], ones[:, 0:1],
                                             start=d == 0, stop=d == 1)
                    last.then_inc(a_ss_done, 1)

                def spread_inverse(h, bank):
                    pe.wait_ge(a_inv_ready, h + 1)
                    pe.matmul(bank, ones[:, :], neg_m[:, h, :], start=True, stop=True)\
                      .then_inc(a_inv_spread, 1)

                pe.wait_ge(m_rows_ready, 1)
                for j in range(ST):
                    last = pe.transpose(stat[:, 4 * j:4 * j + 4], rows[:, 2, j * P:(j + 1) * P],
                                        ident[0:HEADS, 0:HEADS])
                last.then_inc(u_turned, 1)
                spread_row(4, 16)
                o_tile(0)
                pe.wait_ge(em_row_ready, 1)
                spread_row(6, 20)
                pe.wait_ge(a_qk_ready, 8)
                scores(0)
                o_tile(1)
                scores(1)
                mix(0)
                o_tile(2)
                scores(2)
                o_tile(3)
                mix(1)
                o_tile(4)
                scores(3)
                o_tile(5)
                mix(2)
                o_tile(6)
                take_acc(T, 40 + 2)
                head_sum(0, acc[:, 2, :])
                head_sum(1, acc[:, 2, :])
                o_tile(7)
                for h in range(2):
                    take_acc(T, 40 + h)
                    spread_inverse(h, acc[:, h, :])
                pe.wait_ge(a_std_ready, 2)
                head_sum(2, acc[:, 2, :])
                mix(3)
                take_acc(T, 40 + 3)
                spread_inverse(2, acc[:, 3, :])
                pe.wait_ge(a_factor_ready, 3)
                pe.wait_ge(a_std_ready, 3)
                out_projection(U + 25, T_A_OUT, Q_A_OUT, 2,
                               {3: lambda: head_sum(3, aux), 5: lambda: spread_inverse(3, aux[:, :])})

            def mixer_b():
                U, T = U_B, T_B
                first_group(U, T, 4)
                v_half(U + 4, T, 4)

                def chunk(c):
                    bank = acc[:, c % 2, :]
                    take_acc(T, 4 * (2 + c // 2) + c % 2)
                    if c < 12:
                        unit(U + 8 + c, 0, bank)
                        return
                    for k in range(KT):
                        u = U + 20 + k // 2
                        pe.wait_ge(lo_ready, u + 1)
                        last = v_product(bank, c - 12, k, u % SLOTS)
                        if c == 15 and k % 2:
                            last.then_inc(unit_done, 1)
                    if c < 15:
                        last.then_inc(v_part_done, 1)

                def scores(n):
                    h, i = divmod(n, ST)
                    if i == 0:
                        pe.wait_ge(rope_done, 4 * h + 4)
                    for c in range(2):
                        take_acc(T, 4 * (2 + n) + 2 + c)
                        pe.matmul(acc[:, 2 + c, 0:(i + 1) * P], b_qk[:, 2 * h + c, i * P:(i + 1) * P],
                                  b_qk[:, 8 + 2 * h + c, 0:(i + 1) * P], start=True, stop=True)\
                          .then_inc(s_done, 1)

                def turn(n):
                    h, i = divmod(n, ST)
                    pe.wait_ge(p_ready, n + 1)
                    pe.wait_ge(out_free[n % 2], O_B[n % 2] + n // 2 + 1)
                    for j in range(i + 1):
                        last = pe.transpose(outp[:, n % 2, j * P:(j + 1) * P],
                                            b_p[n % 2][:, 0, j * P:(j + 1) * P], ident[:, :])
                    last.then_inc(turned, 1)

                def mix(h):
                    for j in range(2):
                        pe.wait_ge(out_free[j], O_B[j] + 1 + 2 * h + 2)
                    if h % 2 == 0:
                        for tt in range(ST):
                            read_out(pe, T, 4 + tt if h == 0 else 4 * (8 + tt // 2) + tt % 2)
                    if 1 <= h <= 2:
                        pe.wait_ge(b_o_ready, h)
                        pe.wait_ge(b_std_ready, h)
                        pe.wait_ge(b_factor_ready, h)
                    for d in range(2):
                        bank = head_bank(h, d)
                        c0 = h * DV + d * P
                        for j in range(ST):
                            last = pe.matmul(bank[:, j * P:S], b_v[:, j, c0:c0 + P],
                                             b_at[h % 2][:, j, j * P:S], start=j == 0, stop=j == ST - 1)
                    last.then_inc(pv_done, 1)

                def head_sum(h):
                    pe.wait_ge(b_sq_ready, h + 1)
                    for j in range(ST):
                        for d in range(2):
                            last = pe.matmul(stat[:, ST * h + j:ST * h + j + 1],
                                             b_qk[:, 2 * h + d, j * P:(j + 1) * P], ones[:, 0:1],
                                             start=d == 0, stop=d == 1)
                    last.then_inc(b_ss_done, 1)

                def spread_inverse(h):
                    pe.wait_ge(b_inv_ready, h + 1)
                    if h:
                        pe.wait_ge(b_factor_ready, h)
                    pe.matmul(aux[:, :], ones[:, :], b_qk[:, 8 + 2 * h, :], start=True, stop=True)\
                      .then_inc(b_inv_spread, 1)

                chunk(0)
                for n in range(4 * HEADS):
                    scores(n)
                    if n + 1 < 4 * HEADS:
                        chunk(n + 1)
                    if n >= 1:
                        turn(n - 1)
                    if n in (5, 9):
                        mix(n // 4 - 1)
                    if n in (7, 11):
                        head_sum(n // 4 - 1)
                    if n in (8, 12):
                        spread_inverse(n // 4 - 2)
                mix(2)
                turn(15)
                mix(3)
                head_sum(2)

                def before_two():
                    spread_inverse(2)
                    head_sum(3)

                out_projection(U + 24, T_B_OUT, Q_B_OUT, 5, {2: before_two, 4: lambda: spread_inverse(3)})

            pe.wait_ge(pool_consts, 6)
            norm_sum(0, 0)
            norm_sum(0, 1)
            pe.wait_ge(lam_mul_ready, 1)
            pe.matmul(aux[:, 16:18], ones[:, :], lam_mul[:, :], start=True, stop=True).then_inc(lam_sum_done, 1)
            pe.wait_ge(lam_exp_ready, 1)
            pe.wait_ge(early_used, KT)
            colsum(ada_acc, 0)
            pe.wait_ge(early_used, 2 * KT)
            pe.wait_ge(ada_ready, 1)
            colsum(early_acc, 1)
            spread_rstd(0, 0)
            ffn(0, EARLY, ADA_F0)
            mixer_a()
            ffn(1, EARLY + ADA_F0, ADA_F1)
            ffn(2, 0, 0)
            mixer_b()
            ffn(3, 0, 0)

        @block.scalar
        def _(act):
            def high_part(base, more=0, n=1024):
                act.wait_ge(raw_loaded[base % RAWS], 16 * (base // RAWS + 1) + (16 // RAWS) * more)
                if base >= SLOTS:
                    act.wait_ge(unit_done, base + more - SLOTS + 1)
                act.activation(w_hi[base % SLOTS][:, 0:n], raw[base % RAWS][:, 0:n], ACT.Copy)\
                   .then_inc(hi_ready, 1)

            def split_high(q, k, t=slice(0, S), bias=None):
                act.wait_ge(src_ready, q + 1)
                if bias is None:
                    ins = act.activation(h_hi[:, k, t], buf[k % 2][:, t], ACT.Copy)
                else:
                    ins = act.activation(h_hi[:, k, t], buf[k % 2][:, t], ACT.Identity,
                                         bias=bias[:, k:k + 1])
                ins.then_inc(act_hi_ready, 1)

            def root(n, half):
                act.wait_ge(stat_done, 2 * n + half + 1)
                act.activation(std_col[:, 2 * half:2 * half + 2], stat[:, 2 * half:2 * half + 2], ACT.Sqrt,
                               bias=eps[:, 0:1], scale=1.0 / D).then_inc(std_ready, 1)

            def norm(n, U, second_squares=lambda: None):
                root(n, 0)
                if n == 0:
                    root(n, 1)
                else:
                    high_part(U)
                    high_part(U + 1)
                act.wait_ge(ada_ready, 3 * n + 1)
                for k in range(KT):
                    split_high(Q_IN[n] + k, k, tok(0), ada_v[:, 3 * n, :])
                    if n and k in (1, 3):
                        high_part(U + 2 + k // 2)
                if n:
                    second_squares()
                    root(n, 1)
                for k in range(KT):
                    split_high(Q_IN[n] + KT + k, k, tok(1), ada_v[:, 3 * n, :])

            def square(r, i, xs, t=slice(0, S), more=0):
                act.wait_ge(sq_added, ADD_BASE[r] + i + 1 + more)
                act.activation(sq[:, t], xs, ACT.Square).then_inc(sq_done, 1)

            def ffn(p):
                U, T, r = U_FFN[p], T_FFN[p], N_FFN[p]

                def step(i, more):
                    for j in range(2):
                        u, f = U + 4 * i + 2 * j, 2 * i + j
                        F = FT * p + f
                        act.wait_ge(unit_done, u + 1 + 4 * more)
                        if F >= 2:
                            act.wait_ge(g_lo_ready, F - 1 + 2 * more)
                        act.activation(buf[j][:, :], acc[:, 2 * j, :], ACT.Silu)\
                           .then_inc(acc_free[2 * j], 1)
                        high_part(u + 4, 4 * more)
                        act.wait_ge(acc_free[2 * j + 1], T[2 * j + 1] + i + 1 + more)
                        dst = g_hi[:, f, :] if isinstance(more, int) else \
                            g_hi[:, bass.ds(2 * more + f, 1), :].rearrange("p a s -> p (a s)")
                        act.activation(dst, buf[j][:, :], ACT.Copy).then_inc(g_hi_ready, 1)
                        high_part(u + 5, 4 * more)

                step(0, 0)
                with act.Fori(0, FT // 2 - 1) as i:
                    step(1, i)
                W = U + N13

                act.preload_act_table(ACT.Sqrt)

                def out_tile(o, more=0):
                    for m in range(4):
                        high_part(W + 4 * (o + 1) + m, 8 * more, W2_SPLIT[m] * P)
                    act.wait_ge(out_free[o % 2], O_FFN[p][o % 2] + 1 + o // 2 + 1 + more)
                    xs = x[:, o, :] if isinstance(more, int) else \
                        x[:, bass.ds(2 * more + o, 1), :].rearrange("p a s -> p (a s)")
                    square(r, o, xs, more=2 * more)

                def last_tile(half):
                    bank = 1 - half
                    act.wait_ge(out_free[bank], O_FFN[p][bank] + 1 + KT // 2 + half)
                    square(r, KT - 1 + half, x[:, KT - 1, tok(half)], tok(half))

                with act.Fori(0, KT // 2 - 1) as i:
                    out_tile(0, i)
                    out_tile(1, i)
                out_tile(KT - 2)
                last_tile(0)
                return lambda: last_tile(1)

            def out_projection(U, T, r):
                act.preload_act_table(ACT.Sqrt)
                for o in range(4):
                    high_part(U + o + 4)
                    read_out(act, T, o)
                    square(r, o, x[:, o, :])

                def last_tiles(half):
                    for o in range(4, KT):
                        read_out(act, T, o + 4 * half)
                        square(r, o + 4 * half, x[:, o, tok(half)], tok(half))

                last_tiles(0)
                return lambda: last_tiles(1)

            def mixer_a():
                U, T = U_A, T_A
                for t in range(8):
                    high_part(U + t + 4)
                    read_out(act, T, t)
                    act.activation(a_qk[:, t, :], buf[t % 2][:, :], ACT.Silu).then_inc(a_qk_ready, 1)
                high_part(U + 12)
                act.wait_ge(f_arg_ready, 1)
                act.activation(rows[:, 5, :], rows[:, 3, :], ACT.Exp).then_inc(act_step, 1)
                act.wait_ge(act_step, 1)
                act.activation(rows[:, 6, :], rows[:, 5, :], ACT.Ln, bias=1.0).then_inc(f_log_ready, 1)
                v_evac(U + 9, a_v, 0)
                v_evac(U + 13, a_v, 1)
                act.wait_ge(m_rows_ready, 1)
                act.activation(rows[:, 6, :], rows[:, 5, :], ACT.Exp, scale=-1.0).then_inc(em_row_ready, 1)

                def keep_rows(n, dst):
                    for h in range(HEADS):
                        act.wait_ge(spread_done, 4 * n + h + 1)
                        act.activation(dst[:, h, :], acc[:, h, :], ACT.Copy).then_inc(acc_free[h], 1)

                def o_gate(t):
                    act.wait_ge(unit_done, U + 17 + t + 1)
                    act.activation(a_o[:, t, :], stat[:, :], ACT.Tanh, scale=0.5).then_inc(a_o_ready, 1)

                def decays(h):
                    act.wait_ge(diag_ready, h + 1)
                    if h >= 2:
                        act.wait_ge(av_done, h - 1)
                    for j in range(ST):
                        u = u_col[:, 4 * j + h:4 * j + h + 1]
                        o = WT_OFF[j]
                        ins = act.activation(a_wt[h % 2][:, o:o + P], buf[h % 2][:, j * P:(j + 1) * P],
                                             ACT.Exp, bias=u)
                        if j < ST - 1:
                            ins = act.activation(a_wt[h % 2][:, o + P:o + S - j * P],
                                                 neg_m[:, h, (j + 1) * P:S], ACT.Exp, bias=u)
                    ins.then_inc(decay_ready, 1)

                def head_square(h):
                    for d in range(2):
                        act.wait_ge(out_free[d], O_A[d] + 1 + h + 1)
                    act.activation(a_qk[:, h:h + 5:4, :], a_h[:, 2 * h:2 * h + 2, :], ACT.Square)\
                       .then_inc(a_sq_ready, 1)

                def head_root(h, n, bank):
                    act.wait_ge(a_ss_done, h + n)
                    cs = slice(ST * h, ST * (h + n))
                    act.activation(head_std[:, cs], bank[:, cs], ACT.Sqrt, bias=eps[:, 0:1], scale=1.0 / DV)\
                       .then_inc(a_std_ready, n)

                def keep_factor(h, bank):
                    act.wait_ge(a_inv_spread, h + 1)
                    act.activation(exp_m[:, h, :], bank, ACT.Copy).then_inc(a_factor_ready, 1)

                keep_rows(0, neg_m)
                decays(0)
                o_gate(0)
                high_part(U + 21)
                keep_rows(1, exp_m)
                decays(1)
                o_gate(1)
                high_part(U + 22)
                decays(2)
                o_gate(2)
                high_part(U + 23)
                head_square(0)
                o_gate(3)
                high_part(U + 24)
                decays(3)
                o_gate(4)
                high_part(U + 25)
                head_square(1)
                o_gate(5)
                high_part(U + 26)
                o_gate(6)
                high_part(U + 27)
                head_square(2)
                head_root(0, 2, acc[:, 2, :])
                high_part(U + 28)
                keep_factor(0, acc[:, 0, :])
                keep_factor(1, acc[:, 1, :])
                head_root(2, 1, acc[:, 2, :])
                o_gate(7)
                act.preload_act_table(ACT.Sqrt)
                for k in range(KT):
                    split_high(Q_A_OUT + k, k)
                    if k == 1:
                        keep_factor(2, acc[:, 3, :])
                    if k == 3:
                        head_square(3)
                    if k == 4:
                        head_root(3, 1, aux)
                    if k == 5:
                        keep_factor(3, aux[:, :])
                return out_projection(U + 25, T_A_OUT, 1)

            def v_evac(U, dst, half):
                for m in range(4):
                    high_part(U + m + 4)
                act.wait_ge(unit_done, U + 4)
                for tt in range(2):
                    act.activation(dst[:, tt, half * 512:half * 512 + 512], acc[:, tt, :], ACT.Copy)\
                       .then_inc(acc_free[tt], 1)

            def mixer_b():
                U, T = U_B, T_B

                def keep_qk(t, bank):
                    act.activation(b_qk[:, QK_TILE[t], :], acc[:, bank, :], ACT.Copy,
                                   scale=DK ** -0.5 if QK_TILE[t] < 8 else 1.0).then_inc(acc_free[bank], 1)

                for t in range(4):
                    high_part(U + t + 4)
                    act.wait_ge(unit_done, U + t + 1)
                    keep_qk(t, t)
                act.wait_ge(trig_arg, 2)
                act.activation(b_cos[:, :], b_cos[:, :], ACT.Sin).then_inc(trig_ready, 1)
                act.activation(b_sin[:, :], b_sin[:, :], ACT.Sin).then_inc(trig_ready, 1)
                v_evac(U + 4, b_v, 0)

                def keep_chunk(c):
                    if c < 12:
                        act.wait_ge(unit_done, U + 8 + c + 1)
                        keep_qk(4 + c, c % 2)
                        high_part(U + 12 + c)
                        return
                    if c < 15:
                        act.wait_ge(v_part_done, c - 11)
                    else:
                        act.wait_ge(unit_done, U + 24)
                    act.activation(b_v[:, c - 12, 512:1024], acc[:, c % 2, :], ACT.Copy)\
                       .then_inc(acc_free[c % 2], 1)

                def exps(n):
                    h, i = divmod(n, ST)
                    act.wait_ge(max_ready, n + 1)
                    if n >= 2:
                        act.wait_ge(turned, n - 1)
                        act.wait_ge(p_ready, n - 1)
                    for c in range(2):
                        act.activation(b_p[n % 2][:, c, 0:(i + 1) * P], acc[:, 2 + c, 0:(i + 1) * P], ACT.Exp,
                                       bias=neg_max[:, n % 2, c:c + 1], accum_out=row_sum[:, n % 2, c:c + 1])\
                           .then_inc(acc_free[2 + c], 1)

                def keep_turned(n):
                    h, i = divmod(n, ST)
                    act.wait_ge(turned, n + 1)
                    if h >= 2:
                        act.wait_ge(pv_done, h - 1)
                    act.activation(b_at[h % 2][:, 0:i + 1, i * P:(i + 1) * P],
                                   outp[:, n % 2, 0:(i + 1) * P].rearrange("p (j k) -> p j k", k=P), ACT.Copy)\
                       .then_inc(out_free[n % 2], 1)

                def head_square(h):
                    act.wait_ge(b_o_ready, h + 1)
                    act.activation(b_qk[:, 2 * h:2 * h + 2, :], b_o[:, 2 * h:2 * h + 2, :], ACT.Square)\
                       .then_inc(b_sq_ready, 1)

                def head_root(h):
                    act.wait_ge(b_ss_done, h + 1)
                    cs = slice(ST * h, ST * h + ST)
                    act.activation(head_std[:, cs], stat[:, cs], ACT.Sqrt, bias=eps[:, 0:1], scale=1.0 / DV)\
                       .then_inc(b_std_ready, 1)

                def keep_factor(h):
                    act.wait_ge(b_inv_spread, h + 1)
                    act.activation(b_qk[:, 9 + 2 * h, :], aux[:, :], ACT.Copy).then_inc(b_factor_ready, 1)

                for n in range(4 * HEADS):
                    keep_chunk(n)
                    if n in (8, 12):
                        head_root(n // 4 - 2)
                    if n in (9, 13):
                        keep_factor(n // 4 - 2)
                    if n == 15:
                        high_part(U + 24)
                    exps(n)
                    if n == 15:
                        high_part(U + 25)
                    if n >= 1:
                        keep_turned(n - 1)
                    if n in (6, 10):
                        head_square(n // 4 - 1)
                high_part(U + 26)
                keep_turned(15)
                head_square(2)
                high_part(U + 27)
                for k in range(KT):
                    split_high(Q_B_OUT + k, k)
                    if k == 1:
                        head_root(2)
                        head_square(3)
                    if k == 3:
                        keep_factor(2)
                        head_root(3)
                    if k == 5:
                        keep_factor(3)
                return out_projection(U + 24, T_B_OUT, 4)

            act.dma_start(col[:, :], cols).then_inc(col_loaded, 16)
            act.dma_start(x[:, :, :], xT).then_inc(x_loaded, 16)
            act.dma_start(gbias[:, :], gate_bias).then_inc(small_loaded, 16)
            act.dma_start(rope_row[:, :], rope_rows).then_inc(small_loaded, 16)
            act.wait_ge(col_loaded, 16)
            act.activation(cond[:, :], col[:, COLS["c"]:COLS["c"] + KT], ACT.Silu).then_inc(cond_ready, 1)
            act.wait_ge(x_loaded, 16)
            for k in range(KT):
                act.activation(x_sq[:, k, :], x[:, k, :], ACT.Square).then_inc(sq_done, 1)
            act.wait_ge(lam_sum_done, 1)
            act.activation(lam_exp[:, :], aux[:, 16:18], ACT.Exp).then_inc(lam_exp_ready, 1)
            act.wait_ge(pool_consts, 6)
            for u in range(SLOTS):
                high_part(u)
            norm(0, U_F0)
            second_squares = ffn(0)
            for n, (U, phase) in enumerate(((U_A, mixer_a), (U_F1, lambda: ffn(1)), (U_F2, lambda: ffn(2)),
                                            (U_B, mixer_b), (U_F3, lambda: ffn(3)))):
                norm(n + 1, U, second_squares)
                second_squares = phase()
            root(SUBS, 0)
            second_squares()
            root(SUBS, 1)

        @block.vector
        def _(dve):
            chain = [0]

            def link(ins):
                chain[0] += 1
                ins.then_inc(dve_step, 1)
                dve.wait_ge(dve_step, chain[0])

            def colv(name, k, n=1):
                return col[:, COLS[name] + k:COLS[name] + k + n]

            def lows(q, bias, make, t=slice(0, S)):
                def low(k):
                    dve.wait_ge(act_hi_ready, q + k + 1)
                    hi = h_hi[:, k, t].bitcast(F32)
                    if bias is None:
                        ins = dve.tensor_tensor(h_lo[:, k, t], buf[k % 2][:, t], hi, ALU.subtract)
                    else:
                        ins = dve.scalar_tensor_tensor(out=h_lo[:, k, t], in0=buf[k % 2][:, t],
                                                       scalar=bias[:, k:k + 1], in1=hi,
                                                       op0=ALU.add, op1=ALU.subtract)
                    ins.then_inc(act_lo_ready, 1)

                for k in range(KT + 1):
                    if k < KT:
                        if k >= 2:
                            dve.wait_ge(act_lo_ready, q + k - 1)
                        make(k)
                    if k >= 1:
                        low(k - 1)

            def inverse_rms(n, half):
                two = slice(2 * half, 2 * half + 2)
                dve.wait_ge(std_ready, 2 * n + half + 1)
                link(dve.reciprocal(inv_col[:, two], std_col[:, two]))
                dve.tensor_tensor(rstd[:, tok(half)].rearrange("p (j k) -> p j k", k=P),
                                  ident[:, :].unsqueeze(1).broadcast_to([P, 2, P]),
                                  inv_col[:, two].unsqueeze(2).broadcast_to([P, 2, P]), ALU.mult)\
                   .then_inc(rstd_ready, 1)

            def norm(n, second_half=lambda: None):
                dve.wait_ge(ada_ready, 3 * n + 2)
                dve.scalar_tensor_tensor(out=scale_col[:, :], in0=ada_v[:, 3 * n + 1, :], scalar=1.0,
                                         in1=colv("norm_g", n * KT, KT), op0=ALU.add, op1=ALU.mult)\
                   .then_inc(scale_ready, 1)
                for half in range(2):
                    t = tok(half)
                    if half:
                        second_half()
                    inverse_rms(n, half)
                    if half == 0:
                        dve.wait_ge(scale_ready, n + 1)
                    dve.wait_ge(rstd_spread, 2 * n + half + 1)
                    lows(Q_IN[n] + KT * half, ada_v[:, 3 * n, :], lambda k:
                         dve.scalar_tensor_tensor(out=buf[k % 2][:, t], in0=x[:, k, t],
                                                  scalar=scale_col[:, k:k + 1], in1=rstd_bank(half),
                                                  op0=ALU.mult, op1=ALU.mult).then_inc(src_ready, 1), t)

            def prepare_residual(r, factor):
                dve.wait_ge(ada_ready, 3 * r + 3)
                dve.tensor_scalar(gate_col[:, :], ada_v[:, 3 * r + 2, :], factor, None, ALU.mult)\
                   .then_inc(gate_ready, 1)
                dve.memset(sumsq[:, :], 0.0).then_inc(sq_added, 1)
                dve.wait_ge(gate_ready, r + 1)

            def residual(r, i, o, bank, free, t=slice(0, S), more=0, dyn=None):
                xs = x[:, o, t] if dyn is None else x[:, bass.ds(dyn, 1), :].rearrange("p a s -> p (a s)")
                g = gate_col[:, o:o + 1] if dyn is None else gate_col[:, bass.ds(dyn, 1)]
                dve.scalar_tensor_tensor(out=xs, in0=bank, scalar=g, in1=xs, op0=ALU.mult, op1=ALU.add)\
                   .then_inc(free, 1)
                dve.wait_ge(sq_done, KT + SQ_BASE[r] + i + 1 + more)
                dve.wait_ge(sq_added, ADD_BASE[r] + i + 1 + more)
                dve.tensor_tensor(sumsq[:, t], sumsq[:, t], sq[:, t], ALU.add).then_inc(sq_added, 1)

            def ada_evac(sl, more=0):
                dve.wait_ge(colsum_done, sl + 1 + more)
                if isinstance(more, int):
                    dst, b = ada_v[:, sl + more, :], colv("ada_b", (sl + more) * KT, KT)
                else:
                    dst = ada_v[:, bass.ds(more + sl, 1), :].rearrange("p a s -> p (a s)")
                    b = col[:, bass.ds(8 * more + COLS["ada_b"] + sl * KT, KT)]
                dve.tensor_tensor(dst, aux[:, 0:KT], b, ALU.add).then_inc(ada_ready, 1)

            def ada_half(sl, first, more=0):
                for k in range(first, first + 4):
                    a = (sl - EARLY) * KT + k
                    dve.wait_ge(ada_loaded[k % 2], 16 * (a // 2 + 1) + 64 * more)
                    if k == 0:
                        dve.wait_ge(colsum_done, sl + more)
                        ins = dve.tensor_scalar(ada_acc[:, :], ada_raw[0][:, :], cond[:, 0:1], None, ALU.mult)
                    else:
                        dve.wait_ge(ada_used, a + 8 * more)
                        ins = dve.scalar_tensor_tensor(out=ada_acc[:, :], in0=ada_raw[k % 2][:, :],
                                                       scalar=cond[:, k:k + 1], in1=ada_acc[:, :],
                                                       op0=ALU.mult, op1=ALU.add)
                    ins.then_inc(ada_used, 1)

            def ffn(p, ada_first, ada_steps):
                U, T, r = U_FFN[p], T_FFN[p], N_FFN[p]

                def step(i, more, halves, evac):
                    for j in range(2):
                        u, f = U + 4 * i + 2 * j, 2 * i + j
                        F = FT * p + f
                        dve.wait_ge(unit_done, u + 2 + 4 * more)
                        dve.wait_ge(acc_free[2 * j], T[2 * j] + i + 1 + more)
                        dve.tensor_tensor(buf[j][:, :], buf[j][:, :], acc[:, 2 * j + 1, :], ALU.mult)\
                           .then_inc(acc_free[2 * j + 1], 1)
                        dve.wait_ge(g_hi_ready, F + 1 + 2 * more)
                        if isinstance(more, int):
                            lo, hi = g_lo[:, f, :], g_hi[:, f, :]
                        else:
                            lo, hi = (g[:, bass.ds(2 * more + f, 1), :].rearrange("p a s -> p (a s)")
                                      for g in (g_lo, g_hi))
                        dve.tensor_tensor(lo, buf[j][:, :], hi.bitcast(F32), ALU.subtract)\
                           .then_inc(g_lo_ready, 1)
                        if evac and j == 0:
                            ada_evac(ada_first + i - 1, more)
                        if halves:
                            ada_half(ada_first + i, 4 * j, more)

                step(0, 0, ada_steps > 0, False)
                done = 1
                if ada_steps > 1:
                    with dve.Fori(0, ada_steps - 1) as i:
                        step(1, i, True, True)
                    done = ada_steps
                if ada_steps and done < FT // 2:
                    step(done, 0, False, True)
                    done += 1
                    evac_left = False
                else:
                    evac_left = ada_steps > 0
                if done < FT // 2:
                    with dve.Fori(0, FT // 2 - done) as i:
                        step(done, i, False, False)
                if evac_left:
                    ada_evac(ada_first + ada_steps - 1)
                prepare_residual(r, 0.5)
                W = U + N13
                with dve.Fori(0, KT // 2 - 1) as i:
                    for j in range(2):
                        dve.wait_ge(unit_done, W + 4 * j + 4 + 8 * i)
                        residual(r, j, j, outp[:, j, :], out_free[j], more=2 * i, dyn=2 * i + j)
                dve.wait_ge(unit_done, W + 4 * (KT - 1))
                residual(r, KT - 2, KT - 2, outp[:, 0, :], out_free[0])
                dve.wait_ge(half_done, HALVES[r] + 1)
                residual(r, KT - 1, KT - 1, outp[:, 1, tok(0)], out_free[1], tok(0))

                def second_half():
                    dve.wait_ge(unit_done, W + 4 * KT)
                    residual(r, KT, KT - 1, outp[:, 0, tok(1)], out_free[0], tok(1))
                return second_half

            def out_projection(U, r):
                prepare_residual(r, 1.0)
                for o in range(4):
                    dve.wait_ge(unit_done, U + o + 1)
                    residual(r, o, o, acc[:, o % 4, :], acc_free[o % 4])
                for o in range(4, KT):
                    dve.wait_ge(half_done, HALVES[r] + o - 4 + 1)
                    residual(r, o, o, acc[:, o % 4, tok(0)], acc_free[o % 4], tok(0))

                def second_half():
                    for o in range(4, KT):
                        dve.wait_ge(unit_done, U + o + 1)
                        residual(r, o + 4, o, acc[:, o % 4, tok(1)], acc_free[o % 4], tok(1))
                return second_half

            def v_evac(U, dst, half):
                dve.wait_ge(unit_done, U + 4)
                for tt in range(2, 4):
                    dve.tensor_copy(dst[:, tt, half * 512:half * 512 + 512], acc[:, tt, :])\
                       .then_inc(acc_free[tt], 1)

            def mixer_a():
                U, T = U_A, T_A
                for t in range(8):
                    dve.wait_ge(unit_done, U + t + 1)
                    if t >= 2:
                        dve.wait_ge(a_qk_ready, t - 1)
                    y, p = buf[t % 2], acc[:, t % 4, :]
                    tap = [colv("conv_w", TAPS * t + j) for j in range(TAPS)]
                    link(dve.tensor_scalar(y[:, :], p, tap[3], colv("conv_b", t), ALU.mult, ALU.add))
                    for back in range(1, TAPS):
                        ins = dve.scalar_tensor_tensor(out=y[:, back:S], in0=p[:, 0:S - back],
                                                       scalar=tap[3 - back], in1=y[:, back:S],
                                                       op0=ALU.mult, op1=ALU.add)
                        if back < TAPS - 1:
                            link(ins)
                    ins.then_inc(acc_free[t % 4], 1)
                dve.wait_ge(unit_done, U + 9)
                dve.wait_ge(small_loaded, 32)
                R = [rows[:, n, :] for n in range(8)]
                dve.tensor_scalar(R[0], aux[0:HEADS, :], gbias[:, 0:1], None, ALU.add).then_inc(dve_step, 1)
                link(dve.tensor_copy(R[1], aux[32:32 + HEADS, :]))
                chain[0] += 1
                dve.wait_ge(dve_step, chain[0])
                link(dve.tensor_scalar(R[2], R[1], gbias[:, 1:2], None, ALU.add))
                dve.tensor_scalar(R[4], R[2], 0.0, None, ALU.min).then_inc(dve_step, 1)
                chain[0] += 1
                dve.scalar_tensor_tensor(out=R[3], in0=R[2], scalar=-1.0, in1=R[2],
                                         op0=ALU.mult, op1=ALU.min).then_inc(f_arg_ready, 1)
                dve.wait_ge(dve_step, chain[0])
                dve.wait_ge(f_log_ready, 1)
                link(dve.tensor_tensor(R[7], R[4], R[6], ALU.subtract))
                link(dve.tensor_tensor_scan(R[1], rows_one[:, :], R[7], 0.0, ALU.mult, ALU.add))
                link(dve.tensor_tensor(R[2], R[0], R[1], ALU.subtract))
                link(dve.tensor_tensor_scan(R[3], R[2], R[2], 0.0, ALU.max, ALU.max))
                link(dve.tensor_scalar(R[4], R[3], -1.0, None, ALU.mult))
                dve.tensor_tensor(R[5], R[1], R[3], ALU.add).then_inc(m_rows_ready, 1)
                v_evac(U + 9, a_v, 0)
                v_evac(U + 13, a_v, 1)
                dve.wait_ge(u_turned, 1)
                dve.tensor_copy(u_col[:, :], stat[:, 0:ST * HEADS]).then_inc(u_col_ready, 1)

                def diagonal(h):
                    read_out(dve, T, 16 + h)
                    if h >= 2:
                        dve.wait_ge(decay_ready, h - 1)
                    dve.tensor_tensor(buf[h % 2][:, :].rearrange("p (j k) -> p j k", k=P),
                                      neg_m[:, h, :].rearrange("p (j k) -> p j k", k=P),
                                      mask_st[:, :].unsqueeze(1).broadcast_to([P, ST, P]), ALU.add)\
                       .then_inc(diag_ready, 1)

                def weights(h):
                    dve.wait_ge(decay_ready, h + 1)
                    for j in range(ST):
                        dve.wait_ge(st_done, 4 * h + j + 1)
                        w = a_wt[h % 2][:, WT_OFF[j]:WT_OFF[j] + S - j * P]
                        dve.scalar_tensor_tensor(out=w, in0=acc[:, j, 0:S - j * P], scalar=DK ** -0.5, in1=w,
                                                 op0=ALU.mult, op1=ALU.mult)\
                           .then_inc(acc_free[j], 1)

                def heads_out(h):
                    dve.wait_ge(av_done, h + 1)
                    read_out(dve, T, 20 + h)
                    dve.scalar_tensor_tensor(out=rstd[:, :], in0=aux[:, :], scalar=-1.0, in1=exp_m[:, h, :],
                                             op0=ALU.mult, op1=ALU.max).then_inc(dve_step, 1)
                    chain[0] += 1
                    dve.wait_ge(dve_step, chain[0])
                    dve.tensor_tensor(rstd[:, :], aux[:, :], rstd[:, :], ALU.max).then_inc(den_read, 1)
                    dve.wait_ge(den_read, h + 1)
                    link(dve.reciprocal(sq[:, :], rstd[:, :]))
                    for d in range(2):
                        dve.tensor_tensor(a_h[:, 2 * h + d, :], outp[:, d, :], sq[:, :], ALU.mult)\
                           .then_inc(out_free[d], 1)

                def gated(t):
                    dve.wait_ge(a_o_ready, t + 1)
                    dve.scalar_tensor_tensor(out=a_o[:, t, :], in0=a_o[:, t, :], scalar=1.0,
                                             in1=a_h[:, t, :], op0=ALU.add, op1=ALU.mult)\
                       .then_inc(gated_ready, 1)

                def inverse(h):
                    cs = slice(ST * h, ST * h + ST)
                    dve.wait_ge(a_std_ready, h + 1)
                    link(dve.reciprocal(head_inv[:, cs], head_std[:, cs]))
                    dve.tensor_tensor(neg_m[:, h, :].rearrange("p (j k) -> p j k", k=P),
                                      ident[:, :].unsqueeze(1).broadcast_to([P, ST, P]),
                                      head_inv[:, cs].unsqueeze(2).broadcast_to([P, ST, P]), ALU.mult)\
                       .then_inc(a_inv_ready, 1)

                link(dve.tensor_scalar(ag_col[:, :], colv("a_norm_g", 0, 8), 0.5, None, ALU.mult))
                diagonal(0)
                diagonal(1)
                weights(0)
                diagonal(2)
                weights(1)
                diagonal(3)
                heads_out(0)
                weights(2)
                heads_out(1)
                weights(3)
                gated(0)
                gated(1)
                heads_out(2)
                inverse(0)
                inverse(1)
                for t in range(2, 6):
                    gated(t)

                def make(t):
                    h = t // 2
                    if t == 2:
                        inverse(2)
                    if t == 4:
                        heads_out(3)
                    if t == 6:
                        gated(6)
                        gated(7)
                        inverse(3)
                    dve.wait_ge(a_factor_ready, h + 1)
                    dve.wait_ge(gated_ready, t + 1)
                    dve.scalar_tensor_tensor(out=buf[t % 2][:, :], in0=a_o[:, t, :],
                                             scalar=ag_col[:, t:t + 1], in1=exp_m[:, h, :],
                                             op0=ALU.mult, op1=ALU.mult).then_inc(src_ready, 1)
                lows(Q_A_OUT, None, make)
                return out_projection(U + 25, 1)

            def trig_tables():
                C, Sn, A, B = b_cos[:, :], b_sin[:, :], b_rot[:, :], b_tmp[:, :]
                dve.wait_ge(pos_loaded, 16)
                link(dve.tensor_copy(A, pos_i[:, :]))
                link(dve.tensor_scalar(A, A, rope_row[:, 0:1], None, ALU.mult))
                rounder = 1.5 * 2.0 ** 23
                for step in (2.0 ** 20, 2.0 ** 10, 1.0):
                    link(dve.tensor_scalar(B, A, 1.0 / (step * TWO_PI), rounder, ALU.mult, ALU.add))
                    link(dve.tensor_scalar(B, B, rounder, None, ALU.subtract))
                    for part in two_pi_parts(step):
                        link(dve.scalar_tensor_tensor(out=A, in0=B, scalar=-part, in1=A,
                                                      op0=ALU.mult, op1=ALU.add))
                link(dve.tensor_scalar(A, A, math.pi * (1 - 2.0 ** -22), -math.pi * (1 - 2.0 ** -22),
                                       ALU.min, ALU.max))
                dve.tensor_scalar(Sn, A, rope_row[:, 1:2], None, ALU.mult).then_inc(trig_arg, 1)
                link(dve.scalar_tensor_tensor(out=B, in0=A, scalar=-1.0, in1=A, op0=ALU.mult, op1=ALU.min))
                dve.tensor_scalar(C, B, math.pi / 2, None, ALU.add).then_inc(trig_arg, 1)

            def mixer_b():
                U, T = U_B, T_B
                trig_tables()
                dve.wait_ge(trig_ready, 2)
                dve.tensor_scalar(bg_col[:, :], colv("b_norm_g", 0, 2), 1.0 - LAM_INIT, None, ALU.mult)\
                   .then_inc(dve_step, 1)
                chain[0] += 1
                swap = [(n + HALF) % ROPE_DIM for n in range(ROPE_DIM)]

                def rope(t):
                    read_out(dve, T, t if t < 4 else 4 * (2 + (t - 4) // 2) + t % 2)
                    q = b_qk[0:ROPE_DIM, QK_TILE[t], :]
                    link(dve.stream_shuffle(b_rot[:, :], q, swap))
                    dve.tensor_tensor(b_tmp[:, :], q, b_cos[:, :], ALU.mult).then_inc(dve_step, 1)
                    chain[0] += 1
                    link(dve.tensor_tensor(b_rot[:, :], b_rot[:, :], b_sin[:, :], ALU.mult))
                    dve.tensor_tensor(q, b_tmp[:, :], b_rot[:, :], ALU.add).then_inc(rope_done, 1)
                    dve.wait_ge(rope_done, t + 1)

                def maxima(n):
                    h, i = divmod(n, ST)
                    dve.wait_ge(s_done, 2 * n + 2)
                    diag = acc[:, 2:4, i * P:(i + 1) * P]
                    link(dve.tensor_tensor(diag, diag, mask_ts[:, :].unsqueeze(1).broadcast_to([P, 2, P]), ALU.add))
                    link(dve.tensor_reduce(row_max[:, n % 2, :], acc[:, 2:4, 0:(i + 1) * P], AX.X, ALU.max))
                    dve.tensor_scalar(neg_max[:, n % 2, :], row_max[:, n % 2, :], -1.0, None, ALU.mult)\
                       .then_inc(max_ready, 1)

                def combine(n):
                    h, i = divmod(n, ST)
                    N = (i + 1) * P
                    inv, pr = row_inv[:, n % 2, :], b_p[n % 2]
                    for c in range(2):
                        read_out(dve, T, 4 * (2 + n) + 2 + c)
                    link(dve.reciprocal(inv, row_sum[:, n % 2, :]))
                    link(dve.tensor_tensor(inv[:, 1:2], inv[:, 1:2], neg_lam[:, :], ALU.mult))
                    link(dve.tensor_scalar(pr[:, 1, 0:N], pr[:, 1, 0:N], inv[:, 1:2], None, ALU.mult))
                    dve.scalar_tensor_tensor(out=pr[:, 0, 0:N], in0=pr[:, 0, 0:N], scalar=inv[:, 0:1],
                                             in1=pr[:, 1, 0:N], op0=ALU.mult, op1=ALU.add).then_inc(p_ready, 1)

                def keep(h):
                    dve.wait_ge(pv_done, h + 1)
                    dve.tensor_copy(b_o[:, 2 * h, :], head_bank(h, 0)).then_inc(dve_step, 1)
                    chain[0] += 1
                    dve.wait_ge(dve_step, chain[0])
                    dve.tensor_copy(b_o[:, 2 * h + 1, :], head_bank(h, 1)).then_inc(b_o_ready, 1)

                def inverse(h):
                    cs = slice(ST * h, ST * h + ST)
                    dve.wait_ge(b_std_ready, h + 1)
                    link(dve.reciprocal(head_inv[:, cs], head_std[:, cs]))
                    dve.tensor_tensor(b_qk[:, 8 + 2 * h, :].rearrange("p (j k) -> p j k", k=P),
                                      ident[:, :].unsqueeze(1).broadcast_to([P, ST, P]),
                                      head_inv[:, cs].unsqueeze(2).broadcast_to([P, ST, P]), ALU.mult)\
                       .then_inc(b_inv_ready, 1)

                for t in range(4):
                    rope(t)
                v_evac(U + 4, b_v, 0)
                dve.wait_ge(lam_ready, 1)
                for n in range(4 * HEADS):
                    if n < 12:
                        rope(4 + n)
                    maxima(n)
                    if n >= 1:
                        combine(n - 1)
                    if n in (6, 10):
                        keep(n // 4 - 1)
                    if n in (8, 12):
                        inverse(n // 4 - 2)
                combine(15)
                keep(2)

                def make(t):
                    h = t // 2
                    if t == 2:
                        keep(3)
                        inverse(2)
                    if t == 4:
                        inverse(3)
                    dve.wait_ge(b_factor_ready, h + 1)
                    dve.scalar_tensor_tensor(out=buf[t % 2][:, :], in0=b_o[:, t, :],
                                             scalar=bg_col[:, t % 2:t % 2 + 1], in1=b_qk[:, 9 + 2 * h, :],
                                             op0=ALU.mult, op1=ALU.mult).then_inc(src_ready, 1)
                lows(Q_B_OUT, None, make)
                return out_projection(U + 24, 4)

            for j in range(2):
                dve.memset(outp[:, j, :], 0.0).then_inc(out_free[j], 1)
            link(dve.memset(rows_one[:, :], 1.0))
            dve.wait_ge(col_loaded, 16)
            lam = COLS["lam"]
            dve.tensor_tensor(lam_mul[:, :], col[:, lam:lam + 3:2], col[:, lam + 1:lam + 4:2], ALU.mult)\
               .then_inc(lam_mul_ready, 1)
            dve.wait_ge(lam_exp_ready, 1)
            link(dve.tensor_tensor(neg_lam[:, :], lam_exp[:, 1:2], lam_exp[:, 0:1], ALU.subtract))
            dve.tensor_scalar(neg_lam[:, :], neg_lam[:, :], LAM_INIT, None, ALU.subtract).then_inc(lam_ready, 1)
            dve.wait_ge(cond_ready, 1)
            for sl, sums in enumerate((ada_acc, early_acc)):
                for k in range(KT):
                    n = sl * KT + k
                    if n % 4 == 0:
                        dve.wait_ge(early_loaded[n // 4], 16)
                    if k == 0:
                        ins = dve.tensor_scalar(sums[:, :], early_ada[:, n, :], cond[:, 0:1], None, ALU.mult)
                    else:
                        dve.wait_ge(early_used, n)
                        ins = dve.scalar_tensor_tensor(out=sums[:, :], in0=early_ada[:, n, :],
                                                       scalar=cond[:, k:k + 1], in1=sums[:, :],
                                                       op0=ALU.mult, op1=ALU.add)
                    ins.then_inc(early_used, 1)
            ada_evac(0)
            ada_evac(1)
            dve.wait_ge(pool_consts, 6)
            norm(0)
            second_half = ffn(0, EARLY, ADA_F0)
            norm(1, second_half)
            second_half = mixer_a()
            norm(2, second_half)
            second_half = ffn(1, EARLY + ADA_F0, ADA_F1)
            norm(3, second_half)
            second_half = ffn(2, 0, 0)
            norm(4, second_half)
            second_half = mixer_b()
            norm(5, second_half)
            second_half = ffn(3, 0, 0)
            for half in range(2):
                if half:
                    second_half()
                inverse_rms(SUBS, half)
                dve.wait_ge(rstd_spread, 2 * SUBS + half + 1)
                for k in range(KT):
                    dve.scalar_tensor_tensor(out=x[:, k, tok(half)], in0=x[:, k, tok(half)],
                                             scalar=colv("final_g", k), in1=rstd_bank(half),
                                             op0=ALU.mult, op1=ALU.mult).then_inc(src_ready, 1)


def tiles(w):
    n = w.shape[1] // P
    return w.reshape(KT, P, n, P).transpose(2, 1, 0, 3).reshape(n, P, KT * P)


def v_units(w):
    return w.reshape(4, 2, P, 2, 512).transpose(3, 0, 2, 1, 4).reshape(8, P, 1024)


def columns(v):
    return v.reshape(-1, P).T


def kernel(**inputs):
    import concourse.bacc as bacc
    from concourse.bass_utils import run_bass_kernel_spmd

    a = {k: np.asarray(v) for k, v in inputs.items()}
    gates = np.zeros((D, P), np.float32)
    w_in = a["a_w_in"][0]
    gates[:, 0:HEADS] = w_in[:, 3072:3072 + HEADS]
    gates[:, 32:32 + HEADS] = w_in[:, 3072 + HEADS:3080]
    wb_in = a["b_w_in"][0]
    qk, v = tiles(wb_in[:, 0:2048])[list(QK_TILE)], v_units(wb_in[:, 2048:3072])
    cols = np.concatenate([
        columns(a["c"][0]), columns(a["ada_b"]), columns(a["norm_g"]), columns(a["final_g"]),
        a["a_conv_w"][0].reshape(TAPS, 8, P).transpose(2, 1, 0).reshape(P, 32),
        columns(a["a_conv_b"][0]), columns(a["a_norm_g"][0]), columns(a["b_norm_g"][0]),
        a["b_lam"][0].T], axis=1)
    inv_freq = (ROPE_THETA ** (-np.arange(0, ROPE_DIM, 2, dtype=np.float64) / ROPE_DIM)).astype(np.float32)
    rope_rows = np.stack([np.concatenate([inv_freq, inv_freq]),
                          np.repeat(np.array([-1.0, 1.0], np.float32), HALF)], axis=1)
    arrays = {
        "xT": a["x"][0].T.reshape(KT, P, S).transpose(1, 0, 2),
        "cols": cols,
        "gate_bias": a["a_b_if"][0].reshape(2, HEADS).T,
        "rope_rows": rope_rows,
        "positions": a["positions"],
        "ada": a["ada_w"].reshape(LAYERS, KT, P, 9, D).transpose(0, 3, 1, 2, 4).reshape(SLICES * KT, P, D),
        "w13": a["ffn_w13"].reshape(4, KT, P, 2, FT, P).transpose(0, 4, 3, 2, 1, 5).reshape(4 * N13, P, D),
        "w2": a["ffn_w2"].reshape(4, FT, P, KT, P).transpose(0, 3, 2, 1, 4).reshape(4 * KT, P, FF),
        "wa": np.concatenate([tiles(w_in[:, 0:1024]), tiles(gates), v_units(w_in[:, 1024:2048]),
                              tiles(w_in[:, 2048:3072]), tiles(a["a_w_out"][0])]),
        "wb": np.concatenate([qk[0:4], v[0:4], qk[4:16], v[4:8], tiles(a["b_w_out"][0])]),
    }
    nc = bacc.Bacc("TRN2", target_bir_lowering=False, num_devices=1)
    arrays = {k: np.ascontiguousarray(v) for k, v in arrays.items()}
    aps = [nc.dram_tensor(k, v.shape, mybir.dt.from_np(v.dtype), kind="ExternalInput").ap()
           for k, v in arrays.items()]
    out = nc.dram_tensor("out", (KT, P, S), F32, kind="ExternalOutput").ap()
    build_trunk(nc, *aps, out)
    r = run_bass_kernel_spmd(nc, [arrays], core_ids=[0])
    return r.results[0]["out"].reshape(D, S).T.reshape(1, S, D)
```

```python
import math
from contextlib import ExitStack

import numpy as np
import concourse.bass as bass
from concourse import mybir

F32 = mybir.dt.float32
F32R = mybir.dt.float32r
I32 = mybir.dt.int32
ALU = mybir.AluOpType
ACT = mybir.ActivationFunctionType
AX = mybir.AxisListType

P = 128
D = 1024
S = 512
FF = 2816
KT = D // P
FT = FF // P
ST = S // P
HEADS = 4
DK = 128
DV = 256
TAPS = 4
EPS = 1e-6
LAYERS = 2
SUBS = 3 * LAYERS
ROPE_DIM = DK // 4
HALF = ROPE_DIM // 2
ROPE_THETA = 500000.0
LAM_INIT = 0.8 - 0.6 * math.exp(-0.3 * 1)
MASKED = -1e30

SLOTS = 4
RAWS = 2
W2_SPLIT = (6, 6, 5, 5)
W2_START = (0, 6, 12, 17)

N13 = 2 * FT
NW2 = 4 * KT
UNITS_FFN = N13 + NW2
UNITS_A = 8 + 1 + 8 + 8 + 8
UNITS_B = 16 + 8 + 8
U_F0 = 0
U_A = U_F0 + UNITS_FFN
U_F1 = U_A + UNITS_A
U_F2 = U_F1 + UNITS_FFN
U_B = U_F2 + UNITS_FFN
U_F3 = U_B + UNITS_B
U_FFN = (U_F0, U_F1, U_F2, U_F3)




def more_uses(before, *uses):
    return tuple(b + u for b, u in zip(before, uses))


T_F0 = (0, 0, 0, 0)
T_A = more_uses(T_F0, *[N13 // 4] * 4)
T_A_OUT = more_uses(T_A, 10, 10, 10, 10)
T_F1 = more_uses(T_A_OUT, 2, 2, 3, 3)
T_F2 = more_uses(T_F1, *[N13 // 4] * 4)
T_B = more_uses(T_F2, *[N13 // 4] * 4)
T_B_OUT = more_uses(T_B, 10, 10, 18, 18)
T_F3 = more_uses(T_B_OUT, 2, 2, 3, 3)
T_FFN = (T_F0, T_F1, T_F2, T_F3)
O_F0 = (0, 0)
O_A = more_uses(O_F0, 5, 4)
O_A_OUT = more_uses(O_A, HEADS, HEADS)
O_F1 = more_uses(O_A_OUT, 1, 1)
O_F2 = more_uses(O_F1, 5, 4)
O_B = more_uses(O_F2, 5, 4)
O_B_OUT = more_uses(O_B, 2 * HEADS, 2 * HEADS)
O_F3 = more_uses(O_B_OUT, 1, 1)
O_FFN = (O_F0, O_F1, O_F2, O_F3)
N_FFN = (0, 2, 3, 5)
SQUARES = (KT + 1, KT + 4, KT + 1, KT + 1, KT + 4, KT + 1)
SQ_BASE = tuple(sum(SQUARES[:r]) for r in range(SUBS))
ADD_BASE = tuple(SQ_BASE[r] + r for r in range(SUBS))
Q_F0 = 0
Q_A = Q_F0 + 2 * KT
Q_A_OUT = Q_A + 2 * KT
Q_F1 = Q_A_OUT + KT
Q_F2 = Q_F1 + 2 * KT
Q_B = Q_F2 + 2 * KT
Q_B_OUT = Q_B + 2 * KT
Q_F3 = Q_B_OUT + KT
Q_RESULT = Q_F3 + 2 * KT
Q_IN = (Q_F0, Q_A, Q_F1, Q_F2, Q_B, Q_F3, Q_RESULT)
HALVES = tuple(SQ_BASE[r] - KT * r for r in range(SUBS))
QK_TILE = tuple(8 * (r % 4 // 2) + 2 * (r // 4) + r % 2 for r in range(16))
H2 = S // 2
LATE_FFN = 6
LATE_MIXER = (0,1,3,5)

SLICES = 9 * LAYERS
EARLY = 2
ADA_F0 = 8
ADA_F1 = SLICES - EARLY - ADA_F0

COLS = {}
_n = 0
for _name, _w in (("ada_b", SLICES * KT), ("norm_g", SUBS * KT), ("final_g", KT),
                  ("conv_w", TAPS * 8), ("conv_b", 8), ("a_norm_g", 8), ("b_norm_g", 2), ("lam", 4)):
    COLS[_name] = _n
    _n += _w
N_COLS = _n

TWO_PI = 2.0 * math.pi


def two_pi_parts(step):
    rest, parts = step * TWO_PI, []
    for _ in range(4):
        scale = 2.0 ** (10 - math.floor(math.log2(rest)))
        part = math.floor(rest * scale) / scale
        parts.append(part)
        rest -= part
    return parts


def build_trunk(nc, xT, c_row, cols, gate_bias, rope_rows, positions, ada, w13, w2, wa, wb, out):
    ctx = ExitStack()
    with ctx:
        def sem(name):
            return ctx.enter_context(nc.semaphore(name))

        top = [(nc.sbuf_base + 63) // 64 * 64]

        def at(name, shape, dt, offset):
            return nc.alloc_sbuf_tensor_at(name, shape, dt, offset=offset)

        def place(name, shape, dt=F32):
            offset = top[0]
            top[0] += (int(np.prod(shape[1:])) * 4 + 31) // 32 * 32
            return at(name, shape, dt, offset)

        x = place("x", [P, KT, S])
        h_hi = place("h_hi", [P, KT, S], F32R)
        h_lo = place("h_lo", [P, KT, S], F32R)
        raw = [place(f"raw{i}", [P, 1024]) for i in range(RAWS)]
        w_hi = [place(f"w_hi{i}", [P, 1024], F32R) for i in range(SLOTS)]
        w_lo = [place(f"w_lo{i}", [P, 1024], F32R) for i in range(SLOTS)]
        buf = [place(f"buf{i}", [P, S]) for i in range(2)]
        sq = place("sq", [P, S])
        sumsq = place("sumsq", [P, S])
        rstd = place("rstd", [P, S])
        ada_region = top[0]
        ada_raw = [place(f"ada_raw{i}", [P, 1024]) for i in range(2)]
        cond = place("cond", [P, D])
        region = top[0]
        g_hi = place("g_hi", [P, FT, S], F32R)
        g_lo = place("g_lo", [P, FT, S], F32R)
        region_end = top[0]
        col = place("col", [P, N_COLS])
        ada_v = place("ada_v", [P, SLICES, KT])
        ada_sum = place("ada_sum", [P, KT])
        scale_col = place("scale_col", [P, KT])
        gate_col = place("gate_col", [P, KT])
        ones = place("ones", [P, P])
        ident = place("ident", [P, P])
        mask_st = place("mask_st", [P, P])
        mask_ts = place("mask_ts", [P, P])
        select = place("select", [HEADS, HEADS, P])
        eps = place("eps", [P, 1])
        std_col = place("std_col", [P, ST])
        inv_col = place("inv_col", [P, ST])
        head_std = place("head_std", [P, HEADS * ST])
        head_inv = place("head_inv", [P, HEADS * ST])
        ag_col = place("ag_col", [P, 8])
        rows_one = place("rows_one", [HEADS, S])
        gbias = place("gbias", [HEADS, 2])
        rope_row = place("rope_row", [ROPE_DIM, 2])
        lam_mul = place("lam_mul", [P, 2])
        lam_exp = place("lam_exp", [P, 2])
        neg_lam = place("neg_lam", [P, 1])
        u_col = place("u_col", [P, ST * HEADS])
        neg_max = place("neg_max", [P, 2, 2])
        row_max = place("row_max", [P, 2, 2])
        row_sum = place("row_sum", [P, 2, 2])
        row_inv = place("row_inv", [P, 2, 2])
        bg_col = place("bg_col", [P, 2])
        assert top[0] <= nc.sbuf_usable_end, (top[0], nc.sbuf_usable_end)

        def carve(parts, start, end):
            made = []
            for name, shape in parts:
                made.append(at(name, shape, F32, start))
                start += int(np.prod(shape[1:])) * 4
            assert start <= end, (parts, start - end)
            return made

        early_ada, x_sq = carve(
            [("early_ada", [P, EARLY * KT, 1024]), ("x_sq", [P, KT, S])],
            region, region_end)
        a_qk, a_v, a_o, a_h, neg_m, exp_m = carve(
            [("a_qk", [P, 8, S]), ("a_v", [P, ST, 1024]), ("a_o", [P, 8, S]), ("a_h", [P, 8, S]),
             ("neg_m", [P, HEADS, S]), ("exp_m", [P, HEADS, S])], region, region_end)
        rows = at("rows", [HEADS, 8, S], F32, region + 3 * 16384)
        WT_OFF = (0, 512, 896, 1152)
        a_wt = carve([("a_wt0", [P, 1280]), ("a_wt1", [P, 1280])], ada_region, region)
        b_qk, b_v, b_o, b_at0, b_at1, b_cos, b_sin, b_rot, b_tmp = carve(
            [("b_qk", [P, 16, S]), ("b_v", [P, ST, 1024]), ("b_o", [P, 8, S]),
             ("b_at0", [P, ST, S]), ("b_at1", [P, ST, S]),
             ("b_cos", [ROPE_DIM, S]), ("b_sin", [ROPE_DIM, S]), ("b_rot", [ROPE_DIM, S]),
             ("b_tmp", [ROPE_DIM, S])], region, region_end)
        b_at = (b_at0, b_at1)
        b_p = carve([("b_p0", [P, 2, S]), ("b_p1", [P, 2, S])], ada_region, region)
        pos_i = at("pos_i", [ROPE_DIM, S], I32, ada_region + 8192)

        acc = ctx.enter_context(nc.psum_tensor("acc", [P, 4, S], F32))
        outp = ctx.enter_context(nc.psum_tensor("outp", [P, 2, S], F32))
        stat = ctx.enter_context(nc.psum_tensor("stat", [P, S], F32))
        aux = ctx.enter_context(nc.psum_tensor("aux", [P, S], F32))

        raw_loaded = [sem(f"raw_loaded{i}") for i in range(RAWS)]
        hi_ready = sem("hi_ready")
        lo_ready = sem("lo_ready")
        unit_done = sem("unit_done")
        half_done = sem("half_done")
        acc_free = [sem(f"acc_free{i}") for i in range(4)]
        out_free = [sem(f"out_free{i}") for i in range(2)]
        sq_done = sem("sq_done")
        sq_added = sem("sq_added")
        stat_done = sem("stat_done")
        std_ready = sem("std_ready")
        rstd_ready = sem("rstd_ready")
        rstd_spread = sem("rstd_spread")
        scale_ready = sem("scale_ready")
        gate_ready = sem("gate_ready")
        src_ready = sem("src_ready")
        act_hi_ready = sem("act_hi_ready")
        act_lo_ready = sem("act_lo_ready")
        g_hi_ready = sem("g_hi_ready")
        g_lo_ready = sem("g_lo_ready")
        early_loaded = [sem(f"early_loaded{i}") for i in range(EARLY * KT // 2)]
        ada_loaded = [sem(f"ada_loaded{i}") for i in range(2)]
        ada_used = sem("ada_used")
        early_used = sem("early_used")
        x_sq_added = sem("x_sq_added")
        ada_ready = sem("ada_ready")
        c_loaded = sem("c_loaded")
        col_loaded = sem("col_loaded")
        small_loaded = sem("small_loaded")
        pos_loaded = sem("pos_loaded")
        x_loaded = sem("x_loaded")
        cond_ready = sem("cond_ready")
        pool_consts = sem("pool_consts")
        lam_mul_ready = sem("lam_mul_ready")
        lam_sum_done = sem("lam_sum_done")
        lam_exp_ready = sem("lam_exp_ready")
        lam_ready = sem("lam_ready")
        a_qk_ready = sem("a_qk_ready")
        f_arg_ready = sem("f_arg_ready")
        f_log_ready = sem("f_log_ready")
        m_rows_ready = sem("m_rows_ready")
        em_row_ready = sem("em_row_ready")
        u_turned = sem("u_turned")
        u_col_ready = sem("u_col_ready")
        spread_done = sem("spread_done")
        diag_ready = sem("diag_ready")
        decay_ready = sem("decay_ready")
        st_done = sem("st_done")
        av_done = sem("av_done")
        den_read = sem("den_read")
        a_o_ready = sem("a_o_ready")
        gated_ready = sem("gated_ready")
        a_sq_ready = sem("a_sq_ready")
        a_pair_ready = sem("a_pair_ready")
        a_ss_done = sem("a_ss_done")
        a_std_ready = sem("a_std_ready")
        a_inv_ready = sem("a_inv_ready")
        a_inv_spread = sem("a_inv_spread")
        a_factor_ready = sem("a_factor_ready")
        trig_arg = sem("trig_arg")
        trig_ready = sem("trig_ready")
        rope_done = sem("rope_done")
        s_done = sem("s_done")
        max_ready = sem("max_ready")
        p_ready = sem("p_ready")
        turned = sem("turned")
        pv_done = sem("pv_done")
        b_o_ready = sem("b_o_ready")
        v_part_done = sem("v_part_done")
        b_sq_ready = sem("b_sq_ready")
        b_pair_ready = sem("b_pair_ready")
        b_ss_done = sem("b_ss_done")
        b_std_ready = sem("b_std_ready")
        b_inv_ready = sem("b_inv_ready")
        b_inv_spread = sem("b_inv_spread")
        b_factor_ready = sem("b_factor_ready")
        stored = sem("stored")
        dve_step = sem("dve_step")
        act_step = sem("act_step")
        pool_step = sem("pool_step")

        def read_out(eng, T, n):
            eng.wait_ge(acc_free[n % 4], T[n % 4] + n // 4 + 1)

        def tok(half):
            return slice(half * H2, (half + 1) * H2)

        def head_bank(h, d):
            return outp[:, d, :] if h == HEADS - 1 else (stat, aux)[d][:, :]

        def rstd_bank(half):
            return aux[:, 0:H2] if half == 0 else stat[:, H2:S]

        block = ctx.enter_context(nc.Block())

        @block.sync
        def _(sp):
            def load_unit(u, src, n=1024):
                base, more = u
                if base >= RAWS:
                    sp.wait_ge(lo_ready, base + more - RAWS + 1)
                sp.dma_start(raw[base % RAWS][:, 0:n], src).then_inc(raw_loaded[base % RAWS], 16)

            def load_ada(sl, first, more=0):
                for k in range(first, first + 4):
                    a = (sl - EARLY) * KT + k
                    if a >= 2:
                        sp.wait_ge(ada_used, a + more * KT - 1)
                    sp.dma_start(ada_raw[k % 2][:, :], ada[EARLY * KT + a + more * KT])\
                      .then_inc(ada_loaded[k % 2], 16)

            def ffn(p, ada_first, ada_steps):
                U = U_FFN[p]
                last = FT // 2 - 1

                def load13(n, more=0):
                    load_unit((U + n, 4 * more), w13[p * N13 + n + 4 * more])

                def load2(m, o):
                    n, k0 = W2_SPLIT[m] * P, W2_START[m] * P
                    load_unit((U + N13 + m, 4 * o), w2[p * KT + o][:, k0:k0 + n], n)

                def step(i, more, with_ada):
                    for j in range(2):
                        load13(4 * i + 4 + 2 * j, more)
                        load13(4 * i + 5 + 2 * j, more)
                        if with_ada:
                            load_ada(ada_first + i, 4 * j, more)

                for n in range(4):
                    load13(n)
                if ada_steps:
                    step(0, 0, True)
                    with sp.Fori(0, ada_steps - 1) as i:
                        step(1, i, True)
                with sp.Fori(0, last - ada_steps) as i:
                    step(ada_steps, i, False)
                with sp.Fori(0, KT) as o:
                    for m in range(4):
                        load2(m, o)

            for c in range(EARLY * KT // 2):
                sp.dma_start(early_ada[:, 2 * c:2 * c + 2, :],
                             ada[2 * c:2 * c + 2].rearrange("u p n -> p u n")).then_inc(early_loaded[c], 16)
            ffn(0, EARLY, ADA_F0)
            with sp.Fori(0, (UNITS_A - 1) // 4) as i:
                for k in range(4):
                    load_unit((U_A + k, 4 * i), wa[4 * i + k])
            load_unit((U_A + UNITS_A - 1, 0), wa[UNITS_A - 1])
            sp.wait_ge(av_done, HEADS)
            sp.dma_start(cond[:, :], c_row.broadcast_to([P, D])).then_inc(c_loaded, 16)
            ffn(1, EARLY + ADA_F0, ADA_F1)
            ffn(2, 0, 0)
            sp.wait_ge(ada_ready, SLICES)
            sp.dma_start(pos_i[:, :], positions.broadcast_to([ROPE_DIM, S])).then_inc(pos_loaded, 16)
            with sp.Fori(0, UNITS_B // 4) as i:
                for k in range(4):
                    load_unit((U_B + k, 4 * i), wb[4 * i + k])
            ffn(3, 0, 0)
            for half in range(2):
                for k in (0, 4):
                    sp.wait_ge(src_ready, Q_IN[SUBS] + 8 * half + k + 4)
                    sp.dma_start(out[k:k + 4, :, tok(half)].rearrange("k p s -> p k s"),
                                 x[:, k:k + 4, tok(half)]).then_inc(stored, 16)
            sp.wait_ge(stored, 16 * 4)

        @block.gpsimd
        def _(pool):
            pool.memset(ident[:, :], 0.0).then_inc(pool_step, 1)
            pool.memset(mask_st[:, :], 0.0).then_inc(pool_step, 1)
            pool.memset(mask_ts[:, :], 0.0).then_inc(pool_step, 1)
            pool.memset(select[:, :, :], 0.0).then_inc(pool_step, 1)
            pool.memset(ones[:, :], 1.0).then_inc(pool_consts, 1)
            pool.memset(eps[:, :], EPS).then_inc(pool_consts, 1)
            pool.wait_ge(pool_step, 4)
            pool.affine_select(out=ident[:, :], in_=ident[:, :], compare_op=ALU.not_equal, fill=1.0,
                               base=0, pattern=[[-1, P]], channel_multiplier=1).then_inc(pool_consts, 1)
            pool.affine_select(out=mask_st[:, :], in_=mask_st[:, :], compare_op=ALU.is_ge, fill=MASKED,
                               base=0, pattern=[[1, P]], channel_multiplier=-1).then_inc(pool_consts, 1)
            pool.affine_select(out=mask_ts[:, :], in_=mask_ts[:, :], compare_op=ALU.is_ge, fill=MASKED,
                               base=0, pattern=[[-1, P]], channel_multiplier=1).then_inc(pool_consts, 1)
            pool.affine_select(out=select[:, :, :], in_=select[:, :, :], compare_op=ALU.not_equal, fill=1.0,
                               base=0, pattern=[[-1, HEADS], [0, P]], channel_multiplier=1)\
                .then_inc(pool_consts, 1)

            def low_part(base, more, n=1024):
                pool.wait_ge(hi_ready, base + more + 1)
                s = base % SLOTS
                pool.tensor_tensor(w_lo[s][:, 0:n], raw[base % RAWS][:, 0:n],
                                   w_hi[s][:, 0:n].bitcast(F32), ALU.subtract).then_inc(lo_ready, 1)

            def group_loop(U, n):
                with pool.Fori(0, n) as i:
                    for k in range(4):
                        low_part(U + k, 4 * i)

            def ffn(p):
                group_loop(U_FFN[p], N13 // 4)
                with pool.Fori(0, KT) as o:
                    for m in range(4):
                        low_part(U_FFN[p] + N13 + m, 4 * o, W2_SPLIT[m] * P)

            pool.wait_ge(sq_done, 2)
            pool.tensor_tensor(sumsq[:, :], x_sq[:, 0, :], x_sq[:, 1, :], ALU.add).then_inc(x_sq_added, 1)
            for k in range(2, KT):
                pool.wait_ge(sq_done, k + 1)
                pool.wait_ge(x_sq_added, k - 1)
                pool.tensor_tensor(sumsq[:, :], sumsq[:, :], x_sq[:, k, :], ALU.add).then_inc(x_sq_added, 1)
            ffn(0)
            group_loop(U_A, (UNITS_A - 1) // 4)
            low_part(U_A + UNITS_A - 1, 0)
            ffn(1)
            ffn(2)
            group_loop(U_B, UNITS_B // 4)
            ffn(3)

        @block.tensor
        def _(pe):
            def three(bank, a_hi, a_lo, b_hi, b_lo, start, stop):
                pe.matmul(bank, a_hi, b_hi, start=start, stop=False)
                pe.matmul(bank, a_hi, b_lo, start=False, stop=False)
                return pe.matmul(bank, a_lo, b_hi, start=False, stop=stop)

            def block_of(s, n):
                return w_hi[s][:, n * P:(n + 1) * P], w_lo[s][:, n * P:(n + 1) * P]

            def take_acc(T, n):
                if T[n % 4] + n // 4:
                    pe.wait_ge(acc_free[n % 4], T[n % 4] + n // 4)

            def unit(base, more, bank):
                pe.wait_ge(lo_ready, base + more + 1)
                for k in range(KT):
                    last = three(bank, *block_of(base % SLOTS, k), h_hi[:, k, :], h_lo[:, k, :],
                                 k == 0, k == KT - 1)
                last.then_inc(unit_done, 1)

            def first_group(U, T, n):
                for half in range(2):
                    t = tok(half)
                    for pair in range(2):
                        for k in range(KT):
                            if pair == 0:
                                pe.wait_ge(act_lo_ready, Q_IN[n] + 8 * half + k + 1)
                            for s in (2 * pair, 2 * pair + 1):
                                if half == 0 and k == 0:
                                    pe.wait_ge(lo_ready, U + s + 1)
                                    take_acc(T, s)
                                last = three(acc[:, s, t], *block_of((U + s) % SLOTS, k),
                                             h_hi[:, k, t], h_lo[:, k, t], k == 0, k == KT - 1)
                                if half == 1 and k == KT - 1:
                                    last.then_inc(unit_done, 1)
                            if half == 0 and pair == 1 and k == KT // 2 - 1:
                                spread_rstd(n, 1)
                        if half == 0 and pair == 0 and n:
                            norm_sum(n, 1)

            def out_first_group(U, T, q, before):
                for s, k in [(s, k) for k in range(KT - 2) for s in range(4)] + \
                            [(s, k) for s in range(4) for k in range(KT - 2, KT)]:
                    if s == 0:
                        if k in before:
                            before[k]()
                        pe.wait_ge(act_lo_ready, q + k + 1)
                    if k == 0:
                        pe.wait_ge(lo_ready, U + s + 1)
                        take_acc(T, s)
                    last = three(acc[:, s, :], *block_of((U + s) % SLOTS, k),
                                 h_hi[:, k, :], h_lo[:, k, :], k == 0, k == KT - 1)
                    if k == KT - 1:
                        last.then_inc(unit_done, 1)

            def v_half(U, T, first):
                for m in range(4):
                    u = U + m
                    s = u % SLOTS
                    pe.wait_ge(lo_ready, u + 1)
                    for tt in range(ST):
                        if m == 0:
                            take_acc(T, first + tt)
                        for k in (2 * m, 2 * m + 1):
                            last = v_product(acc[:, tt, :], tt, k, s)
                    last.then_inc(unit_done, 1)

            def v_product(bank, tt, k, s):
                t, n = slice(tt * P, tt * P + P), k % 2 * 512
                return three(bank, h_hi[:, k, t], h_lo[:, k, t], w_hi[s][:, n:n + 512],
                             w_lo[s][:, n:n + 512], k == 0, k == KT - 1)

            def norm_sum(n, half):
                r = n - 1
                if r >= 0:
                    pe.wait_ge(sq_added, ADD_BASE[r] + 1 + (KT if half == 0 else SQUARES[r]))
                else:
                    pe.wait_ge(x_sq_added, KT - 1)
                for j in (2 * half, 2 * half + 1):
                    last = pe.matmul(stat[:, j:j + 1], sumsq[:, j * P:(j + 1) * P], ones[:, 0:1],
                                     start=True, stop=True)
                last.then_inc(stat_done, 1)

            def spread_rstd(n, half):
                pe.wait_ge(rstd_ready, 2 * n + half + 1)
                pe.matmul(rstd_bank(half), ones[:, :], rstd[:, tok(half)], start=True, stop=True)\
                  .then_inc(rstd_spread, 1)

            def ffn(p):
                U, T, W = U_FFN[p], T_FFN[p], U_FFN[p] + N13
                first_group(U, T, N_FFN[p])

                with pe.Fori(0, FT // 2 - 1) as i:
                    for k in range(4):
                        pe.wait_ge(acc_free[k], T[k] + 1 + i)
                        unit(U + 4 + k, 4 * i, acc[:, k, :])

                def out_tile(j, bank, t, use, more=0, hold=False, between=lambda m: None):
                    pe.wait_ge(out_free[bank], O_FFN[p][bank] + 1 + use + more)
                    for m in range(4):
                        base = W + 4 * j + m
                        pe.wait_ge(lo_ready, base + 1 + 8 * more)
                        pe.wait_ge(g_lo_ready, FT * p + W2_START[m] + W2_SPLIT[m])
                        for b in range(W2_SPLIT[m]):
                            kt = W2_START[m] + b
                            last = three(outp[:, bank, t], *block_of(base % SLOTS, b),
                                         g_hi[:, kt, t], g_lo[:, kt, t], kt == 0, kt == FT - 1)
                        if not hold:
                            last.then_inc(unit_done, 1)
                        elif m == 3:
                            last.then_inc(half_done, 1)
                        between(m)

                whole = slice(0, S)
                with pe.Fori(0, KT // 2 - 1) as i:
                    out_tile(0, 0, whole, 0, i)
                    out_tile(1, 1, whole, 0, i)
                out_tile(KT - 2, 0, whole, KT // 2 - 1)
                out_tile(KT - 1, 1, tok(0), KT // 2 - 1, hold=True)
                n = N_FFN[p] + 1

                def norm_first_half(m):
                    if m == 0:
                        norm_sum(n, 0)
                    if m == 1:
                        spread_rstd(n, 0)
                out_tile(KT - 1, 0, tok(1), KT // 2, between=norm_first_half)
                if p == 3:
                    norm_sum(n, 1)
                    spread_rstd(n, 1)

            def out_projection(U, T, O, q, n, before):
                out_first_group(U, T, q, before)
                for half in range(2):
                    t = tok(half)
                    for s in range(4, 8):
                        if half and s < 6:
                            pe.wait_ge(out_free[s - 4], O[s - 4] + 1)
                            bank = outp[:, s - 4, t]
                        else:
                            take_acc(T, s + 4 * half)
                            bank = acc[:, s % 4, t]
                        pe.wait_ge(lo_ready, U + s + 1)
                        for k in range(KT):
                            last = three(bank, *block_of((U + s) % SLOTS, k),
                                         h_hi[:, k, t], h_lo[:, k, t], k == 0, k == KT - 1)
                        last.then_inc(unit_done if half else half_done, 1)
                        if half and s == 4:
                            norm_sum(n, 0)
                        if half and s == 5:
                            spread_rstd(n, 0)

            def mixer_a():
                U, T = U_A, T_A
                first_group(U, T, 1)
                for s in range(4, 8):
                    take_acc(T, s)
                    unit(U + s, 0, acc[:, s % 4, :])
                unit(U + 8, 0, aux[:, :])
                v_half(U + 9, T, 8)
                v_half(U + 13, T, 12)

                def o_tile(t):
                    if t == 0:
                        pe.wait_ge(u_col_ready, 1)
                    else:
                        pe.wait_ge(a_o_ready, t)
                    unit(U + 17 + t, 0, stat[:, :])

                def spread_row(row, first):
                    for h in range(HEADS):
                        take_acc(T, first + h)
                        pe.matmul(acc[:, h, :], select[:, h, :], rows[:, row, :], start=True, stop=True)\
                          .then_inc(spread_done, 1)

                def scores(h):
                    for j in range(ST):
                        take_acc(T, 24 + 4 * h + j)
                        pe.matmul(acc[:, j, 0:S - j * P], a_qk[:, 4 + h, j * P:(j + 1) * P],
                                  a_qk[:, h, j * P:S], start=True, stop=True).then_inc(st_done, 1)

                def mix(h):
                    pe.wait_ge(out_free[0], O_A[0] + h + 1)
                    pe.wait_ge(out_free[1], O_A[1] + h + 1)
                    if h:
                        pe.wait_ge(den_read, h)
                    for j in range(ST):
                        read_out(pe, T, 24 + 4 * h + j)
                        w = a_wt[h % 2][:, WT_OFF[j]:WT_OFF[j] + S - j * P]
                        pe.matmul(aux[:, j * P:S], ones[:, :], w, start=j == 0, stop=j == ST - 1)
                        for d in range(2):
                            c0 = h * DV + d * P
                            last = pe.matmul(outp[:, d, j * P:S], a_v[:, j, c0:c0 + P], w,
                                             start=j == 0, stop=j == ST - 1)
                    last.then_inc(av_done, 1)

                def head_sum(h, bank):
                    pe.wait_ge(a_pair_ready, h + 1)
                    for j in range(ST):
                        last = pe.matmul(bank[:, ST * h + j:ST * h + j + 1],
                                         a_qk[:, h, j * P:(j + 1) * P], ones[:, 0:1], start=True, stop=True)
                    last.then_inc(a_ss_done, 1)

                def spread_inverse(h, bank):
                    pe.wait_ge(a_inv_ready, h + 1)
                    pe.matmul(bank, ones[:, :], neg_m[:, h, :], start=True, stop=True)\
                      .then_inc(a_inv_spread, 1)

                pe.wait_ge(m_rows_ready, 1)
                for j in range(ST):
                    last = pe.transpose(stat[:, 4 * j:4 * j + 4], rows[:, 2, j * P:(j + 1) * P],
                                        ident[0:HEADS, 0:HEADS])
                last.then_inc(u_turned, 1)
                spread_row(4, 16)
                o_tile(0)
                pe.wait_ge(em_row_ready, 1)
                spread_row(6, 20)
                pe.wait_ge(a_qk_ready, 8)
                scores(0)
                o_tile(1)
                scores(1)
                mix(0)
                o_tile(2)
                scores(2)
                o_tile(3)
                mix(1)
                o_tile(4)
                scores(3)
                o_tile(5)
                mix(2)
                o_tile(6)
                take_acc(T, 40 + 2)
                head_sum(0, acc[:, 2, :])
                head_sum(1, acc[:, 2, :])
                o_tile(7)
                for h in range(2):
                    take_acc(T, 40 + h)
                    spread_inverse(h, acc[:, h, :])
                pe.wait_ge(a_std_ready, 2)
                head_sum(2, acc[:, 2, :])
                mix(3)
                take_acc(T, 40 + 3)
                spread_inverse(2, acc[:, 3, :])
                pe.wait_ge(a_factor_ready, 3)
                pe.wait_ge(a_std_ready, 3)
                out_projection(U + 25, T_A_OUT, O_A_OUT, Q_A_OUT, 2,
                               {3: lambda: head_sum(3, aux), 4: lambda: spread_inverse(3, aux[:, :])})

            def mixer_b():
                U, T = U_B, T_B
                first_group(U, T, 4)
                v_half(U + 4, T, 4)

                def chunk(c):
                    bank = acc[:, c % 2, :]
                    take_acc(T, 4 * (2 + c // 2) + c % 2)
                    if c < 12:
                        unit(U + 8 + c, 0, bank)
                        return
                    for k in range(KT):
                        u = U + 20 + k // 2
                        pe.wait_ge(lo_ready, u + 1)
                        last = v_product(bank, c - 12, k, u % SLOTS)
                        if c == 15 and k % 2:
                            last.then_inc(unit_done, 1)
                    if c < 15:
                        last.then_inc(v_part_done, 1)

                def scores(n):
                    h, i = divmod(n, ST)
                    if i == 0:
                        pe.wait_ge(rope_done, 4 * h + 4)
                    for c in range(2):
                        take_acc(T, 4 * (2 + n) + 2 + c)
                        pe.matmul(acc[:, 2 + c, 0:(i + 1) * P], b_qk[:, 2 * h + c, i * P:(i + 1) * P],
                                  b_qk[:, 8 + 2 * h + c, 0:(i + 1) * P], start=True, stop=True)\
                          .then_inc(s_done, 1)

                def turn(n):
                    h, i = divmod(n, ST)
                    pe.wait_ge(p_ready, n + 1)
                    pe.wait_ge(out_free[n % 2], O_B[n % 2] + n // 2 + 1)
                    for j in range(i + 1):
                        last = pe.transpose(outp[:, n % 2, j * P:(j + 1) * P],
                                            b_p[n % 2][:, 0, j * P:(j + 1) * P], ident[:, :])
                    last.then_inc(turned, 1)

                def mix(h):
                    for j in range(2):
                        pe.wait_ge(out_free[j], O_B[j] + 1 + 2 * h + 2)
                    if h % 2 == 0:
                        for tt in range(ST):
                            read_out(pe, T, 4 + tt if h == 0 else 4 * (8 + tt // 2) + tt % 2)
                    if 1 <= h <= 2:
                        pe.wait_ge(b_o_ready, h)
                        pe.wait_ge(b_std_ready, h)
                        pe.wait_ge(b_factor_ready, h)
                    for d in range(2):
                        bank = head_bank(h, d)
                        c0 = h * DV + d * P
                        for j in range(ST):
                            last = pe.matmul(bank[:, j * P:S], b_v[:, j, c0:c0 + P],
                                             b_at[h % 2][:, j, j * P:S], start=j == 0, stop=j == ST - 1)
                    last.then_inc(pv_done, 1)

                def head_sum(h):
                    pe.wait_ge(b_pair_ready, h + 1)
                    for j in range(ST):
                        last = pe.matmul(stat[:, ST * h + j:ST * h + j + 1],
                                         b_qk[:, 2 * h, j * P:(j + 1) * P], ones[:, 0:1], start=True, stop=True)
                    last.then_inc(b_ss_done, 1)

                def spread_inverse(h):
                    pe.wait_ge(b_inv_ready, h + 1)
                    if h:
                        pe.wait_ge(b_factor_ready, h)
                    pe.matmul(aux[:, :], ones[:, :], b_qk[:, 8 + 2 * h, :], start=True, stop=True)\
                      .then_inc(b_inv_spread, 1)

                chunk(0)
                for n in range(4 * HEADS):
                    scores(n)
                    if n + 1 < 4 * HEADS:
                        chunk(n + 1)
                    if n >= 1:
                        turn(n - 1)
                    if n in (5, 9):
                        mix(n // 4 - 1)
                    if n in (7, 11):
                        head_sum(n // 4 - 1)
                    if n in (8, 12):
                        spread_inverse(n // 4 - 2)
                mix(2)
                turn(15)
                mix(3)
                head_sum(2)

                def before_two():
                    spread_inverse(2)
                    head_sum(3)

                out_projection(U + 24, T_B_OUT, O_B_OUT, Q_B_OUT, 5, {2: before_two, 4: lambda: spread_inverse(3)})

            pe.wait_ge(pool_consts, 6)
            pe.wait_ge(lam_mul_ready, 1)
            pe.matmul(aux[:, 0:2], ones[:, :], lam_mul[:, :], start=True, stop=True).then_inc(lam_sum_done, 1)
            pe.wait_ge(lam_exp_ready, 1)
            norm_sum(0, 0)
            norm_sum(0, 1)
            spread_rstd(0, 0)
            ffn(0)
            mixer_a()
            ffn(1)
            ffn(2)
            mixer_b()
            ffn(3)

        @block.scalar
        def _(act):
            def high_part(base, more=0, n=1024):
                act.wait_ge(raw_loaded[base % RAWS], 16 * (base // RAWS + 1) + (16 // RAWS) * more)
                if base >= SLOTS:
                    act.wait_ge(unit_done, base + more - SLOTS + 1)
                act.activation(w_hi[base % SLOTS][:, 0:n], raw[base % RAWS][:, 0:n], ACT.Copy)\
                   .then_inc(hi_ready, 1)

            def split_high(q, k, t=slice(0, S), bias=None):
                act.wait_ge(src_ready, q + 1)
                if bias is None:
                    ins = act.activation(h_hi[:, k, t], buf[k % 2][:, t], ACT.Copy)
                else:
                    ins = act.activation(h_hi[:, k, t], buf[k % 2][:, t], ACT.Identity,
                                         bias=bias[:, k:k + 1])
                ins.then_inc(act_hi_ready, 1)

            def root(n, half):
                act.wait_ge(stat_done, 2 * n + half + 1 if n else 2)
                act.activation(std_col[:, 2 * half:2 * half + 2], stat[:, 2 * half:2 * half + 2], ACT.Sqrt,
                               bias=eps[:, 0:1], scale=1.0 / D).then_inc(std_ready, 1)

            def norm(n, U, between):
                root(n, 0)
                if n == 0:
                    root(n, 1)
                high_part(U)
                act.wait_ge(ada_ready, 3 * n + 1)
                for k in range(KT):
                    if k in between:
                        between[k]()
                    if k == 0:
                        high_part(U + 1)
                    split_high(Q_IN[n] + k, k, tok(0), ada_v[:, 3 * n, :])
                    if k in (4, 6):
                        high_part(U + k // 2)
                if n:
                    root(n, 1)
                for k in range(KT):
                    split_high(Q_IN[n] + KT + k, k, tok(1), ada_v[:, 3 * n, :])

            def square(r, i, xs, t=slice(0, S), more=0):
                act.wait_ge(sq_added, ADD_BASE[r] + i + 1 + more)
                act.activation(sq[:, t], xs, ACT.Square).then_inc(sq_done, 1)

            def ffn(p):
                U, T, r = U_FFN[p], T_FFN[p], N_FFN[p]

                def step(i, more):
                    for j in range(2):
                        u, f = U + 4 * i + 2 * j, 2 * i + j
                        F = FT * p + f
                        act.wait_ge(unit_done, u + 1 + 4 * more)
                        if F >= 2:
                            act.wait_ge(g_lo_ready, F - 1 + 2 * more)
                        act.activation(buf[j][:, :], acc[:, 2 * j, :], ACT.Silu)\
                           .then_inc(acc_free[2 * j], 1)
                        high_part(u + 4, 4 * more)
                        act.wait_ge(acc_free[2 * j + 1], T[2 * j + 1] + i + 1 + more)
                        dst = g_hi[:, f, :] if isinstance(more, int) else \
                            g_hi[:, bass.ds(2 * more + f, 1), :].rearrange("p a s -> p (a s)")
                        act.activation(dst, buf[j][:, :], ACT.Copy).then_inc(g_hi_ready, 1)
                        high_part(u + 5, 4 * more)

                if p == 1:
                    act.wait_ge(c_loaded, 32)
                    act.activation(cond[:, :], cond[:, :], ACT.Silu).then_inc(cond_ready, 1)
                step(0, 0)
                with act.Fori(0, FT // 2 - 1) as i:
                    step(1, i)
                W = U + N13

                act.preload_act_table(ACT.Sqrt)

                def out_tile(o, more=0):
                    for m in range(4):
                        high_part(W + 4 * (o + 1) + m, 8 * more, W2_SPLIT[m] * P)
                    act.wait_ge(out_free[o % 2], O_FFN[p][o % 2] + 1 + o // 2 + 1 + more)
                    xs = x[:, o, :] if isinstance(more, int) else \
                        x[:, bass.ds(2 * more + o, 1), :].rearrange("p a s -> p (a s)")
                    square(r, o, xs, more=2 * more)

                def last_tile(half):
                    bank = 1 - half
                    act.wait_ge(out_free[bank], O_FFN[p][bank] + 1 + KT // 2 + half)
                    square(r, KT - 1 + half, x[:, KT - 1, tok(half)], tok(half))

                with act.Fori(0, KT // 2 - 1) as i:
                    out_tile(0, i)
                    out_tile(1, i)
                out_tile(KT - 2)
                last_tile(0)
                return {LATE_FFN: lambda: last_tile(1)}

            def out_projection(U, T, O, r):
                for o in range(4):
                    high_part(U + o + 4)
                    read_out(act, T, o)
                    square(r, o, x[:, o, :])

                def last_tile(o, half):
                    if half and o < 6:
                        act.wait_ge(out_free[o - 4], O[o - 4] + 2)
                    else:
                        read_out(act, T, o + 4 * half)
                    square(r, o + 4 * half, x[:, o, tok(half)], tok(half))

                for o in range(4, KT):
                    last_tile(o, 0)
                return {k: lambda o=o: last_tile(o, 1) for k, o in zip(LATE_MIXER, range(4, KT))}

            def mixer_a():
                U, T = U_A, T_A
                for t in range(8):
                    high_part(U + t + 4)
                    read_out(act, T, t)
                    act.activation(a_qk[:, t, :], buf[t % 2][:, :], ACT.Silu).then_inc(a_qk_ready, 1)
                high_part(U + 12)
                act.wait_ge(f_arg_ready, 1)
                act.activation(rows[:, 5, :], rows[:, 3, :], ACT.Exp).then_inc(act_step, 1)
                act.wait_ge(act_step, 1)
                act.activation(rows[:, 6, :], rows[:, 5, :], ACT.Ln, bias=1.0).then_inc(f_log_ready, 1)
                v_evac(U + 9, a_v, 0)
                v_evac(U + 13, a_v, 1)
                act.wait_ge(m_rows_ready, 1)
                act.activation(rows[:, 6, :], rows[:, 5, :], ACT.Exp, scale=-1.0).then_inc(em_row_ready, 1)

                def keep_rows(n, dst):
                    for h in range(HEADS):
                        act.wait_ge(spread_done, 4 * n + h + 1)
                        act.activation(dst[:, h, :], acc[:, h, :], ACT.Copy).then_inc(acc_free[h], 1)

                def o_gate(t):
                    act.wait_ge(unit_done, U + 17 + t + 1)
                    act.activation(a_o[:, t, :], stat[:, :], ACT.Tanh, scale=0.5).then_inc(a_o_ready, 1)

                def decays(h):
                    act.wait_ge(diag_ready, h + 1)
                    if h >= 2:
                        act.wait_ge(av_done, h - 1)
                    for j in range(ST):
                        u = u_col[:, 4 * j + h:4 * j + h + 1]
                        o = WT_OFF[j]
                        ins = act.activation(a_wt[h % 2][:, o:o + P], buf[h % 2][:, j * P:(j + 1) * P],
                                             ACT.Exp, bias=u)
                        if j < ST - 1:
                            ins = act.activation(a_wt[h % 2][:, o + P:o + S - j * P],
                                                 neg_m[:, h, (j + 1) * P:S], ACT.Exp, bias=u)
                    ins.then_inc(decay_ready, 1)

                def head_square(h):
                    for d in range(2):
                        act.wait_ge(out_free[d], O_A[d] + 1 + h + 1)
                    act.activation(a_qk[:, h:h + 5:4, :], a_h[:, 2 * h:2 * h + 2, :], ACT.Square)\
                       .then_inc(a_sq_ready, 1)

                def head_root(h, n, bank):
                    act.wait_ge(a_ss_done, h + n)
                    cs = slice(ST * h, ST * (h + n))
                    act.activation(head_std[:, cs], bank[:, cs], ACT.Sqrt, bias=eps[:, 0:1], scale=1.0 / DV)\
                       .then_inc(a_std_ready, n)

                def keep_factor(h, bank):
                    act.wait_ge(a_inv_spread, h + 1)
                    act.activation(exp_m[:, h, :], bank, ACT.Copy).then_inc(a_factor_ready, 1)

                keep_rows(0, neg_m)
                decays(0)
                o_gate(0)
                high_part(U + 21)
                keep_rows(1, exp_m)
                decays(1)
                o_gate(1)
                high_part(U + 22)
                decays(2)
                o_gate(2)
                high_part(U + 23)
                head_square(0)
                o_gate(3)
                high_part(U + 24)
                decays(3)
                o_gate(4)
                high_part(U + 25)
                head_square(1)
                o_gate(5)
                high_part(U + 26)
                o_gate(6)
                high_part(U + 27)
                head_square(2)
                head_root(0, 2, acc[:, 2, :])
                high_part(U + 28)
                keep_factor(0, acc[:, 0, :])
                keep_factor(1, acc[:, 1, :])
                head_root(2, 1, acc[:, 2, :])
                o_gate(7)
                act.preload_act_table(ACT.Sqrt)
                for k in range(KT):
                    split_high(Q_A_OUT + k, k)
                    if k == 1:
                        keep_factor(2, acc[:, 3, :])
                    if k == 3:
                        head_square(3)
                    if k == 4:
                        head_root(3, 1, aux)
                    if k == 5:
                        keep_factor(3, aux[:, :])
                return out_projection(U + 25, T_A_OUT, O_A_OUT, 1)

            def v_evac(U, dst, half):
                for m in range(4):
                    high_part(U + m + 4)
                act.wait_ge(unit_done, U + 4)
                for tt in range(2):
                    act.activation(dst[:, tt, half * 512:half * 512 + 512], acc[:, tt, :], ACT.Copy)\
                       .then_inc(acc_free[tt], 1)

            def mixer_b():
                U, T = U_B, T_B

                def keep_qk(t, bank):
                    act.activation(b_qk[:, QK_TILE[t], :], acc[:, bank, :], ACT.Copy,
                                   scale=DK ** -0.5 if QK_TILE[t] < 8 else 1.0).then_inc(acc_free[bank], 1)

                for t in range(4):
                    high_part(U + t + 4)
                    act.wait_ge(unit_done, U + t + 1)
                    keep_qk(t, t)
                act.wait_ge(trig_arg, 2)
                act.activation(b_cos[:, :], b_cos[:, :], ACT.Sin).then_inc(trig_ready, 1)
                act.activation(b_sin[:, :], b_sin[:, :], ACT.Sin).then_inc(trig_ready, 1)
                v_evac(U + 4, b_v, 0)

                def keep_chunk(c):
                    if c < 12:
                        act.wait_ge(unit_done, U + 8 + c + 1)
                        keep_qk(4 + c, c % 2)
                        high_part(U + 12 + c)
                        return
                    if c < 15:
                        act.wait_ge(v_part_done, c - 11)
                    else:
                        act.wait_ge(unit_done, U + 24)
                    act.activation(b_v[:, c - 12, 512:1024], acc[:, c % 2, :], ACT.Copy)\
                       .then_inc(acc_free[c % 2], 1)

                def exps(n):
                    h, i = divmod(n, ST)
                    act.wait_ge(max_ready, n + 1)
                    if n >= 2:
                        act.wait_ge(turned, n - 1)
                        act.wait_ge(p_ready, n - 1)
                    for c in range(2):
                        act.activation(b_p[n % 2][:, c, 0:(i + 1) * P], acc[:, 2 + c, 0:(i + 1) * P], ACT.Exp,
                                       bias=neg_max[:, n % 2, c:c + 1], accum_out=row_sum[:, n % 2, c:c + 1])\
                           .then_inc(acc_free[2 + c], 1)

                def keep_turned(n):
                    h, i = divmod(n, ST)
                    act.wait_ge(turned, n + 1)
                    if h >= 2:
                        act.wait_ge(pv_done, h - 1)
                    act.activation(b_at[h % 2][:, 0:i + 1, i * P:(i + 1) * P],
                                   outp[:, n % 2, 0:(i + 1) * P].rearrange("p (j k) -> p j k", k=P), ACT.Copy)\
                       .then_inc(out_free[n % 2], 1)

                def head_square(h):
                    act.wait_ge(b_o_ready, h + 1)
                    act.activation(b_qk[:, 2 * h:2 * h + 2, :], b_o[:, 2 * h:2 * h + 2, :], ACT.Square)\
                       .then_inc(b_sq_ready, 1)

                def head_root(h):
                    act.wait_ge(b_ss_done, h + 1)
                    cs = slice(ST * h, ST * h + ST)
                    act.activation(head_std[:, cs], stat[:, cs], ACT.Sqrt, bias=eps[:, 0:1], scale=1.0 / DV)\
                       .then_inc(b_std_ready, 1)

                def keep_factor(h):
                    act.wait_ge(b_inv_spread, h + 1)
                    act.activation(b_qk[:, 9 + 2 * h, :], aux[:, :], ACT.Copy).then_inc(b_factor_ready, 1)

                for n in range(4 * HEADS):
                    keep_chunk(n)
                    if n in (8, 12):
                        head_root(n // 4 - 2)
                    if n in (9, 13):
                        keep_factor(n // 4 - 2)
                    if n == 15:
                        high_part(U + 24)
                    exps(n)
                    if n == 15:
                        high_part(U + 25)
                    if n >= 1:
                        keep_turned(n - 1)
                    if n in (6, 10):
                        head_square(n // 4 - 1)
                high_part(U + 26)
                keep_turned(15)
                head_square(2)
                high_part(U + 27)
                for k in range(KT):
                    split_high(Q_B_OUT + k, k)
                    if k == 1:
                        head_root(2)
                        head_square(3)
                    if k == 3:
                        keep_factor(2)
                        head_root(3)
                    if k == 5:
                        keep_factor(3)
                return out_projection(U + 24, T_B_OUT, O_B_OUT, 4)

            act.dma_start(cond[:, :], c_row.broadcast_to([P, D])).then_inc(c_loaded, 16)
            act.dma_start(col[:, :], cols).then_inc(col_loaded, 16)
            act.dma_start(x[:, :, :], xT).then_inc(x_loaded, 16)
            act.dma_start(gbias[:, :], gate_bias).then_inc(small_loaded, 16)
            act.dma_start(rope_row[:, :], rope_rows).then_inc(small_loaded, 16)
            act.wait_ge(col_loaded, 16)
            act.wait_ge(c_loaded, 16)
            act.activation(cond[:, :], cond[:, :], ACT.Silu).then_inc(cond_ready, 1)
            act.wait_ge(lam_sum_done, 1)
            act.activation(lam_exp[:, :], aux[:, 0:2], ACT.Exp).then_inc(lam_exp_ready, 1)
            act.preload_act_table(ACT.Sqrt)
            act.wait_ge(x_loaded, 16)
            for k in range(KT):
                act.activation(x_sq[:, k, :], x[:, k, :], ACT.Square).then_inc(sq_done, 1)
            act.wait_ge(pool_consts, 6)
            norm(0, U_F0, {})
            norm(1, U_A, ffn(0))
            norm(2, U_F1, mixer_a())
            norm(3, U_F2, ffn(1))
            norm(4, U_B, ffn(2))
            norm(5, U_F3, mixer_b())
            between = ffn(3)
            root(SUBS, 0)
            between[LATE_FFN]()
            root(SUBS, 1)

        @block.vector
        def _(dve):
            chain = [0]

            def link(ins):
                chain[0] += 1
                ins.then_inc(dve_step, 1)
                dve.wait_ge(dve_step, chain[0])

            def colv(name, k, n=1):
                return col[:, COLS[name] + k:COLS[name] + k + n]

            def lows(q, bias, make, t=slice(0, S)):
                def low(k):
                    dve.wait_ge(act_hi_ready, q + k + 1)
                    hi = h_hi[:, k, t].bitcast(F32)
                    if bias is None:
                        ins = dve.tensor_tensor(h_lo[:, k, t], buf[k % 2][:, t], hi, ALU.subtract)
                    else:
                        ins = dve.scalar_tensor_tensor(out=h_lo[:, k, t], in0=buf[k % 2][:, t],
                                                       scalar=bias[:, k:k + 1], in1=hi,
                                                       op0=ALU.add, op1=ALU.subtract)
                    ins.then_inc(act_lo_ready, 1)

                for k in range(KT + 1):
                    if k < KT:
                        if k >= 2:
                            dve.wait_ge(act_lo_ready, q + k - 1)
                        make(k)
                    if k >= 1:
                        low(k - 1)

            def inverse_rms(n, half):
                two = slice(2 * half, 2 * half + 2)
                dve.wait_ge(std_ready, 2 * n + half + 1)
                link(dve.reciprocal(inv_col[:, two], std_col[:, two]))
                dve.tensor_tensor(rstd[:, tok(half)].rearrange("p (j k) -> p j k", k=P),
                                  ident[:, :].unsqueeze(1).broadcast_to([P, 2, P]),
                                  inv_col[:, two].unsqueeze(2).broadcast_to([P, 2, P]), ALU.mult)\
                   .then_inc(rstd_ready, 1)

            def norm(n, between):
                dve.wait_ge(ada_ready, 3 * n + 2)
                dve.scalar_tensor_tensor(out=scale_col[:, :], in0=ada_v[:, 3 * n + 1, :], scalar=1.0,
                                         in1=colv("norm_g", n * KT, KT), op0=ALU.add, op1=ALU.mult)\
                   .then_inc(scale_ready, 1)
                def modulated(k, half):
                    if half == 0 and k in between:
                        between[k]()
                    if k == 0:
                        dve.wait_ge(rstd_spread, 2 * n + half + 1)
                    dve.scalar_tensor_tensor(out=buf[k % 2][:, tok(half)], in0=x[:, k, tok(half)],
                                             scalar=scale_col[:, k:k + 1], in1=rstd_bank(half),
                                             op0=ALU.mult, op1=ALU.mult).then_inc(src_ready, 1)

                for half in range(2):
                    if n or half:
                        inverse_rms(n, half)
                    if half == 0:
                        dve.wait_ge(scale_ready, n + 1)
                    lows(Q_IN[n] + KT * half, ada_v[:, 3 * n, :], lambda k: modulated(k, half), tok(half))

            def prepare_residual(r, factor):
                dve.wait_ge(ada_ready, 3 * r + 3)
                dve.tensor_scalar(gate_col[:, :], ada_v[:, 3 * r + 2, :], factor, None, ALU.mult)\
                   .then_inc(gate_ready, 1)
                dve.memset(sumsq[:, :], 0.0).then_inc(sq_added, 1)
                dve.wait_ge(gate_ready, r + 1)

            def residual(r, i, o, bank, free, t=slice(0, S), more=0, dyn=None):
                xs = x[:, o, t] if dyn is None else x[:, bass.ds(dyn, 1), :].rearrange("p a s -> p (a s)")
                g = gate_col[:, o:o + 1] if dyn is None else gate_col[:, bass.ds(dyn, 1)]
                dve.scalar_tensor_tensor(out=xs, in0=bank, scalar=g, in1=xs, op0=ALU.mult, op1=ALU.add)\
                   .then_inc(free, 1)
                dve.wait_ge(sq_done, KT + SQ_BASE[r] + i + 1 + more)
                dve.wait_ge(sq_added, ADD_BASE[r] + i + 1 + more)
                dve.tensor_tensor(sumsq[:, t], sumsq[:, t], sq[:, t], ALU.add).then_inc(sq_added, 1)

            def ada_tile(src, t, done):
                dve.tensor_tensor_reduce(out=src, in0=src, in1=cond[:, :], scale=1.0, scalar=0.0,
                                         op0=ALU.mult, op1=ALU.add, accum_out=ada_sum[:, t:t + 1])\
                   .then_inc(done, 1)

            def ada_bias(sl, more=0):
                if isinstance(more, int):
                    dst, b = ada_v[:, sl, :], colv("ada_b", sl * KT, KT)
                else:
                    dst = ada_v[:, bass.ds(more + sl, 1), :].rearrange("p a s -> p (a s)")
                    b = col[:, bass.ds(8 * more + COLS["ada_b"] + sl * KT, KT)]
                dve.tensor_tensor(dst, ada_sum[:, :], b, ALU.add).then_inc(ada_ready, 1)

            def ada_half(sl, first, more=0):
                for k in range(first, first + 4):
                    a = (sl - EARLY) * KT + k
                    dve.wait_ge(ada_loaded[k % 2], 16 * (a // 2 + 1) + 64 * more)
                    if k == 0:
                        dve.wait_ge(ada_ready, sl + more)
                    ada_tile(ada_raw[k % 2][:, :], k, ada_used)
                if first:
                    dve.wait_ge(ada_used, (sl - EARLY + 1) * KT + 8 * more)
                    ada_bias(sl, more)

            def ffn(p, ada_first, ada_steps):
                U, T, r = U_FFN[p], T_FFN[p], N_FFN[p]

                def step(i, more, with_ada):
                    for j in range(2):
                        u, f = U + 4 * i + 2 * j, 2 * i + j
                        F = FT * p + f
                        dve.wait_ge(unit_done, u + 2 + 4 * more)
                        dve.wait_ge(acc_free[2 * j], T[2 * j] + i + 1 + more)
                        dve.tensor_tensor(buf[j][:, :], buf[j][:, :], acc[:, 2 * j + 1, :], ALU.mult)\
                           .then_inc(acc_free[2 * j + 1], 1)
                        dve.wait_ge(g_hi_ready, F + 1 + 2 * more)
                        if isinstance(more, int):
                            lo, hi = g_lo[:, f, :], g_hi[:, f, :]
                        else:
                            lo, hi = (g[:, bass.ds(2 * more + f, 1), :].rearrange("p a s -> p (a s)")
                                      for g in (g_lo, g_hi))
                        dve.tensor_tensor(lo, buf[j][:, :], hi.bitcast(F32), ALU.subtract)\
                           .then_inc(g_lo_ready, 1)
                        if with_ada:
                            ada_half(ada_first + i, 4 * j, more)

                if ada_steps:
                    dve.wait_ge(cond_ready, 1 if p == 0 else 2)
                step(0, 0, ada_steps > 0)
                if ada_steps:
                    with dve.Fori(0, ada_steps - 1) as i:
                        step(1, i, True)
                done = max(ada_steps, 1)
                with dve.Fori(0, FT // 2 - done) as i:
                    step(done, i, False)
                prepare_residual(r, 0.5)
                W = U + N13
                with dve.Fori(0, KT // 2 - 1) as i:
                    for j in range(2):
                        dve.wait_ge(unit_done, W + 4 * j + 4 + 8 * i)
                        residual(r, j, j, outp[:, j, :], out_free[j], more=2 * i, dyn=2 * i + j)
                dve.wait_ge(unit_done, W + 4 * (KT - 1))
                residual(r, KT - 2, KT - 2, outp[:, 0, :], out_free[0])
                dve.wait_ge(half_done, HALVES[r] + 1)
                residual(r, KT - 1, KT - 1, outp[:, 1, tok(0)], out_free[1], tok(0))

                def second_half():
                    dve.wait_ge(unit_done, W + 4 * KT)
                    residual(r, KT, KT - 1, outp[:, 0, tok(1)], out_free[0], tok(1))
                return {LATE_FFN: second_half}

            def out_projection(U, r):
                prepare_residual(r, 1.0)
                for o in range(4):
                    dve.wait_ge(unit_done, U + o + 1)
                    residual(r, o, o, acc[:, o % 4, :], acc_free[o % 4])
                for o in range(4, KT):
                    dve.wait_ge(half_done, HALVES[r] + o - 4 + 1)
                    residual(r, o, o, acc[:, o % 4, tok(0)], acc_free[o % 4], tok(0))

                def second_half(o):
                    dve.wait_ge(unit_done, U + o + 1)
                    bank, free = (outp, out_free) if o < 6 else (acc, acc_free)
                    residual(r, o + 4, o, bank[:, o % 4, tok(1)], free[o % 4], tok(1))
                return {k: lambda o=o: second_half(o) for k, o in zip(LATE_MIXER, range(4, KT))}

            def v_evac(U, dst, half):
                dve.wait_ge(unit_done, U + 4)
                for tt in range(2, 4):
                    dve.tensor_copy(dst[:, tt, half * 512:half * 512 + 512], acc[:, tt, :])\
                       .then_inc(acc_free[tt], 1)

            def mixer_a():
                U, T = U_A, T_A
                for t in range(8):
                    dve.wait_ge(unit_done, U + t + 1)
                    if t >= 2:
                        dve.wait_ge(a_qk_ready, t - 1)
                    y, p = buf[t % 2], acc[:, t % 4, :]
                    tap = [colv("conv_w", TAPS * t + j) for j in range(TAPS)]
                    link(dve.tensor_scalar(y[:, :], p, tap[3], colv("conv_b", t), ALU.mult, ALU.add))
                    for back in range(1, TAPS):
                        ins = dve.scalar_tensor_tensor(out=y[:, back:S], in0=p[:, 0:S - back],
                                                       scalar=tap[3 - back], in1=y[:, back:S],
                                                       op0=ALU.mult, op1=ALU.add)
                        if back < TAPS - 1:
                            link(ins)
                    ins.then_inc(acc_free[t % 4], 1)
                dve.wait_ge(unit_done, U + 9)
                dve.wait_ge(small_loaded, 32)
                R = [rows[:, n, :] for n in range(8)]
                dve.tensor_scalar(R[0], aux[0:HEADS, :], gbias[:, 0:1], None, ALU.add).then_inc(dve_step, 1)
                link(dve.tensor_copy(R[1], aux[32:32 + HEADS, :]))
                chain[0] += 1
                dve.wait_ge(dve_step, chain[0])
                link(dve.tensor_scalar(R[2], R[1], gbias[:, 1:2], None, ALU.add))
                dve.tensor_scalar(R[4], R[2], 0.0, None, ALU.min).then_inc(dve_step, 1)
                chain[0] += 1
                dve.scalar_tensor_tensor(out=R[3], in0=R[2], scalar=-1.0, in1=R[2],
                                         op0=ALU.mult, op1=ALU.min).then_inc(f_arg_ready, 1)
                dve.wait_ge(dve_step, chain[0])
                dve.wait_ge(f_log_ready, 1)
                link(dve.tensor_tensor(R[7], R[4], R[6], ALU.subtract))
                link(dve.tensor_tensor_scan(R[1], rows_one[:, :], R[7], 0.0, ALU.mult, ALU.add))
                link(dve.tensor_tensor(R[2], R[0], R[1], ALU.subtract))
                link(dve.tensor_tensor_scan(R[3], R[2], R[2], 0.0, ALU.max, ALU.max))
                link(dve.tensor_scalar(R[4], R[3], -1.0, None, ALU.mult))
                dve.tensor_tensor(R[5], R[1], R[3], ALU.add).then_inc(m_rows_ready, 1)
                v_evac(U + 9, a_v, 0)
                v_evac(U + 13, a_v, 1)
                dve.wait_ge(u_turned, 1)
                dve.tensor_copy(u_col[:, :], stat[:, 0:ST * HEADS]).then_inc(u_col_ready, 1)

                def diagonal(h):
                    read_out(dve, T, 16 + h)
                    if h >= 2:
                        dve.wait_ge(decay_ready, h - 1)
                    dve.tensor_tensor(buf[h % 2][:, :].rearrange("p (j k) -> p j k", k=P),
                                      neg_m[:, h, :].rearrange("p (j k) -> p j k", k=P),
                                      mask_st[:, :].unsqueeze(1).broadcast_to([P, ST, P]), ALU.add)\
                       .then_inc(diag_ready, 1)

                def weights(h):
                    dve.wait_ge(decay_ready, h + 1)
                    for j in range(ST):
                        dve.wait_ge(st_done, 4 * h + j + 1)
                        w = a_wt[h % 2][:, WT_OFF[j]:WT_OFF[j] + S - j * P]
                        dve.scalar_tensor_tensor(out=w, in0=acc[:, j, 0:S - j * P], scalar=DK ** -0.5, in1=w,
                                                 op0=ALU.mult, op1=ALU.mult)\
                           .then_inc(acc_free[j], 1)

                def heads_out(h):
                    dve.wait_ge(av_done, h + 1)
                    read_out(dve, T, 20 + h)
                    dve.scalar_tensor_tensor(out=rstd[:, :], in0=aux[:, :], scalar=-1.0, in1=exp_m[:, h, :],
                                             op0=ALU.mult, op1=ALU.max).then_inc(dve_step, 1)
                    chain[0] += 1
                    dve.wait_ge(dve_step, chain[0])
                    dve.tensor_tensor(rstd[:, :], aux[:, :], rstd[:, :], ALU.max).then_inc(den_read, 1)
                    dve.wait_ge(den_read, h + 1)
                    link(dve.reciprocal(sq[:, :], rstd[:, :]))
                    for d in range(2):
                        dve.tensor_tensor(a_h[:, 2 * h + d, :], outp[:, d, :], sq[:, :], ALU.mult)\
                           .then_inc(out_free[d], 1)

                def gated(t):
                    dve.wait_ge(a_o_ready, t + 1)
                    dve.scalar_tensor_tensor(out=a_o[:, t, :], in0=a_o[:, t, :], scalar=1.0,
                                             in1=a_h[:, t, :], op0=ALU.add, op1=ALU.mult)\
                       .then_inc(gated_ready, 1)

                def pair(h):
                    dve.wait_ge(a_sq_ready, h + 1)
                    dve.tensor_tensor(a_qk[:, h, :], a_qk[:, h, :], a_qk[:, 4 + h, :], ALU.add)\
                       .then_inc(a_pair_ready, 1)

                def inverse(h):
                    cs = slice(ST * h, ST * h + ST)
                    dve.wait_ge(a_std_ready, h + 1)
                    link(dve.reciprocal(head_inv[:, cs], head_std[:, cs]))
                    dve.tensor_tensor(neg_m[:, h, :].rearrange("p (j k) -> p j k", k=P),
                                      ident[:, :].unsqueeze(1).broadcast_to([P, ST, P]),
                                      head_inv[:, cs].unsqueeze(2).broadcast_to([P, ST, P]), ALU.mult)\
                       .then_inc(a_inv_ready, 1)

                link(dve.tensor_scalar(ag_col[:, :], colv("a_norm_g", 0, 8), 0.5, None, ALU.mult))
                diagonal(0)
                diagonal(1)
                weights(0)
                diagonal(2)
                weights(1)
                diagonal(3)
                heads_out(0)
                weights(2)
                heads_out(1)
                weights(3)
                gated(0)
                gated(1)
                pair(0)
                pair(1)
                heads_out(2)
                gated(2)
                gated(3)
                pair(2)
                inverse(0)
                inverse(1)
                gated(4)
                gated(5)

                def make(t):
                    h = t // 2
                    if t == 2:
                        inverse(2)
                    if t == 4:
                        heads_out(3)
                    if t == 5:
                        pair(3)
                    if t == 6:
                        gated(6)
                        gated(7)
                        inverse(3)
                    dve.wait_ge(a_factor_ready, h + 1)
                    dve.wait_ge(gated_ready, t + 1)
                    dve.scalar_tensor_tensor(out=buf[t % 2][:, :], in0=a_o[:, t, :],
                                             scalar=ag_col[:, t:t + 1], in1=exp_m[:, h, :],
                                             op0=ALU.mult, op1=ALU.mult).then_inc(src_ready, 1)
                lows(Q_A_OUT, None, make)
                return out_projection(U + 25, 1)

            def trig_tables():
                C, Sn, A, B = b_cos[:, :], b_sin[:, :], b_rot[:, :], b_tmp[:, :]
                dve.wait_ge(pos_loaded, 16)
                link(dve.tensor_copy(A, pos_i[:, :]))
                link(dve.tensor_scalar(A, A, rope_row[:, 0:1], None, ALU.mult))
                rounder = 1.5 * 2.0 ** 23
                for step in (2.0 ** 20, 2.0 ** 10, 1.0):
                    link(dve.tensor_scalar(B, A, 1.0 / (step * TWO_PI), rounder, ALU.mult, ALU.add))
                    link(dve.tensor_scalar(B, B, rounder, None, ALU.subtract))
                    for part in two_pi_parts(step):
                        link(dve.scalar_tensor_tensor(out=A, in0=B, scalar=-part, in1=A,
                                                      op0=ALU.mult, op1=ALU.add))
                link(dve.tensor_scalar(A, A, math.pi * (1 - 2.0 ** -22), -math.pi * (1 - 2.0 ** -22),
                                       ALU.min, ALU.max))
                dve.tensor_scalar(Sn, A, rope_row[:, 1:2], None, ALU.mult).then_inc(trig_arg, 1)
                link(dve.scalar_tensor_tensor(out=B, in0=A, scalar=-1.0, in1=A, op0=ALU.mult, op1=ALU.min))
                dve.tensor_scalar(C, B, math.pi / 2, None, ALU.add).then_inc(trig_arg, 1)

            def mixer_b():
                U, T = U_B, T_B
                trig_tables()
                dve.wait_ge(trig_ready, 2)
                dve.tensor_scalar(bg_col[:, :], colv("b_norm_g", 0, 2), 1.0 - LAM_INIT, None, ALU.mult)\
                   .then_inc(dve_step, 1)
                chain[0] += 1
                swap = [(n + HALF) % ROPE_DIM for n in range(ROPE_DIM)]

                def rope(t):
                    read_out(dve, T, t if t < 4 else 4 * (2 + (t - 4) // 2) + t % 2)
                    q = b_qk[0:ROPE_DIM, QK_TILE[t], :]
                    link(dve.stream_shuffle(b_rot[:, :], q, swap))
                    dve.tensor_tensor(b_tmp[:, :], q, b_cos[:, :], ALU.mult).then_inc(dve_step, 1)
                    chain[0] += 1
                    link(dve.tensor_tensor(b_rot[:, :], b_rot[:, :], b_sin[:, :], ALU.mult))
                    dve.tensor_tensor(q, b_tmp[:, :], b_rot[:, :], ALU.add).then_inc(rope_done, 1)
                    dve.wait_ge(rope_done, t + 1)

                def maxima(n):
                    h, i = divmod(n, ST)
                    dve.wait_ge(s_done, 2 * n + 2)
                    diag = acc[:, 2:4, i * P:(i + 1) * P]
                    link(dve.tensor_tensor(diag, diag, mask_ts[:, :].unsqueeze(1).broadcast_to([P, 2, P]), ALU.add))
                    link(dve.tensor_reduce(row_max[:, n % 2, :], acc[:, 2:4, 0:(i + 1) * P], AX.X, ALU.max))
                    dve.tensor_scalar(neg_max[:, n % 2, :], row_max[:, n % 2, :], -1.0, None, ALU.mult)\
                       .then_inc(max_ready, 1)

                def combine(n):
                    h, i = divmod(n, ST)
                    N = (i + 1) * P
                    inv, pr = row_inv[:, n % 2, :], b_p[n % 2]
                    for c in range(2):
                        read_out(dve, T, 4 * (2 + n) + 2 + c)
                    link(dve.reciprocal(inv, row_sum[:, n % 2, :]))
                    link(dve.tensor_tensor(inv[:, 1:2], inv[:, 1:2], neg_lam[:, :], ALU.mult))
                    link(dve.tensor_scalar(pr[:, 1, 0:N], pr[:, 1, 0:N], inv[:, 1:2], None, ALU.mult))
                    dve.scalar_tensor_tensor(out=pr[:, 0, 0:N], in0=pr[:, 0, 0:N], scalar=inv[:, 0:1],
                                             in1=pr[:, 1, 0:N], op0=ALU.mult, op1=ALU.add).then_inc(p_ready, 1)

                def keep(h):
                    dve.wait_ge(pv_done, h + 1)
                    dve.tensor_copy(b_o[:, 2 * h, :], head_bank(h, 0)).then_inc(dve_step, 1)
                    chain[0] += 1
                    dve.wait_ge(dve_step, chain[0])
                    dve.tensor_copy(b_o[:, 2 * h + 1, :], head_bank(h, 1)).then_inc(b_o_ready, 1)

                def pair(h):
                    dve.wait_ge(b_sq_ready, h + 1)
                    dve.tensor_tensor(b_qk[:, 2 * h, :], b_qk[:, 2 * h, :], b_qk[:, 2 * h + 1, :], ALU.add)\
                       .then_inc(b_pair_ready, 1)

                def inverse(h):
                    cs = slice(ST * h, ST * h + ST)
                    dve.wait_ge(b_std_ready, h + 1)
                    link(dve.reciprocal(head_inv[:, cs], head_std[:, cs]))
                    dve.tensor_tensor(b_qk[:, 8 + 2 * h, :].rearrange("p (j k) -> p j k", k=P),
                                      ident[:, :].unsqueeze(1).broadcast_to([P, ST, P]),
                                      head_inv[:, cs].unsqueeze(2).broadcast_to([P, ST, P]), ALU.mult)\
                       .then_inc(b_inv_ready, 1)

                for t in range(4):
                    rope(t)
                v_evac(U + 4, b_v, 0)
                dve.wait_ge(lam_ready, 1)
                for n in range(4 * HEADS):
                    if n in (7, 11):
                        pair(n // 4 - 1)
                    if n < 12:
                        rope(4 + n)
                    maxima(n)
                    if n >= 1:
                        combine(n - 1)
                    if n in (6, 10):
                        keep(n // 4 - 1)
                    if n in (8, 12):
                        inverse(n // 4 - 2)
                combine(15)
                keep(2)

                def make(t):
                    h = t // 2
                    if t == 1:
                        pair(2)
                    if t == 2:
                        keep(3)
                        inverse(2)
                    if t == 3:
                        pair(3)
                    if t == 4:
                        inverse(3)
                    dve.wait_ge(b_factor_ready, h + 1)
                    dve.scalar_tensor_tensor(out=buf[t % 2][:, :], in0=b_o[:, t, :],
                                             scalar=bg_col[:, t % 2:t % 2 + 1], in1=b_qk[:, 9 + 2 * h, :],
                                             op0=ALU.mult, op1=ALU.mult).then_inc(src_ready, 1)
                lows(Q_B_OUT, None, make)
                return out_projection(U + 24, 4)

            for j in range(2):
                dve.memset(outp[:, j, :], 0.0).then_inc(out_free[j], 1)
            link(dve.memset(rows_one[:, :], 1.0))
            dve.wait_ge(col_loaded, 16)
            lam = COLS["lam"]
            dve.tensor_tensor(lam_mul[:, :], col[:, lam:lam + 3:2], col[:, lam + 1:lam + 4:2], ALU.mult)\
               .then_inc(lam_mul_ready, 1)
            dve.wait_ge(lam_exp_ready, 1)
            link(dve.tensor_tensor(neg_lam[:, :], lam_exp[:, 1:2], lam_exp[:, 0:1], ALU.subtract))
            dve.tensor_scalar(neg_lam[:, :], neg_lam[:, :], LAM_INIT, None, ALU.subtract).then_inc(lam_ready, 1)
            dve.wait_ge(cond_ready, 1)
            for sl in range(EARLY):
                for k in range(KT):
                    n = sl * KT + k
                    if n % 2 == 0:
                        dve.wait_ge(early_loaded[n // 2], 16)
                    if k == 0 and sl:
                        dve.wait_ge(ada_ready, sl)
                    ada_tile(early_ada[:, n, :], k, early_used)
                    if n == EARLY * KT - 3:
                        dve.wait_ge(pool_consts, 6)
                        inverse_rms(0, 0)
                dve.wait_ge(early_used, (sl + 1) * KT)
                ada_bias(sl)
            norm(0, {})
            norm(1, ffn(0, EARLY, ADA_F0))
            norm(2, mixer_a())
            norm(3, ffn(1, EARLY + ADA_F0, ADA_F1))
            norm(4, ffn(2, 0, 0))
            norm(5, mixer_b())
            between = ffn(3, 0, 0)
            for half in range(2):
                if half:
                    between[LATE_FFN]()
                inverse_rms(SUBS, half)
                dve.wait_ge(rstd_spread, 2 * SUBS + half + 1)
                for k in range(KT):
                    dve.scalar_tensor_tensor(out=x[:, k, tok(half)], in0=x[:, k, tok(half)],
                                             scalar=colv("final_g", k), in1=rstd_bank(half),
                                             op0=ALU.mult, op1=ALU.mult).then_inc(src_ready, 1)


def tiles(w):
    n = w.shape[1] // P
    return w.reshape(KT, P, n, P).transpose(2, 1, 0, 3).reshape(n, P, KT * P)


def v_units(w):
    return w.reshape(4, 2, P, 2, 512).transpose(3, 0, 2, 1, 4).reshape(8, P, 1024)


def columns(v):
    return v.reshape(-1, P).T


def kernel(**inputs):
    import concourse.bacc as bacc
    from concourse.bass_utils import run_bass_kernel_spmd

    a = {k: np.asarray(v) for k, v in inputs.items()}
    gates = np.zeros((D, P), np.float32)
    w_in = a["a_w_in"][0]
    gates[:, 0:HEADS] = w_in[:, 3072:3072 + HEADS]
    gates[:, 32:32 + HEADS] = w_in[:, 3072 + HEADS:3080]
    wb_in = a["b_w_in"][0]
    qk, v = tiles(wb_in[:, 0:2048])[list(QK_TILE)], v_units(wb_in[:, 2048:3072])
    cols = np.concatenate([
        columns(a["ada_b"]), columns(a["norm_g"]), columns(a["final_g"]),
        a["a_conv_w"][0].reshape(TAPS, 8, P).transpose(2, 1, 0).reshape(P, 32),
        columns(a["a_conv_b"][0]), columns(a["a_norm_g"][0]), columns(a["b_norm_g"][0]),
        a["b_lam"][0].T], axis=1)
    inv_freq = (ROPE_THETA ** (-np.arange(0, ROPE_DIM, 2, dtype=np.float64) / ROPE_DIM)).astype(np.float32)
    rope_rows = np.stack([np.concatenate([inv_freq, inv_freq]),
                          np.repeat(np.array([-1.0, 1.0], np.float32), HALF)], axis=1)
    arrays = {
        "xT": a["x"][0].T.reshape(KT, P, S).transpose(1, 0, 2),
        "c_row": a["c"],
        "cols": cols,
        "gate_bias": a["a_b_if"][0].reshape(2, HEADS).T,
        "rope_rows": rope_rows,
        "positions": a["positions"],
        "ada": a["ada_w"].reshape(LAYERS, D, 9, KT, P).transpose(0, 2, 3, 4, 1).reshape(SLICES * KT, P, D),
        "w13": a["ffn_w13"].reshape(4, KT, P, 2, FT, P).transpose(0, 4, 3, 2, 1, 5).reshape(4 * N13, P, D),
        "w2": a["ffn_w2"].reshape(4, FT, P, KT, P).transpose(0, 3, 2, 1, 4).reshape(4 * KT, P, FF),
        "wa": np.concatenate([tiles(w_in[:, 0:1024]), tiles(gates), v_units(w_in[:, 1024:2048]),
                              tiles(w_in[:, 2048:3072]), tiles(a["a_w_out"][0])]),
        "wb": np.concatenate([qk[0:4], v[0:4], qk[4:16], v[4:8], tiles(a["b_w_out"][0])]),
    }
    nc = bacc.Bacc("TRN2", target_bir_lowering=False, num_devices=1)
    arrays = {k: np.ascontiguousarray(v) for k, v in arrays.items()}
    aps = [nc.dram_tensor(k, v.shape, mybir.dt.from_np(v.dtype), kind="ExternalInput").ap()
           for k, v in arrays.items()]
    out = nc.dram_tensor("out", (KT, P, S), F32, kind="ExternalOutput").ap()
    build_trunk(nc, *aps, out)
    r = run_bass_kernel_spmd(nc, [arrays], core_ids=[0])
    return r.results[0]["out"].reshape(D, S).T.reshape(1, S, D)
```
